# Optimizing a Trainium2 kernel written in Bass

```python
import jax
import jax.numpy as jnp
from jax import lax

D_MODEL = 2048
BATCH = 1
SEQ = 512
DEPTH = 1

GRID_W = 64
CTX_LEN = 256

MLA_HEADS = 8
MLA_NOPE = 128
MLA_ROPE = 64
MLA_V = 128
Q_LORA = 512
KV_LORA = 256
ROPE_THETA = 10000.0
Q_BLOCK = 128

ML_HEADS = 4
ML_QK = 128
ML_V = 256
ML_INNER = ML_HEADS * ML_V
ML_CONV = 3
CHUNK = 64
N_GATES = 4 * ML_HEADS

D_FF = 5632
FFN_CONV = 3

MIX_WIDTH = MLA_HEADS * MLA_V + ML_INNER
OFF_CKV = Q_LORA
OFF_KR = Q_LORA + KV_LORA
OFF_U = OFF_KR + MLA_ROPE
OFF_V = OFF_U + ML_INNER
OFF_O = OFF_V + ML_INNER
OFF_G = OFF_O + ML_INNER
IN_COLS = OFF_G + N_GATES

ALPHA = (2.0 * DEPTH) ** 0.25
BETA = (8.0 * DEPTH) ** -0.25
EPS = 1e-6
N_MOD = 6

kernel_name = "hybrid_mla_mlstm_convffn_dit"

def rms_norm(x, g):
    xf = x.astype(jnp.float32)
    y = xf * lax.rsqrt(jnp.mean(xf * xf, axis=-1, keepdims=True) + EPS)
    return (y * g).astype(x.dtype)

def layer_norm(x, g, b):
    xf = x.astype(jnp.float32)
    mu = jnp.mean(xf, axis=-1, keepdims=True)
    var = jnp.mean(jnp.square(xf - mu), axis=-1, keepdims=True)
    return ((xf - mu) * lax.rsqrt(var + EPS) * g + b).astype(x.dtype)

def modulate(x, mod, i):
    return x * (1.0 + mod[..., i + 1, :]) + mod[..., i, :]

def dwconv_centred(x, w, b):
    k = w.shape[0]
    y = lax.conv_general_dilated(
        x, w[:, None, :].astype(x.dtype), window_strides=(1,), padding=[(k // 2, k // 2)],
        dimension_numbers=("NWC", "WIO", "NWC"), feature_group_count=x.shape[-1])
    return y + b

def axial_angles(n_rows):
    row = jnp.repeat(jnp.arange(n_rows), GRID_W).astype(jnp.float32)
    col = jnp.tile(jnp.arange(GRID_W), n_rows).astype(jnp.float32)
    n_freq = MLA_ROPE // 4
    inv = ROPE_THETA ** (-jnp.arange(n_freq, dtype=jnp.float32) / n_freq)
    return row[:, None] * inv, col[:, None] * inv

def rotate_half(x, ang):
    f = ang.shape[-1]
    cos = jnp.cos(ang)[:, None, :]
    sin = jnp.sin(ang)[:, None, :]
    x1, x2 = x[..., :f], x[..., f:]
    return jnp.concatenate([x1 * cos - x2 * sin, x1 * sin + x2 * cos], axis=-1).astype(x.dtype)

def rope2d(x, ang_row, ang_col):
    half = MLA_ROPE // 2
    return jnp.concatenate([rotate_half(x[..., :half], ang_row), rotate_half(x[..., half:], ang_col)], axis=-1)

def to_heads(a):
    return jnp.transpose(a, (0, 2, 1, 3))

def from_heads(a):
    b, h, s, d = a.shape
    return jnp.transpose(a, (0, 2, 1, 3)).reshape(b, s, h * d)

def mla_queries(z, g_q, w_uq):
    b, s, _ = z.shape
    c_q = rms_norm(z[..., :Q_LORA], g_q)
    q = (c_q @ w_uq).reshape(b, s, MLA_HEADS, MLA_NOPE + MLA_ROPE)
    return q[..., :MLA_NOPE], q[..., MLA_NOPE:]

def mla_keys_values(z, g_kv, w_ukv):
    b, s, _ = z.shape
    c_kv = rms_norm(z[..., OFF_CKV:OFF_KR], g_kv)
    k_rope = z[..., OFF_KR:OFF_U][:, :, None, :]
    kv = (c_kv @ w_ukv).reshape(b, s, MLA_HEADS, MLA_NOPE + MLA_V)
    return kv[..., :MLA_NOPE], k_rope, kv[..., MLA_NOPE:]

def key_heads(k_nope, k_rope):
    k_rope = jnp.broadcast_to(k_rope, k_nope.shape[:-1] + (MLA_ROPE,))
    return jnp.concatenate([k_nope, k_rope], axis=-1)

def block_attention(q, k, v):
    b, h, s, dq = q.shape
    nb = s // Q_BLOCK
    scale = dq ** -0.5
    qb = jnp.moveaxis(q.reshape(b, h, nb, Q_BLOCK, dq), 2, 0)

    def one_block(qi):
        sc = jnp.einsum("bhqd,bhkd->bhqk", qi, k, preferred_element_type=jnp.float32) * scale
        p = jax.nn.softmax(sc, axis=-1)
        return jnp.einsum("bhqk,bhkd->bhqd", p.astype(v.dtype), v)

    out = lax.map(one_block, qb)
    return jnp.moveaxis(out, 0, 2).reshape(b, h, s, v.shape[-1])

def mlstm_project(z, conv_w, conv_b, w_mq, w_mk, b_gate):
    b, s, _ = z.shape
    u = jax.nn.silu(dwconv_centred(z[..., OFF_U:OFF_V], conv_w, conv_b)).reshape(b, s, ML_HEADS, ML_V)
    q = jnp.einsum("bshd,hde->bhse", u, w_mq) * (ML_QK ** -0.5)
    k = jnp.einsum("bshd,hde->bhse", u, w_mk)
    v = to_heads(z[..., OFF_V:OFF_O].reshape(b, s, ML_HEADS, ML_V))
    o = z[..., OFF_O:OFF_G]
    gates = (z[..., OFF_G:] + b_gate).astype(jnp.float32)
    gates = jnp.transpose(gates.reshape(b, s, 4, ML_HEADS), (2, 0, 3, 1))
    return q, k, v, o, gates

def mlstm_chunkwise(q, k, v, ig, fg, state):
    b, h, s, dk = q.shape
    dv = v.shape[-1]
    nc = s // CHUNK

    def chunks(a):
        return jnp.moveaxis(a.reshape((b, h, nc, CHUNK) + a.shape[3:]), 2, 0)

    lf = jax.nn.log_sigmoid(fg)
    lower = jnp.tril(jnp.ones((CHUNK, CHUNK), dtype=bool))

    def step(carry, xs):
        c_st, n_st, m_st = carry
        qc, kc, vc, ic, fc = xs
        bc = jnp.cumsum(fc, axis=-1)
        m_inter = bc + m_st[..., None]
        dmat = jnp.where(lower, bc[..., :, None] - bc[..., None, :] + ic[..., None, :], -jnp.inf)
        m_t = jnp.maximum(m_inter, jnp.max(dmat, axis=-1))
        w_inter = jnp.exp(m_inter - m_t)
        p = jnp.exp(dmat - m_t[..., None]) * jnp.einsum("bhtd,bhsd->bhts", qc, kc)
        num = w_inter[..., None] * jnp.einsum("bhtd,bhde->bhte", qc, c_st) + jnp.einsum("bhts,bhse->bhte", p, vc)
        den = w_inter * jnp.einsum("bhtd,bhd->bht", qc, n_st) + jnp.sum(p, axis=-1)
        h_c = num / jnp.maximum(jnp.abs(den), jnp.exp(-m_t))[..., None]
        b_last = bc[..., -1]
        g_log = b_last[..., None] - bc + ic
        m_new = jnp.maximum(b_last + m_st, jnp.max(g_log, axis=-1))
        decay = jnp.exp(b_last + m_st - m_new)
        wk = jnp.exp(g_log - m_new[..., None])
        c_new = decay[..., None, None] * c_st + jnp.einsum("bhs,bhsd,bhse->bhde", wk, kc, vc)
        n_new = decay[..., None] * n_st + jnp.einsum("bhs,bhsd->bhd", wk, kc)
        return (c_new, n_new, m_new), h_c

    f32 = jnp.float32
    xs = (chunks(q.astype(f32)), chunks(k.astype(f32)), chunks(v.astype(f32)), chunks(ig), chunks(lf))
    state, hs = lax.scan(step, state, xs)
    return jnp.moveaxis(hs, 0, 2).reshape(b, h, s, dv), state

def mlstm_bidirectional(qc, kc, vc, gc, q, k, v, g):
    b, h, _, dk = q.shape
    dv = v.shape[-1]
    f32 = jnp.float32
    init = (jnp.zeros((b, h, dk, dv), f32), jnp.zeros((b, h, dk), f32), jnp.zeros((b, h), f32))

    def flip(a):
        return jnp.flip(a, axis=2)

    hc_f, st_f = mlstm_chunkwise(qc, kc, vc, gc[0], gc[1], init)
    hc_b, st_b = mlstm_chunkwise(flip(qc), flip(kc), flip(vc), flip(gc[2]), flip(gc[3]), init)
    h_f, _ = mlstm_chunkwise(q, k, v, g[0], g[1], st_f)
    h_b, _ = mlstm_chunkwise(flip(q), flip(k), flip(v), flip(g[2]), flip(g[3]), st_b)
    return h_f + flip(h_b), hc_f + flip(hc_b)

def mlstm_output(hm, o, g_hn):
    mu = jnp.mean(hm, axis=-1, keepdims=True)
    var = jnp.mean(jnp.square(hm - mu), axis=-1, keepdims=True)
    hn = (hm - mu) * lax.rsqrt(var + EPS) * g_hn[:, None, :]
    return (jax.nn.sigmoid(o.astype(jnp.float32)) * from_heads(hn)).astype(o.dtype)

def token_mixer(h, hc, ang_row, ang_col, w_in, g_q, w_uq, g_kv, w_ukv, ml_conv_w, ml_conv_b,
                w_mq, w_mk, b_gate, g_hn, w_out, update_ctx):
    z = h @ w_in
    zc = hc @ w_in
    qn, qr = mla_queries(z, g_q, w_uq)
    kn, kr, v = mla_keys_values(z, g_kv, w_ukv)
    kn_c, kr_c, v_c = mla_keys_values(zc, g_kv, w_ukv)
    q_lat = to_heads(jnp.concatenate([qn, rope2d(qr, ang_row, ang_col)], axis=-1))
    k_lat = to_heads(key_heads(kn, rope2d(kr, ang_row, ang_col)))
    k_ctx = to_heads(key_heads(kn_c, kr_c))
    v_lat, v_ctx = to_heads(v), to_heads(v_c)
    a = block_attention(q_lat, jnp.concatenate([k_ctx, k_lat], axis=2), jnp.concatenate([v_ctx, v_lat], axis=2))
    mq, mk, mv, o, gt = mlstm_project(z, ml_conv_w, ml_conv_b, w_mq, w_mk, b_gate)
    mq_c, mk_c, mv_c, o_c, gt_c = mlstm_project(zc, ml_conv_w, ml_conv_b, w_mq, w_mk, b_gate)
    hm, hm_c = mlstm_bidirectional(mq_c, mk_c, mv_c, gt_c, mq, mk, mv, gt)
    y = jnp.concatenate([from_heads(a), mlstm_output(hm, o, g_hn)], axis=-1) @ w_out
    if not update_ctx:
        return y, None
    qn_c, qr_c = mla_queries(zc, g_q, w_uq)
    a_c = block_attention(to_heads(jnp.concatenate([qn_c, qr_c], axis=-1)), k_ctx, v_ctx)
    yc = jnp.concatenate([from_heads(a_c), mlstm_output(hm_c, o_c, g_hn)], axis=-1) @ w_out
    return y, yc

def conv_ffn(h, w_up, conv_w, conv_b, w_down):
    gu = h @ w_up
    gate = dwconv_centred(gu[..., :D_FF], conv_w, conv_b)
    return (jax.nn.silu(gate) * gu[..., D_FF:]) @ w_down

def setup_inputs(seed: int = 0) -> dict:
    key = jax.random.key(seed)
    ks = jax.random.split(key, 26)
    f32 = jnp.float32

    def nrm(k, shape, s):
        return jax.random.normal(k, shape, f32) * s

    nl = DEPTH
    forget_bias = jnp.linspace(3.0, 6.0, ML_HEADS, dtype=f32)
    zeros_h = jnp.zeros((ML_HEADS,), f32)
    gate_base = jnp.stack([zeros_h, forget_bias, zeros_h, forget_bias]).reshape(-1)
    return {
        "x": nrm(ks[0], (BATCH, SEQ, D_MODEL), 1.0),
        "c": nrm(ks[1], (BATCH, D_MODEL), 1.0),
        "ctx": nrm(ks[2], (BATCH, CTX_LEN, D_MODEL), 1.0),
        "c_ctx": nrm(ks[3], (D_MODEL,), 1.0),
        "w_ada": nrm(ks[4], (nl, D_MODEL, N_MOD * D_MODEL), 0.5 * D_MODEL ** -0.5),
        "b_ada": nrm(ks[5], (nl, N_MOD * D_MODEL), 0.02),
        "w_in": nrm(ks[6], (nl, D_MODEL, IN_COLS), D_MODEL ** -0.5),
        "g_q": 1.0 + nrm(ks[7], (nl, Q_LORA), 0.02),
        "w_uq": nrm(ks[8], (nl, Q_LORA, MLA_HEADS * (MLA_NOPE + MLA_ROPE)), Q_LORA ** -0.5),
        "g_kv": 1.0 + nrm(ks[9], (nl, KV_LORA), 0.02),
        "w_ukv": nrm(ks[10], (nl, KV_LORA, MLA_HEADS * (MLA_NOPE + MLA_V)), KV_LORA ** -0.5),
        "ml_conv_w": nrm(ks[11], (nl, ML_CONV, ML_INNER), ML_CONV ** -0.5),
        "ml_conv_b": nrm(ks[12], (nl, ML_INNER), 0.02),
        "w_mq": nrm(ks[13], (nl, ML_HEADS, ML_V, ML_QK), ML_V ** -0.5),
        "w_mk": nrm(ks[14], (nl, ML_HEADS, ML_V, ML_QK), ML_V ** -0.5),
        "b_gate": gate_base + nrm(ks[15], (nl, N_GATES), 0.1),
        "g_hn": 1.0 + nrm(ks[16], (nl, ML_HEADS, ML_V), 0.02),
        "w_out": nrm(ks[17], (nl, MIX_WIDTH, D_MODEL), BETA * MIX_WIDTH ** -0.5),
        "ln1_g": 1.0 + nrm(ks[18], (nl, D_MODEL), 0.02),
        "ln1_b": nrm(ks[19], (nl, D_MODEL), 0.02),
        "w_up": nrm(ks[20], (nl, D_MODEL, 2 * D_FF), D_MODEL ** -0.5),
        "ffn_conv_w": nrm(ks[21], (nl, FFN_CONV, D_FF), FFN_CONV ** -0.5),
        "ffn_conv_b": nrm(ks[22], (nl, D_FF), 0.02),
        "w_down": nrm(ks[23], (nl, D_FF, D_MODEL), BETA * D_FF ** -0.5),
        "ln2_g": 1.0 + nrm(ks[24], (nl, D_MODEL), 0.02),
        "ln2_b": nrm(ks[25], (nl, D_MODEL), 0.02),
    }

def reference(x, c, ctx, c_ctx, w_ada, b_ada, w_in, g_q, w_uq, g_kv, w_ukv, ml_conv_w, ml_conv_b,
              w_mq, w_mk, b_gate, g_hn, w_out, ln1_g, ln1_b, w_up, ffn_conv_w, ffn_conv_b, w_down,
              ln2_g, ln2_b):
    n_rows = x.shape[1] // GRID_W
    ang_row, ang_col = axial_angles(n_rows)
    xc = ctx
    for layer in range(DEPTH):
        update_ctx = layer < DEPTH - 1
        mod = (jax.nn.silu(c) @ w_ada[layer] + b_ada[layer]).reshape(c.shape[0], 1, N_MOD, D_MODEL)
        mod_c = (jax.nn.silu(c_ctx) @ w_ada[layer] + b_ada[layer]).reshape(1, 1, N_MOD, D_MODEL)
        y, yc = token_mixer(modulate(x, mod, 0), modulate(xc, mod_c, 0), ang_row, ang_col,
                            w_in[layer], g_q[layer], w_uq[layer], g_kv[layer], w_ukv[layer],
                            ml_conv_w[layer], ml_conv_b[layer], w_mq[layer], w_mk[layer], b_gate[layer],
                            g_hn[layer], w_out[layer], update_ctx)
        x = layer_norm(ALPHA * x + mod[..., 2, :] * y, ln1_g[layer], ln1_b[layer])
        f = conv_ffn(modulate(x, mod, 3), w_up[layer], ffn_conv_w[layer], ffn_conv_b[layer], w_down[layer])
        x = layer_norm(ALPHA * x + mod[..., 5, :] * f, ln2_g[layer], ln2_b[layer])
        if update_ctx:
            xc = layer_norm(ALPHA * xc + mod_c[..., 2, :] * yc, ln1_g[layer], ln1_b[layer])
            fc = conv_ffn(modulate(xc, mod_c, 3), w_up[layer], ffn_conv_w[layer], ffn_conv_b[layer], w_down[layer])
            xc = layer_norm(ALPHA * xc + mod_c[..., 5, :] * fc, ln2_g[layer], ln2_b[layer])
    return x


_drawn_inputs = setup_inputs


def setup_inputs(seed=0):
    import zlib

    import numpy as np

    out = dict(_drawn_inputs(seed))
    spreads = {}
    factors = {'ctx': 3.917,
     'c_ctx': 3.521,
     'b_ada': 4.956,
     'g_q': 8.0,
     'w_uq': 6.584,
     'g_kv': 8.0,
     'ml_conv_b': 8.0,
     'g_hn': 61.197,
     'ln1_g': 7.672,
     'ln1_b': 7.775,
     'ffn_conv_b': 25.477,
     'ln2_g': 8.252,
     'ln2_b': 7.763}
    for name, (base, spread) in spreads.items():
        noise = np.random.default_rng([zlib.crc32(name.encode()), seed]).standard_normal(out[name].shape)
        drawn = base * np.exp(spread * noise) if base else spread * noise
        out[name] = jnp.asarray(drawn.astype(out[name].dtype))
    for name, factor in factors.items():
        out[name] = (out[name] * factor).astype(out[name].dtype)
    return out
```

```python
from contextlib import ExitStack

import numpy as np

import concourse.bass as bass
from concourse import mybir

F32 = mybir.dt.float32
F32R = mybir.dt.float32r
ALU = mybir.AluOpType
ACT = mybir.ActivationFunctionType
AX = mybir.AxisListType

P = 128
D = 2048
KT = D // P
LAT = 512
CTX = 256
TOK = CTX + LAT
GRID_W = 64
HEADS = 8
NOPE = 128
ROPE = 64
VD = 128
QD = NOPE + ROPE
Q_LORA = 512
KV_LORA = 256
QK = 4
KVK = 2
ML_HEADS = 4
ML_QK = 128
ML_V = 256
ML_INNER = ML_HEADS * ML_V
UK = ML_INNER // P
N_GATES = 16
D_FF = 5632
FC = D_FF // P
OFF_CKV = Q_LORA
OFF_KR = Q_LORA + KV_LORA
OFF_U = OFF_KR + ROPE
OFF_V = OFF_U + ML_INNER
OFF_O = OFF_V + ML_INNER
OFF_G = OFF_O + ML_INNER
TB = TOK // P
LB = LAT // P
CB = CTX // P
ALPHA = 2.0 ** 0.25
EPS = 1e-6
ATT_SCALE = float(QD) ** -0.5
ML_SCALE = float(ML_QK) ** -0.5
EXP_MAX = 87.0

V_ADA = 0
V_GQ = 96
V_GKV = 100
V_GHN = 102
V_MLW = 128
V_MLB = 152
V_LN1G = 160
V_LN1B = 176
V_FB = 192
V_FW = 256
V_ALL = V_FW + 3 * FC

C_SWAP = 0
C_KDUP = 128
C_KSWAP = 256
C_COS = 384
C_SIN = C_COS + LAT
C_MASKF = C_SIN + LAT
C_MASKB = C_MASKF + P
C_SEL = C_MASKB + P
C_ALL = C_SEL + ML_HEADS * P


def host_constants():
    c = np.zeros((P, C_ALL), np.float32)
    part = np.array([r + 16 if r % 32 < 16 else r - 16 for r in range(ROPE)])
    for m in range(P):
        h, r = divmod(m, ROPE)
        c[h * ROPE + part[r], C_SWAP + m] = 1.0
        c[ROPE + r, C_KDUP + m] = 1.0
        c[ROPE + part[r], C_KSWAP + m] = 1.0
    inv = np.float32(10000.0) ** (-np.arange(16, dtype=np.float32) / 16)
    t = np.arange(LAT)
    pos = np.stack([t // GRID_W, t % GRID_W]).astype(np.float32)
    for m in range(P):
        r = m % ROPE
        ang = (pos[r // 32] * inv[r % 16]).astype(np.float32)
        c[m, C_COS:C_COS + LAT] = np.cos(ang)
        c[m, C_SIN:C_SIN + LAT] = np.sin(ang) * (-1.0 if r % 32 < 16 else 1.0)
    s, q = np.meshgrid(np.arange(P), np.arange(P), indexing="ij")
    c[:, C_MASKF:C_MASKF + P] = s <= q
    c[:, C_MASKB:C_MASKB + P] = s >= q
    for h in range(ML_HEADS):
        c[h, C_SEL + h * P:C_SEL + (h + 1) * P] = 1.0
    return c, np.eye(P, dtype=np.float32)


KB = 1024
SB0 = 16512


class Chain:

    def __init__(self, eng, sem):
        self.eng, self.sem, self.n = eng, sem, 0

    def at(self, value):
        self.n = value

    def after(self, ins):
        ins.then_inc(self.sem, 1)
        self.n = self.n + 1
        self.eng.wait_ge(self.sem, self.n)


class StageSems:

    def __init__(self, nc):
        self.nc, self.stack, self.handles, self.last = nc, ExitStack(), [], None

    def __call__(self, name):
        handle = self.stack.enter_context(self.nc.semaphore(name))
        self.handles.append(handle)
        return handle

    def clear_last(self, pool):
        for handle in self.last.handles:
            pool.sem_clear(handle)

    def close(self):
        self.stack.close()


def load_and_modulate(nc, io, sb, sem, psum):
    ident, ones, vecs, cT, modT = sb["ident"], sb["ones"], sb["vecs"], sb["cT"], sb["modT"]
    ps = psum["all"]
    vrows = nc.alloc_sbuf_tensor_at("a_vrows", [P, 5, P], F32, offset=SB0 + 204 * KB)
    ccrow = nc.alloc_sbuf_tensor_at("a_ccrow", [32, P], F32, offset=SB0 + 207 * KB)
    wada = nc.alloc_sbuf_tensor_at("a_wada", [P, 4, 4, 512], F32, offset=SB0 + 118 * KB)
    xnat = nc.alloc_sbuf_tensor_at("a_xnat", [P, TB, D], F32, offset=SB0 + 150 * KB)
    mrows = nc.alloc_sbuf_tensor_at("a_mrows", [2, 8, 512], F32, offset=SB0 + 22 * KB)
    xmod = nc.alloc_sbuf_tensor_at("a_xmod", [P, 2, TOK], F32, offset=SB0 + 198 * KB)
    hT_hi, hT_lo = sb["hT_hi"], sb["hT_lo"]
    NJ = 2 * D // 512

    small_in = sem("a_small_in")
    x_in = sem("a_x_in")
    w_in = [sem(f"a_w_in{s}") for s in range(4)]
    zeroed = sem("a_zeroed")
    silu_done = sem("a_silu_done")
    turned = sem("a_turned")
    turned_kept = sem("a_turned_kept")
    w_used = sem("a_w_used")
    rows_kept = sem("a_rows_kept")
    mod_turned = sem("a_mod_turned")
    mod_ready = sem("a_mod_ready")
    x_turned = sem("a_x_turned")
    xmod_ready = sem("a_xmod_ready")
    hi_ready = sem("a_hi_ready")
    lo_ready = sem("a_lo_ready")
    dve_own = sem("a_dve_own")

    def rows(ap):
        return ap.rearrange("(r p) -> r p", p=P)

    block = nc.Block()
    with block as block:
        @block.sync
        def _(sp):
            sp.dma_start(ident[:], io["ident"]).then_inc(small_in, 16)
            sp.dma_start(ccrow[0:16, :], rows(io["c"][0])).then_inc(small_in, 16)
            sp.dma_start(ccrow[16:32, :], rows(io["c_ctx"])).then_inc(small_in, 16)
            at = [(0, V_ADA, rows(io["b_ada"][0])), (0, V_GQ, rows(io["g_q"][0])), (0, V_GKV, rows(io["g_kv"][0])),
                  (0, V_GHN, io["g_hn"][0].rearrange("h (a p) -> (h a) p", p=P)),
                  (1, V_MLW, io["ml_conv_w"][0].rearrange("w (a p) -> (w a) p", p=P)),
                  (1, V_MLB, rows(io["ml_conv_b"][0])), (1, V_LN1G, rows(io["ln1_g"][0])),
                  (1, V_LN1B, rows(io["ln1_b"][0])), (1, V_FB, rows(io["ffn_conv_b"][0]))]
            for b, v, src in at:
                r = v - b * P
                sp.wait_ge(zeroed, 1)
                sp.dma_start(vrows[r:r + src.shape[0], b, :], src).then_inc(small_in, 16)
            fw = io["ffn_conv_w"][0].rearrange("w (a p) -> (w a) p", p=P)
            sp.dma_start(vrows[:, 2, :], fw[0:P]).then_inc(small_in, 16)
            sp.dma_start(vrows[0:3 * FC - P, 3, :], fw[P:3 * FC]).then_inc(small_in, 16)
            wv = io["w_ada"][0].rearrange("(k p) m -> p k m", p=P)
            for s in range(4):
                sp.dma_start(wada[:, s], wv[:, 4 * s:4 * s + 4, 0:512]).then_inc(w_in[s], 16)
            for b in range(TB):
                src = io["ctx"][0, b * P:(b + 1) * P, :] if b < CB else io["x"][0, (b - CB) * P:(b - CB + 1) * P, :]
                sp.dma_start(xnat[:, b, :], src).then_inc(x_in, 16)
            with sp.Fori(1, NJ) as j:
                for s in range(4):
                    sp.wait_ge(w_used, 4 * j + s - 3)
                    sp.dma_start(wada[:, s], wv[:, 4 * s:4 * s + 4, bass.ds(j * 512, 512)]).then_inc(w_in[s], 16)

        @block.gpsimd
        def _(pool):
            nc.gpsimd.memset(vrows[:], 0.0).then_inc(zeroed, 1)

        @block.scalar
        def _(act):
            act.wait_ge(small_in, 16 * 14)
            nc.scalar.activation(ccrow[:], ccrow[:], ACT.Silu).then_inc(silu_done, 1)
            with act.Fori(0, NJ // 2) as i:
                for e in range(2):
                    act.wait_ge(w_used, 8 * i + 4 * e + 4)
                    nc.scalar.activation(mrows[:, bass.ds(2 * i + e, 1), :], ps[0:2, e:e + 1, :],
                                         ACT.Copy).then_inc(rows_kept, 1)
            for k in range(KT):
                act.wait_ge(xmod_ready, k + 1)
                nc.scalar.activation(hT_hi[:, k, :], xmod[:, k % 2, :], ACT.Copy).then_inc(hi_ready, 1)

        @block.vector
        def _(dve):
            own = Chain(dve, dve_own)
            nc.vector.memset(ones[:], 1.0)
            nc.vector.memset(sb["eps"][:], EPS)
            dve.wait_ge(turned, 1)
            nc.vector.tensor_copy(cT[:], ps[:, 7, 0:32]).then_inc(turned_kept, 1)
            dve.wait_ge(turned, 2)
            own.after(nc.vector.tensor_copy(vecs[:], ps[:, 6, 0:V_ALL]))
            dve.wait_ge(mod_turned, 1)
            mt = ps[:, 4, 0:64].rearrange("p (a b) -> p a b", b=2)
            for b in range(2):
                last = nc.vector.tensor_tensor(modT[:, :, b], mt[:, :, b], vecs[:, V_ADA:V_ADA + 32], ALU.add)
            own.after(last)
            own.after(nc.vector.tensor_scalar(modT[:, KT:2 * KT, :], modT[:, KT:2 * KT, :], 1.0, None, ALU.add))
            def lo_part(k):
                dve.wait_ge(hi_ready, k + 1)
                nc.vector.tensor_tensor(hT_lo[:, k, :], xmod[:, k % 2, :], hT_hi[:, k, :].bitcast(F32),
                                        ALU.subtract).then_inc(lo_ready, 1)

            for k in range(KT):
                dve.wait_ge(x_turned, k + 1)
                if k >= 2:
                    dve.wait_ge(lo_ready, k - 1)
                pst = ps[:, 2 * (k % 2):2 * (k % 2) + 2, :].rearrange("p a b -> p (a b)")
                nc.vector.tensor_scalar(xmod[:, k % 2, 0:CTX], pst[:, 0:CTX], modT[:, k + KT, 1:2],
                                        modT[:, k, 1:2], ALU.mult, ALU.add)
                nc.vector.tensor_scalar(xmod[:, k % 2, CTX:TOK], pst[:, CTX:TOK], modT[:, k + KT, 0:1],
                                        modT[:, k, 0:1], ALU.mult, ALU.add).then_inc(xmod_ready, 1)
                if k >= 1:
                    lo_part(k - 1)
            lo_part(KT - 1)

        @block.tensor
        def _(pe):
            pe.wait_ge(silu_done, 1)
            nc.tensor.transpose(ps[:, 7, 0:32], ccrow[:], ident[0:32, 0:32]).then_inc(turned, 1)
            for b in range(3):
                nc.tensor.transpose(ps[:, 6, b * P:(b + 1) * P], vrows[:, b, :], ident[:])
            nc.tensor.transpose(ps[:, 6, 3 * P:V_ALL], vrows[0:V_ALL - 3 * P, 3, :], ident[0:V_ALL - 3 * P, 0:V_ALL - 3 * P]).then_inc(turned, 1)
            pe.wait_ge(turned_kept, 1)
            pe.wait_ge(dve_own, 1)
            with pe.Fori(0, NJ // 2) as i:
                for e in range(2):
                    pe.wait_ge(rows_kept, 2 * i)
                    for s in range(4):
                        pe.wait_ge(w_in[s], 32 * i + 16 * e + 16)
                        for k in range(4):
                            kt = 4 * s + k
                            mm = nc.tensor.matmul(ps[0:2, e, :], cT[:, kt:kt + KT + 1:KT], wada[:, s, k, :],
                                                  start=(kt == 0), stop=(kt == KT - 1))
                        mm.then_inc(w_used, 1)
            pe.wait_ge(rows_kept, NJ)
            for n in range(32):
                mm = nc.tensor.transpose(ps[:, 4, 2 * n:2 * n + 2], mrows[:, n // 4, (n % 4) * P:(n % 4 + 1) * P], ident[0:2, 0:2])
            mm.then_inc(mod_turned, 1)
            pe.wait_ge(x_in, 16 * TB)
            pe.wait_ge(dve_own, 3)
            for k in range(KT):
                if k >= 2:
                    pe.wait_ge(xmod_ready, k - 1)
                for b in range(TB):
                    mm = nc.tensor.transpose(ps[:, 2 * (k % 2) + b // 4, (b % 4) * P:(b % 4 + 1) * P],
                                             xnat[:, b, k * P:(k + 1) * P], ident[:])
                mm.then_inc(x_turned, 1)


def project_in(nc, io, sb, sem, psum):
    vecs, cT = sb["vecs"], sb["cT"]
    ps = psum["all"]
    hT_hi, hT_lo, zq, zkv, krg = sb["hT_hi"], sb["hT_lo"], sb["zq"], sb["zkv"], sb["krg"]
    scratch = io["scratch"]

    def at(name, shape, dtype, kb):
        return nc.alloc_sbuf_tensor_at(name, shape, dtype, offset=SB0 + int(kb * KB))

    raw = at("b_raw", [P, 4, 8 * P], F32, 118)
    w_hi = at("b_w_hi", [P, 2, 8 * P], F32R, 134)
    w_lo = at("b_w_lo", [P, 2, 8 * P], F32R, 142)
    conv = at("b_conv", [P, 2, TOK], F32, 150)
    u_out = at("b_u_out", [P, 2, TOK], F32, 156)
    o_out = at("b_o_out", [P, 2, LAT], F32, 162)
    v_out = at("b_v_out", [P, 2, 512], F32, 166)
    kr_raw = at("b_kr_raw", [P, KT, ROPE], F32, 170)
    g_raw = at("b_g_raw", [P, KT, N_GATES], F32, 174)

    Q0 = 2
    KV0 = Q0 + 2 * QK
    U0 = KV0 + 2 * KVK
    O0 = U0 + 2 * UK
    V0 = O0 + 2 * UK
    N = V0 + 16

    kr_in = sem("b_kr_in")
    raw_in = [sem(f"b_raw_in{s}") for s in range(4)]
    zeroed = sem("b_zeroed")
    hi_ready = sem("b_hi_ready")
    lo_ready = sem("b_lo_ready")
    half_done = sem("b_half_done")
    psum_kept = sem("b_psum_kept")
    conv_ready = sem("b_conv_ready")
    silu_ready = sem("b_silu_ready")
    u_sent = [sem(f"b_u_sent{s}") for s in range(2)]
    o_ready = sem("b_o_ready")
    o_sent = [sem(f"b_o_sent{s}") for s in range(2)]
    v_ready = sem("b_v_ready")
    v_sent = [sem(f"b_v_sent{s}") for s in range(2)]
    dve_own = sem("b_dve_own")

    def fetched(eng, n, it=0):
        eng.wait_ge(raw_in[(n - 2) % 4], 16 * (it + (n - 2) // 4 + 1))

    def hi_part(act, n, it=0):
        fetched(act, n, it)
        act.wait_ge(half_done, 4 * it + n - 1)
        nc.scalar.activation(w_hi[:, n % 2, :], raw[:, (n - 2) % 4, :], ACT.Copy).then_inc(hi_ready, 1)

    def lo_part(dve, n, it=0):
        dve.wait_ge(hi_ready, 4 * it + n + 1)
        nc.vector.tensor_tensor(w_lo[:, n % 2, :], raw[:, (n - 2) % 4, :], w_hi[:, n % 2, :].bitcast(F32),
                                ALU.subtract).then_inc(lo_ready, 1)

    def krg_parts():
        both = [(64, 64 + ROPE, kr_raw[:, :, :])]
        for d in range(2):
            for g in range(2):
                c0 = (2 * d + g) * ML_HEADS
                both.append((32 * g + 4 * d, 32 * g + 4 * d + 4, g_raw[:, :, c0:c0 + ML_HEADS]))
        return both

    w_hi_full = w_hi[:].rearrange("p s (k m) -> p (s k) m", m=P)
    w_lo_full = w_lo[:].rearrange("p s (k m) -> p (s k) m", m=P)

    block = nc.Block()
    with block as block:
        @block.sync
        def _(sp):
            wv = io["w_in"][0].rearrange("(k p) m -> p k m", p=P)
            sp.dma_start(kr_raw[:], wv[:, :, OFF_KR:OFF_U]).then_inc(kr_in, 16)
            sp.dma_start(g_raw[:], wv[:, :, OFF_G:OFF_G + N_GATES]).then_inc(kr_in, 16)

            def fetch(n, col, half, it=0):
                s = (n - 2) % 4
                sp.dma_start(raw[:, s, :].rearrange("p (k m) -> p k m", m=P),
                             wv[:, 8 * half:8 * half + 8, bass.ds(col, P)]).then_inc(raw_in[s], 16)

            for n in range(4):
                fetch(Q0 + n, n // 2 * P, n % 2)
            for n0, n1, col0 in [(Q0 + 4, KV0, 2 * P), (KV0, U0, OFF_CKV), (U0, O0, OFF_U), (O0, V0, OFF_O)]:
                with sp.Fori(0, (n1 - n0) // 4) as i:
                    for s in range(4):
                        sp.wait_ge(lo_ready, 4 * i + n0 + s - 3)
                        fetch(n0 + s, col0 + i * 2 * P + s // 2 * P, s % 2)
            for c in range(2):
                with sp.Fori(0, 2) as i:
                    for s in range(4):
                        sp.wait_ge(lo_ready, 4 * i + V0 + 8 * c + s - 3)
                        sp.dma_start(raw[:, s, :].rearrange("p (k m) -> p k m", m=512),
                                     wv[:, bass.ds(i * 8 + 2 * s, 2), OFF_V + 512 * c:OFF_V + 512 * (c + 1)])\
                          .then_inc(raw_in[s], 16)

        @block.gpsimd
        def _(pool):
            sem.clear_last(pool)
            nc.gpsimd.memset(w_hi[:].bitcast(F32), 0.0)
            nc.gpsimd.memset(w_lo[:].bitcast(F32), 0.0).then_inc(zeroed, 1)
            sum_ada(nc, io, sb, sem, pool, range(0, 5))

        @block.scalar
        def _(act):
            act.wait_ge(kr_in, 32)
            act.wait_ge(zeroed, 1)
            for a, b, src in krg_parts():
                last = nc.scalar.activation(w_hi_full[:, :, a:b], src, ACT.Copy)
            last.then_inc(hi_ready, 2)
            hi_part(act, Q0)
            act.wait_ge(half_done, 2)
            nc.scalar.activation(krg[:, 0:CTX], ps[:, 2, 0:CTX], ACT.Copy)
            nc.scalar.activation(krg[:, CTX:TOK], ps[:, 0, :], ACT.Copy).then_inc(psum_kept, 1)

            def chunks(n0, n1, keep):
                with act.Fori(0, (n1 - n0) // 4) as i:
                    for s in range(4):
                        hi_part(act, n0 + s + 1, i)
                        if s % 2:
                            keep(i, s // 2)

            def keep_q(i, e):
                act.wait_ge(half_done, 4 * i + Q0 + 2 * e + 2)
                nc.scalar.activation(zq[:, bass.ds(2 * i + e, 1), :], ps[:, 1 - e:2 - e, :], ACT.Copy).then_inc(psum_kept, 1)

            def keep_kv(i, e):
                act.wait_ge(half_done, 4 * i + KV0 + 2 * e + 2)
                nc.scalar.activation(zkv[:, e, 0:CTX], ps[:, 3 - e, 0:CTX], ACT.Copy)
                nc.scalar.activation(zkv[:, e, CTX:TOK], ps[:, 1 - e, :], ACT.Copy).then_inc(psum_kept, 1)

            def keep_u(i, e):
                act.wait_ge(conv_ready, 2 * i + e + 1)
                act.wait_ge(u_sent[e], 16 * i)
                nc.scalar.activation(u_out[:, e, :], conv[:, e, :], ACT.Silu).then_inc(silu_ready, 1)
                act.wait_ge(silu_ready, 2 * i + e + 1)
                act.dma_start(scratch["u"][bass.ds(2 * i + e, 1)].rearrange("a p t -> p a t"), u_out[:, e:e + 1, :])\
                   .then_inc(u_sent[e], 16)

            def keep_o(i, e):
                act.wait_ge(half_done, 4 * i + O0 + 2 * e + 2)
                act.wait_ge(o_sent[e], 16 * i)
                nc.scalar.activation(o_out[:, e, :], ps[:, 1 - e, :], ACT.Sigmoid).then_inc(o_ready, 1)
                act.wait_ge(o_ready, 2 * i + e + 1)
                act.dma_start(scratch["o"][bass.ds(2 * i + e, 1)].rearrange("a p t -> p a t"), o_out[:, e:e + 1, :])\
                   .then_inc(o_sent[e], 16)

            chunks(Q0, KV0, keep_q)
            chunks(KV0, U0, keep_kv)
            chunks(U0, O0, keep_u)
            chunks(O0, V0, keep_o)
            for c in range(2):
                for s in range(8):
                    n = V0 + 8 * c + s
                    if n + 1 < N:
                        hi_part(act, n + 1)
                act.wait_ge(half_done, V0 + 8 * c + 8)
                for t in range(TB):
                    e = t % 2
                    if 6 * c + t >= 2:
                        act.wait_ge(v_sent[e], 16 * ((6 * c + t) // 2))
                    nc.scalar.activation(v_out[:, e, :], ps[:, 2 + t, :], ACT.Copy).then_inc(v_ready, 1)
                    act.wait_ge(v_ready, 6 * c + t + 1)
                    act.dma_start(scratch["v"][t, :, 512 * c:512 * (c + 1)], v_out[:, e, :]).then_inc(v_sent[e], 16)
            for e in range(2):
                act.wait_ge(u_sent[e], 16 * UK // 2)
                act.wait_ge(o_sent[e], 16 * UK // 2)
                act.wait_ge(v_sent[e], 16 * TB)

        @block.vector
        def _(dve):
            dve.wait_ge(hi_ready, 2)
            for a, b, src in krg_parts():
                last = nc.vector.tensor_tensor(w_lo_full[:, :, a:b], src, w_hi_full[:, :, a:b].bitcast(F32), ALU.subtract)
            last.then_inc(lo_ready, 2)
            lo_part(dve, Q0)
            own = Chain(dve, dve_own)

            def chunks(n0, n1, then=None):
                with dve.Fori(0, (n1 - n0) // 4) as i:
                    for s in range(4):
                        lo_part(dve, n0 + s + 1, i)
                        if then and s % 2:
                            then(i, s // 2)

            def convolve(i, e):
                dve.wait_ge(half_done, 4 * i + U0 + 2 * e + 2)
                dve.wait_ge(silu_ready, 2 * i)
                own.at(2 * (2 * i + e))
                parts = [(ps[:, 3 - e, 0:CTX], conv[:, e, 0:CTX], CTX), (ps[:, 1 - e, :], conv[:, e, CTX:TOK], LAT)]

                def w(j):
                    return vecs[:, bass.ds(2 * i + (V_MLW + 8 * j + e), 1)]

                for src, dst, n in parts:
                    last = nc.vector.tensor_scalar(dst, src, w(1), vecs[:, bass.ds(2 * i + (V_MLB + e), 1)],
                                                   ALU.mult, ALU.add)
                own.after(last)
                for src, dst, n in parts:
                    last = nc.vector.scalar_tensor_tensor(dst[:, 1:n], src[:, 0:n - 1], w(0), dst[:, 1:n],
                                                          ALU.mult, ALU.add)
                own.after(last)
                for src, dst, n in parts:
                    last = nc.vector.scalar_tensor_tensor(dst[:, 0:n - 1], src[:, 1:n], w(2), dst[:, 0:n - 1],
                                                          ALU.mult, ALU.add)
                last.then_inc(conv_ready, 1)

            chunks(Q0, KV0)
            chunks(KV0, U0)
            chunks(U0, O0, convolve)
            chunks(O0, V0)
            for n in range(V0, N - 1):
                lo_part(dve, n + 1)

        @block.tensor
        def _(pe):
            def chunk(n, it, lat, ctx, w_step=None):
                for half in range(2):
                    pe.wait_ge(lo_ready, 4 * it + n + half + 1)
                    for k in range(8):
                        kt = 8 * half + k
                        for p, (w, h) in enumerate([(w_hi, hT_hi), (w_hi, hT_lo), (w_lo, hT_hi)]):
                            first, last = kt == 0 and p == 0, kt == KT - 1 and p == 2
                            lhs = w[:, (n + half) % 2, k * P:(k + 1) * P]
                            if ctx is not None:
                                nc.tensor.matmul(ps[:, ctx, 0:CTX], lhs, h[:, kt, 0:CTX], start=first, stop=last)
                            mm = nc.tensor.matmul(ps[:, lat, :], lhs, h[:, kt, CTX:TOK], start=first, stop=last)
                    mm.then_inc(half_done, 1)

            chunk(0, 0, 0, 2)
            with pe.Fori(0, QK // 2) as i:
                for e in range(2):
                    pe.wait_ge(psum_kept, 2 * i + e)
                    chunk(Q0 + 2 * e, i, 1 - e, None)
            for e in range(2):
                pe.wait_ge(psum_kept, QK + e)
                chunk(KV0 + 2 * e, 0, 1 - e, 3 - e)
            X0 = 1 + QK + KVK
            pe.wait_ge(psum_kept, X0)
            with pe.Fori(0, UK // 2) as i:
                for e in range(2):
                    pe.wait_ge(conv_ready, 2 * i)
                    chunk(U0 + 2 * e, i, 1 - e, 3 - e)
            pe.wait_ge(conv_ready, UK)
            with pe.Fori(0, UK // 2) as i:
                for e in range(2):
                    pe.wait_ge(o_ready, 2 * i)
                    chunk(O0 + 2 * e, i, 1 - e, None)
            for c in range(2):
                for s in range(8):
                    n = V0 + 8 * c + s
                    pe.wait_ge(lo_ready, n + 1)
                    for k in range(2):
                        kt = 2 * s + k
                        for t in range(TB):
                            if c and kt == 0:
                                pe.wait_ge(v_ready, t + 1)
                            for p, (w, h) in enumerate([(w_hi, hT_hi), (w_hi, hT_lo), (w_lo, hT_hi)]):
                                mm = nc.tensor.matmul(ps[:, 2 + t, :], h[:, kt, t * P:(t + 1) * P],
                                                      w[:, n % 2, k * 512:(k + 1) * 512],
                                                      start=(kt == 0 and p == 0), stop=(kt == KT - 1 and p == 2))
                    mm.then_inc(half_done, 1)


ADA_COLS = 1024


def sum_ada(nc, io, sb, sem, pool, parts):
    cT = sb["cT"]
    tag = f"ada{parts[0]}"

    def at(name, shape, kb):
        return nc.alloc_sbuf_tensor_at(f"{tag}_{name}", shape, F32, offset=SB0 + int(kb * KB))

    w = at("w", [P, 4, ADA_COLS], 179)
    acc = at("acc", [P, ADA_COLS], 195)
    prod = at("prod", [P, 2, ADA_COLS], 199)
    w_in = [sem(f"{tag}_w_in{s}") for s in range(4)]
    own_sem = sem(f"{tag}_own")
    sent = sem(f"{tag}_sent")
    wv = io["w_ada"][0].rearrange("(k p) m -> p k m", p=P)
    own = Chain(pool, own_sem)

    def fetch(part, k):
        c0 = 2 * D + part * ADA_COLS
        pool.dma_start(w[:, k % 4, :], wv[:, k, c0:c0 + ADA_COLS] if isinstance(part, int) else
                       wv[:, k, bass.ds(c0, ADA_COLS)]).then_inc(w_in[k % 4], 16)

    with pool.Fori(0, len(parts)) as i:
        part = i + parts[0]
        own.at((2 * KT - 1) * i)
        for k in range(3):
            fetch(part, k)
        pool.wait_ge(sent, 16 * i)
        for k in range(KT):
            pool.wait_ge(w_in[k % 4], 64 * i + 16 * (k // 4 + 1))
            out = acc[:] if k == 0 else prod[:, k % 2, :]
            own.after(nc.gpsimd.tensor_tensor(out, w[:, k % 4, :], cT[:, k:k + 1].to_broadcast([P, ADA_COLS]), ALU.mult))
            if k + 3 < KT:
                fetch(part, k + 3)
            if k:
                own.after(nc.gpsimd.tensor_tensor(acc[:], acc[:], prod[:, k % 2, :], ALU.add))
        pool.dma_start(io["scratch"]["ada"][bass.ds(part, 1)].rearrange("a p m -> p a m"), acc[:]).then_inc(sent, 16)
    pool.wait_ge(sent, 16 * len(parts))


def attention(nc, io, sb, sem, psum):
    vecs, ident, ones = sb["vecs"], sb["ident"], sb["ones"]
    ps = psum["all"]
    zq, zkv, krg, yT = sb["zq"], sb["zkv"], sb["krg"], sb["yT"]

    def at(name, shape, kb):
        return nc.alloc_sbuf_tensor_at(name, shape, F32, offset=SB0 + int(kb * KB))

    wq = at("c_wq", [P, 2, QK, 2 * QD], 54)
    wkv = at("c_wkv", [P, 2, KVK, 4 * P], 66)
    kr2 = at("c_kr2", [P, TOK], 74)
    cst = at("c_cst", [P, C_MASKF], 77)
    qn = at("c_qn", [P, 2, LAT], 83)
    qr = at("c_qr", [P, LAT], 87)
    qr_raw = at("c_qr_raw", [P, LAT], 89)
    rot = at("c_rot", [P, LAT], 91)
    kn = at("c_kn", [P, 2, TOK], 93)
    vv = at("c_v", [P, TB, 2 * VD], 99)
    prob = at("c_prob", [P, 2, TOK], 106)
    probT = at("c_probT", [P, 2, TB, LAT], 112)
    sq = at("c_sq", [P, QK, TOK], 136)
    rms = at("c_rms", [P, 2, TOK], 148)
    stat = at("c_stat", [P, 4, 2 * LB * 2], 178)

    cst_in = sem("c_cst_in")
    w_in = [sem(f"c_w_in{s}") for s in range(2)]
    sq_ready = sem("c_sq_ready")
    sum_ready = sem("c_sum_ready")
    root_ready = sem("c_root_ready")
    norm_ready = sem("c_norm_ready")
    kr_turned = sem("c_kr_turned")
    kr_ready = sem("c_kr_ready")
    proj_done = sem("c_proj_done")
    proj_kept = sem("c_proj_kept")
    swap_done = sem("c_swap_done")
    qr_ready = sem("c_qr_ready")
    scores_done = sem("c_scores_done")
    negmax_ready = sem("c_negmax_ready")
    exp_ready = sem("c_exp_ready")
    prob_ready = sem("c_prob_ready")
    turned = sem("c_turned")
    turned_kept = sem("c_turned_kept")
    out_done = sem("c_out_done")
    out_kept = sem("c_out_kept")
    dve_own = sem("c_dve_own")

    PAIRS = HEADS // 2
    U = 2 * LB
    def scores(u):
        return ps[:, 2 * (u % 2):2 * (u % 2) + 2, :].rearrange("p a b -> p (a b)")[:, 0:TOK]

    turned_ps = ps[:, 4:6, :].rearrange("p a b -> p (a b)")[:, 0:TOK]

    block = nc.Block()
    with block as block:
        @block.sync
        def _(sp):
            sp.dma_start(cst[:], io["consts"][:, 0:C_MASKF]).then_inc(cst_in, 16)
            uq = io["w_uq"][0].rearrange("(k p) m -> p k m", p=P)
            ukv = io["w_ukv"][0].rearrange("(k p) m -> p k m", p=P)

            def fetch(pair, s):
                for e in range(2):
                    c0 = pair * 2 * QD + e * QD
                    sp.dma_start(wq[:, s, :, e * NOPE:(e + 1) * NOPE], uq[:, :, bass.ds(c0, NOPE)]).then_inc(w_in[s], 16)
                    sp.dma_start(wq[:, s, :, 2 * NOPE + e * ROPE:2 * NOPE + (e + 1) * ROPE],
                                 uq[:, :, bass.ds(c0 + NOPE, ROPE)]).then_inc(w_in[s], 16)
                sp.dma_start(wkv[:, s], ukv[:, :, bass.ds(pair * 4 * P, 4 * P)]).then_inc(w_in[s], 16)

            for s in range(2):
                fetch(s, s)
            with sp.Fori(1, PAIRS // 2) as i:
                for s in range(2):
                    sp.wait_ge(proj_done, 10 * (2 * i + s))
                    fetch(2 * i + s, s)

        @block.gpsimd
        def _(pool):
            sem.clear_last(pool)
            sum_ada(nc, io, sb, sem, pool, range(5, 7))

        def keep_turned(act, pair, u):
            act.wait_ge(turned, U * pair + u + 1)
            e, b = divmod(u, LB)
            nc.scalar.activation(probT[:, e, :, b * P:(b + 1) * P], turned_ps.rearrange("p (a b) -> p a b", b=P),
                                 ACT.Copy).then_inc(turned_kept, 1)

        @block.scalar
        def _(act):
            nc.scalar.activation(sq[:, :, 0:LAT], zq[:], ACT.Square).then_inc(sq_ready, 1)
            act.wait_ge(sum_ready, 1)
            nc.scalar.activation(rms[:, 0, 0:LAT], ps[:, 0, :], ACT.Sqrt, bias=sb["eps"][:],
                                 scale=1.0 / Q_LORA).then_inc(root_ready, 1)
            nc.scalar.activation(sq[:, 0:KVK, :], zkv[:], ACT.Square).then_inc(sq_ready, 1)
            act.wait_ge(sum_ready, 2)
            nc.scalar.activation(rms[:, 1, :], ps[:, 2:4, :].rearrange("p a b -> p (a b)")[:, 0:TOK], ACT.Sqrt,
                                 bias=sb["eps"][:], scale=1.0 / KV_LORA).then_inc(root_ready, 1)
            with act.Fori(0, PAIRS // 2) as i:
                for s in range(2):
                    pair = 2 * i + s
                    for n in range(10):
                        act.wait_ge(proj_done, 10 * pair + n + 1)
                        bank = 6 + n % 2
                        if n == 0:
                            act.wait_ge(qr_ready, 1 * pair)
                            dst, src = qr_raw[:], ps[:, bank, :]
                        elif n < 3:
                            dst, src = qn[:, n - 1, :], ps[:, bank, :]
                        elif n < 7:
                            e, half = divmod(n - 3, 2)
                            cols = slice(0, CTX) if half == 0 else slice(CTX, TOK)
                            dst, src = kn[:, e, cols], ps[:, bank, 0:cols.stop - cols.start]
                        else:
                            t = 2 * (n - 7)
                            dst, src = vv[:, t:t + 2, :], ps[:, bank, :].rearrange("p (a b) -> p a b", a=2)
                        nc.scalar.activation(dst, src, ACT.Copy).then_inc(proj_kept, 1)
                    for u in range(U):
                        act.wait_ge(negmax_ready, U * pair + u + 1)
                        if u >= 2:
                            act.wait_ge(turned, U * pair + u - 1)
                        nc.scalar.activation(prob[:, u % 2, :], scores(u), ACT.Exp, bias=stat[:, 0, u:u + 1],
                                             scale=ATT_SCALE, accum_out=stat[:, 1, u:u + 1]).then_inc(exp_ready, 1)
                        if u >= 1:
                            keep_turned(act, pair, u - 1)
                    keep_turned(act, pair, U - 1)
                    for e in range(2):
                        act.wait_ge(out_done, 2 * pair + e + 1)
                        nc.scalar.activation(yT[:, bass.ds(2 * pair + e, 1), :], ps[:, 6 + e:7 + e, :],
                                             ACT.Copy).then_inc(out_kept, 1)

        @block.vector
        def _(dve):
            own = Chain(dve, dve_own)
            for r, z, nk, v, n in [(0, zq, QK, V_GQ, LAT), (1, zkv, KVK, V_GKV, TOK)]:
                dve.wait_ge(root_ready, r + 1)
                own.after(nc.vector.reciprocal(rms[:, r, 0:n], rms[:, r, 0:n]))
                for k in range(nk):
                    last = nc.vector.scalar_tensor_tensor(z[:, k, :], z[:, k, :], vecs[:, v + k:v + k + 1],
                                                          rms[:, r, 0:n], ALU.mult, ALU.mult)
                last.then_inc(norm_ready, 1)
            dve.wait_ge(kr_turned, 1)
            dve.wait_ge(cst_in, 16)
            nc.vector.tensor_copy(kr2[:, 0:CTX], ps[:, 4, 0:CTX])
            nc.vector.tensor_tensor(kr2[:, CTX:TOK], ps[:, 5, :], cst[:, C_COS:C_COS + LAT], ALU.mult)
            own.after(nc.vector.tensor_tensor(rot[:], ps[:, 6, :], cst[:, C_SIN:C_SIN + LAT], ALU.mult))
            nc.vector.tensor_tensor(kr2[:, CTX:TOK], kr2[:, CTX:TOK], rot[:], ALU.add).then_inc(kr_ready, 1)
            base = own.n
            with dve.Fori(0, PAIRS) as pair:
                own.at(base + (1 + 2 * U) * pair)
                dve.wait_ge(swap_done, pair + 1)
                dve.wait_ge(proj_kept, 10 * pair + 10)
                dve.wait_ge(scores_done, U * pair)
                nc.vector.tensor_tensor(rot[:], ps[:, 5, :], cst[:, C_SIN:C_SIN + LAT], ALU.mult)
                own.after(nc.vector.tensor_tensor(qr[:], qr_raw[:], cst[:, C_COS:C_COS + LAT], ALU.mult))
                nc.vector.tensor_tensor(qr[:], qr[:], rot[:], ALU.add).then_inc(qr_ready, 1)
                for u in range(U):
                    dve.wait_ge(scores_done, U * pair + u + 1)
                    own.after(nc.vector.tensor_reduce(stat[:, 2, u:u + 1], scores(u), AX.X, ALU.max))
                    nc.vector.tensor_scalar(stat[:, 0, u:u + 1], stat[:, 2, u:u + 1], -ATT_SCALE, None, ALU.mult)\
                      .then_inc(negmax_ready, 1)
                    dve.wait_ge(exp_ready, U * pair + u + 1)
                    own.after(nc.vector.reciprocal(stat[:, 2, U + u:U + u + 1], stat[:, 1, u:u + 1]))
                    nc.vector.tensor_scalar(prob[:, u % 2, :], prob[:, u % 2, :], stat[:, 2, U + u:U + u + 1], None,
                                            ALU.mult).then_inc(prob_ready, 1)

        @block.tensor
        def _(pe):
            pe.wait_ge(sq_ready, 1)
            for k in range(QK):
                mm = nc.tensor.matmul(ps[:, 0, :], ones[:], sq[:, k, 0:LAT], start=(k == 0), stop=(k == QK - 1))
            mm.then_inc(sum_ready, 1)
            pe.wait_ge(sq_ready, 2)
            for k in range(KVK):
                nc.tensor.matmul(ps[:, 2, :], ones[:], sq[:, k, 0:512], start=(k == 0), stop=(k == KVK - 1))
                mm = nc.tensor.matmul(ps[:, 3, 0:TOK - 512], ones[:], sq[:, k, 512:TOK], start=(k == 0), stop=(k == KVK - 1))
            mm.then_inc(sum_ready, 1)
            pe.wait_ge(cst_in, 16)
            kr = krg[ROPE:P, :]
            nc.tensor.matmul(ps[:, 4, 0:CTX], cst[ROPE:P, C_KDUP:C_KDUP + P], kr[:, 0:CTX], start=True, stop=True)
            nc.tensor.matmul(ps[:, 5, :], cst[ROPE:P, C_KDUP:C_KDUP + P], kr[:, CTX:TOK], start=True, stop=True)
            nc.tensor.matmul(ps[:, 6, :], cst[ROPE:P, C_KSWAP:C_KSWAP + P], kr[:, CTX:TOK], start=True,
                             stop=True).then_inc(kr_turned, 1)
            pe.wait_ge(norm_ready, 2)
            pe.wait_ge(kr_ready, 1)
            with pe.Fori(0, PAIRS // 2) as i:
                for s in range(2):
                    pair = 2 * i + s
                    pe.wait_ge(w_in[s], 80 * i + 80)
                    pe.wait_ge(out_kept, 2 * pair)
                    n = 0
                    wkvs = wkv[:, s].rearrange("p k (e m) -> p k e m", m=2 * P)

                    def bank_free(n):
                        if n >= 2:
                            pe.wait_ge(proj_kept, 10 * pair + n - 1)

                    for c0 in (2 * NOPE, 0, NOPE):
                        bank_free(n)
                        for k in range(QK):
                            mm = nc.tensor.matmul(ps[:, 6 + n % 2, :], wq[:, s, k, c0:c0 + P], zq[:, k, :], start=(k == 0), stop=(k == QK - 1))
                        mm.then_inc(proj_done, 1)
                        n += 1
                    pe.wait_ge(proj_kept, 10 * pair + 1)
                    nc.tensor.matmul(ps[:, 5, :], cst[:, C_SWAP:C_SWAP + P], qr_raw[:], start=True, stop=True)\
                      .then_inc(swap_done, 1)
                    for e in range(2):
                        for a, b in [(0, CTX), (CTX, TOK)]:
                            bank_free(n)
                            for k in range(KVK):
                                mm = nc.tensor.matmul(ps[:, 6 + n % 2, 0:b - a], wkvs[:, k, e, 0:NOPE], zkv[:, k, a:b],
                                                      start=(k == 0), stop=(k == KVK - 1))
                            mm.then_inc(proj_done, 1)
                            n += 1
                    for t in range(0, TB, 2):
                        bank_free(n)
                        for tt in range(2):
                            for k in range(KVK):
                                mm = nc.tensor.matmul(ps[:, 6 + n % 2, tt * 256:(tt + 1) * 256],
                                                      zkv[:, k, (t + tt) * P:(t + tt + 1) * P], wkvs[:, k, :, NOPE:2 * P],
                                                      start=(k == 0), stop=(k == KVK - 1))
                        mm.then_inc(proj_done, 1)
                        n += 1

                    def score(u):
                        e, b = divmod(u, LB)
                        if u < 2:
                            pe.wait_ge(prob_ready, U * pair)
                        else:
                            pe.wait_ge(exp_ready, U * pair + u - 1)
                        r = slice(e * ROPE, (e + 1) * ROPE)
                        out = ps[:, 2 * (u % 2):2 * (u % 2) + 2, :]
                        for j, (a, c) in enumerate([(0, 512), (512, TOK)]):
                            nc.tensor.matmul(out[:, j, 0:c - a], qn[:, e, b * P:(b + 1) * P], kn[:, e, a:c], start=True, stop=False)
                            mm = nc.tensor.matmul(out[:, j, 0:c - a], qr[r, b * P:(b + 1) * P], kr2[r, a:c], start=False, stop=True)
                        mm.then_inc(scores_done, 1)

                    def turn(u):
                        pe.wait_ge(prob_ready, U * pair + u + 1)
                        pe.wait_ge(turned_kept, U * pair + u)
                        for t in range(TB):
                            mm = nc.tensor.transpose(ps[:, 4 + t // 4, (t % 4) * P:(t % 4 + 1) * P],
                                                     prob[:, u % 2, t * P:(t + 1) * P], ident[:])
                        mm.then_inc(turned, 1)

                    def weigh(e):
                        pe.wait_ge(turned_kept, U * pair + LB * (e + 1))
                        for t in range(TB):
                            mm = nc.tensor.matmul(ps[:, 6 + e, :], vv[:, t, e * VD:(e + 1) * VD], probT[:, e, t, :],
                                                  start=(t == 0), stop=(t == TB - 1))
                        mm.then_inc(out_done, 1)

                    pe.wait_ge(proj_kept, 10 * pair + 10)
                    pe.wait_ge(qr_ready, pair + 1)
                    for u in range(U + 1):
                        if u < U:
                            score(u)
                        if u >= 1:
                            turn(u - 1)
                        if u == LB + 2:
                            weigh(0)
                    weigh(1)


def matrix_memory(nc, io, sb, sem, psum):
    vecs, ident = sb["vecs"], sb["ident"]
    ps = psum["all"]
    krg, yT = sb["krg"], sb["yT"]
    scratch = io["scratch"]

    def at(name, shape, kb):
        return nc.alloc_sbuf_tensor_at(name, shape, F32, offset=SB0 + int(kb * KB))

    H = ML_HEADS
    mask = at("d_mask", [P, 2, P], 21)
    negmb = at("d_negmb", [P, 2 * H, LAT], 5)
    cols = at("d_cols", [P, 2, TB + LB, H], 207)
    uh = at("d_uh", [P, 2, 2, TOK], 54)
    v1 = at("d_v1", [P, 2, TB, ML_V + 1], 66)
    wm = at("d_wm", [P, 2, 2, 2, P], 79)
    qT = at("d_qT", [P, LAT], 83)
    kT = at("d_kT", [P, TOK], 85)
    sT = at("d_sT", [P, 2, TB, LAT], 88)
    decay = at("d_decay", [P, 2, TB, LAT], 112)
    probT = at("d_probT", [P, 2, TB, LAT], 136)
    hid = at("d_hid", [P, LB, H, ML_V], 160)
    small = at("d_small", [P, 64], 176)
    gate = at("d_gate", [H, 4, TOK], 112)
    soft = at("d_soft", [H, 2, TOK], 124)
    runs = at("d_runs", [H, 2, TOK], 130)
    arow = at("d_arow", [H, 2, TOK], 136)
    mrow = at("d_mrow", [H, 2, LAT], 142)
    erow = at("d_erow", [H, 2, LAT], 146)
    init = at("d_init", [H, 2, 2], 150)
    bias = at("d_bias", [H, 4], 150.25)
    sel = at("d_sel", [H, H * P], 151)
    sig_o = at("d_sig_o", [P, UK, LAT], 54)
    stats = at("d_stats", [P, LB * H, 6], 176.5)
    mv = at("d_mv", [P, LB * H, 2], 177)
    rstd = at("d_rstd", [P, LB * H], 177.5)

    gate_in = sem("d_gate_in")
    const_in = sem("d_const_in")
    mask_in = sem("d_mask_in")
    head_in = [sem(f"d_head_in{s}") for s in range(2)]
    ones_ready = sem("d_ones_ready")
    biased = sem("d_biased")
    soft_own = sem("d_soft_own")
    soft_ready = sem("d_soft_ready")
    arow_ready = sem("d_arow_ready")
    erow_ready = sem("d_erow_ready")
    eexp_ready = sem("d_eexp_ready")
    cols_turned = sem("d_cols_turned")
    cols_ready = sem("d_cols_ready")
    spread = sem("d_spread")
    spread_kept = sem("d_spread_kept")
    qk_done = sem("d_qk_done")
    qk_kept = sem("d_qk_kept")
    s_done = sem("d_s_done")
    s_kept = sem("d_s_kept")
    expo_ready = sem("d_expo_ready")
    decay_ready = sem("d_decay_ready")
    prob_ready = sem("d_prob_ready")
    num_done = sem("d_num_done")
    num_kept = sem("d_num_kept")
    o_in = sem("d_o_in")
    var_ready = sem("d_var_ready")
    root_ready = sem("d_root_ready")
    normed = sem("d_normed")
    y_turned = sem("d_y_turned")
    y_kept = sem("d_y_kept")
    dve_own = sem("d_dve_own")

    def span(d, j):
        return (j * P, LAT) if d == 0 else (0, (j + 1) * P)

    block = nc.Block()
    with block as block:
        @block.sync
        def _(sp):
            for d in range(2):
                for g in range(2):
                    r = 32 * g + H * d
                    sp.dma_start(gate[:, 2 * d + g, :], krg[r:r + H, :]).then_inc(gate_in, 16)
            sp.dma_start(bias[:], io["b_gate"][0].rearrange("(g h) -> h g", h=H),
                         allow_slow_non_contiguous=True).then_inc(gate_in, 16)
            sp.dma_start(sel[:], io["consts"][0:H, C_SEL:C_SEL + H * P]).then_inc(const_in, 16)
            u_v = scratch["u"].rearrange("c p t -> p c t")
            v_v = scratch["v"].rearrange("t p m -> p t m")

            def fetch(h, s):
                sp.dma_start(uh[:, s], u_v[:, bass.ds(2 * h, 2), :]).then_inc(head_in[s], 16)
                for q, w in enumerate([io["w_mq"], io["w_mk"]]):
                    sp.dma_start(wm[:, s, q], w[0, bass.ds(h, 1)].rearrange("a (k p) m -> p (a k) m", p=P))\
                      .then_inc(head_in[s], 16)
                sp.dma_start(v1[:, s, :, 0:ML_V], v_v[:, :, bass.ds(h * ML_V, ML_V)]).then_inc(head_in[s], 16)

            for s in range(2):
                fetch(s, s)
            sp.wait_ge(gate_in, 80)
            sp.dma_start(mask[:].rearrange("p a b -> p (a b)"), io["consts"][:, C_MASKF:C_MASKF + 2 * P]).then_inc(mask_in, 16)
            with sp.Fori(1, H // 2) as i:
                for s in range(2):
                    sp.wait_ge(num_done, 2 * LB * (2 * i + s - 1))
                    fetch(2 * i + s, s)
            sp.wait_ge(num_done, 2 * LB * H)
            sp.dma_start(sig_o[:], scratch["o"].rearrange("c p t -> p c t")).then_inc(o_in, 16)

        @block.gpsimd
        def _(pool):
            sem.clear_last(pool)
            nc.gpsimd.memset(v1[:, :, :, ML_V:ML_V + 1], 1.0).then_inc(ones_ready, 1)
            sum_ada(nc, io, sb, sem, pool, range(7, 8))

        @block.scalar
        def _(act):
            act.wait_ge(biased, 1)
            own = Chain(act, soft_own)
            f = gate[:].rearrange("h (d g) t -> h g d t", g=2)[:, 1]
            own.after(nc.scalar.activation(soft[:], f, ACT.Abs))
            own.after(nc.scalar.activation(soft[:], soft[:], ACT.Exp, scale=-1.0))
            nc.scalar.activation(soft[:], soft[:], ACT.Ln, bias=1.0).then_inc(soft_ready, 1)
            act.wait_ge(erow_ready, 1)
            nc.scalar.activation(erow[:], erow[:], ACT.Exp).then_inc(eexp_ready, 1)
            for n in range(2 * H):
                act.wait_ge(spread, n + 1)
                nc.scalar.activation(negmb[:, n, :], ps[:, 6 + n % 2, :], ACT.Copy).then_inc(spread_kept, 1)
            with act.Fori(0, H // 2) as i:
                for s in range(2):
                    h = 2 * i + s
                    act.wait_ge(qk_done, h + 1)
                    nc.scalar.activation(qT[:], ps[:, 0, :], ACT.Copy, scale=ML_SCALE)
                    nc.scalar.activation(kT[:, 0:CTX], ps[:, 2, 0:CTX], ACT.Copy)
                    nc.scalar.activation(kT[:, CTX:TOK], ps[:, 1, :], ACT.Copy).then_inc(qk_kept, 1)
                    for b in range(TB):
                        act.wait_ge(s_done, TB * h + b + 1)
                        if b == 0:
                            act.wait_ge(prob_ready, 2 * (2 * i))
                        nc.scalar.activation(sT[:, s, b, :], ps[:, b % 4, :], ACT.Copy).then_inc(s_kept, 1)
                    for d in range(2):
                        act.wait_ge(expo_ready, 2 * h + d + 1)
                        nc.scalar.activation(decay[:, d, 0:CB, :], decay[:, d, 0:CB, :], ACT.Exp)
                        for j in range(LB):
                            a, c = span(d, j)
                            last = nc.scalar.activation(decay[:, d, CB + j, a:c], decay[:, d, CB + j, a:c], ACT.Exp)
                        last.then_inc(decay_ready, 1)
            act.wait_ge(var_ready, 1)
            nc.scalar.activation(rstd[:], mv[:, :, 1], ACT.Sqrt, bias=sb["eps"][:]).then_inc(root_ready, 1)

        @block.vector
        def _(dve):
            own = Chain(dve, dve_own)
            dve.wait_ge(gate_in, 80)
            for g in range(4):
                last = nc.vector.tensor_scalar(gate[:, g, :], gate[:, g, :], bias[:, g:g + 1], None, ALU.add)
            last.then_inc(biased, 1)
            dve.wait_ge(biased, 1)
            f = gate[:].rearrange("h (d g) t -> h g d t", g=2)[:, 1]
            dve.wait_ge(soft_ready, 1)
            own.after(nc.vector.scalar_tensor_tensor(f, f, 0.0, soft[:], ALU.min, ALU.subtract))
            ctx, lat = slice(0, CTX), slice(CTX, TOK)

            def back(x):
                return x[:, ::-1]

            lf = [gate[:, 1, :], gate[:, 3, :]]
            order = [(back, lambda x: x), (lambda x: x, back)]
            for d in range(2):
                for part, turn in zip((ctx, lat), order[d]):
                    x = turn(lf[d][:, part])
                    last = nc.vector.tensor_tensor_scan(turn(runs[:, d, part]), x, x, 0.0, ALU.add, ALU.bypass)
            own.after(last)
            for d in range(2):
                i_row = gate[:, 2 * d, :]
                nc.vector.tensor_tensor(arow[:, d, lat], i_row[:, lat], runs[:, d, lat], ALU.subtract)
                if d == 0:
                    nc.vector.tensor_tensor(arow[:, d, 0:CTX - 1], i_row[:, 0:CTX - 1], runs[:, d, 1:CTX], ALU.add)
                    last = nc.vector.tensor_copy(arow[:, d, CTX - 1:CTX], i_row[:, CTX - 1:CTX])
                else:
                    nc.vector.tensor_tensor(arow[:, d, 1:CTX], i_row[:, 1:CTX], runs[:, d, 0:CTX - 1], ALU.add)
                    last = nc.vector.tensor_copy(arow[:, d, 0:1], i_row[:, 0:1])
            last.then_inc(arow_ready, 1)
            dve.wait_ge(arow_ready, 1)
            own.after(nc.vector.tensor_reduce(init[:, :, 0:1], arow[:, :, ctx], AX.X, ALU.max))
            for d, t in [(0, 0), (1, CTX - 1)]:
                last = nc.vector.tensor_tensor(init[:, d, 1:2], init[:, d, 0:1], runs[:, d, t:t + 1], ALU.max)
            own.after(last)
            for d in range(2):
                turn = order[d][1]
                x = turn(arow[:, d, lat])
                last = nc.vector.tensor_tensor_scan(turn(mrow[:, d, :]), x, x, init[:, d, 1:2], ALU.max, ALU.max)
            own.after(last)
            own.after(nc.vector.tensor_tensor(erow[:], mrow[:], runs[:, :, lat], ALU.add))
            nc.vector.tensor_scalar(erow[:], erow[:], -1.0, EXP_MAX, ALU.mult, ALU.min)
            nc.vector.tensor_scalar(mrow[:], mrow[:], -1.0, None, ALU.mult).then_inc(erow_ready, 1)
            dve.wait_ge(cols_turned, 1)
            nc.vector.tensor_copy(cols[:].rearrange("p a b c -> p (a b c)"), ps[:, 5, 0:2 * (TB + LB) * H]).then_inc(cols_ready, 1)
            dve.wait_ge(cols_ready, 1)
            dve.wait_ge(spread_kept, 2 * H)
            dve.wait_ge(mask_in, 16)
            base = own.n
            per = 2 * (2 + 3 * LB)
            colv = cols[:]
            with dve.Fori(0, H // 2) as i:
                for s in range(2):
                    h = 2 * i + s
                    own.at(base + per * h)
                    for d in range(2):
                        m = negmb[:, bass.ds(h + H * d, 1), :]
                        dve.wait_ge(prob_ready, 2 * h)
                        for b in range(TB):
                            a, c = (0, LAT) if b < CB else span(d, b - CB)
                            last = nc.vector.tensor_scalar(decay[:, d, b:b + 1, a:c], m[:, :, a:c],
                                                           colv[:, d, b, bass.ds(h, 1)], 0.0, ALU.add, ALU.min)
                        last.then_inc(expo_ready, 1)
                    for d in range(2):
                        dve.wait_ge(decay_ready, 2 * h + d + 1)
                        if d == 0:
                            dve.wait_ge(s_kept, TB * (h + 1))
                        dve.wait_ge(num_done, 2 * LB * h)
                        own.after(nc.vector.tensor_tensor(probT[:, d, 0:CB, :], decay[:, d, 0:CB, :], sT[:, s, 0:CB, :], ALU.mult))
                        for j in range(LB):
                            a, c = span(d, j)
                            last = nc.vector.tensor_tensor(probT[:, d, CB + j, a:c], decay[:, d, CB + j, a:c],
                                                           sT[:, s, CB + j, a:c], ALU.mult)
                        own.after(last)
                        for j in range(LB):
                            x = probT[:, d, CB + j, j * P:(j + 1) * P]
                            last = nc.vector.tensor_tensor(x, x, mask[:, d, :], ALU.mult)
                        last.then_inc(prob_ready, 1)
                    for d in range(2):
                        for t in range(LB):
                            n = 2 * LB * h + LB * d + t
                            src = ps[:, 4 + t % 2, :]
                            dve.wait_ge(num_done, n + 1)
                            own.after(nc.vector.tensor_scalar(small[:, t:t + 1], src[:, ML_V:ML_V + 1], -1.0,
                                                              colv[:, d, TB + t, bass.ds(h, 1)], ALU.mult, ALU.max))
                            own.after(nc.vector.tensor_tensor(small[:, t:t + 1], small[:, t:t + 1],
                                                              src[:, ML_V:ML_V + 1], ALU.max))
                            own.after(nc.vector.reciprocal(small[:, 8 + t:9 + t], small[:, t:t + 1]))
                            out = hid[:, t, bass.ds(h, 1), :]
                            num = ps[:, 4 + t % 2:5 + t % 2, 0:ML_V]
                            if d == 0:
                                nc.vector.tensor_scalar(out, num, small[:, 8 + t:9 + t], None, ALU.mult).then_inc(num_kept, 1)
                            else:
                                nc.vector.scalar_tensor_tensor(out, num, small[:, 8 + t:9 + t], out, ALU.mult, ALU.add)\
                                  .then_inc(num_kept, 1)
            own.at(base + per * H)
            dve.wait_ge(num_kept, 2 * LB * H)
            for t in range(LB):
                for h in range(H):
                    last = nc.vector.bn_stats(stats[:, t * H + h, :], hid[:, t, h, :])
            own.after(last)
            for x in range(LB * H):
                last = nc.vector.bn_aggr(mv[:, x, :], stats[:, x, :])
            last.then_inc(var_ready, 1)
            dve.wait_ge(root_ready, 1)
            own.after(nc.vector.reciprocal(rstd[:], rstd[:]))
            for t in range(LB):
                for h in range(H):
                    x = t * H + h
                    last = nc.vector.tensor_scalar(hid[:, t, h, :], hid[:, t, h, :], mv[:, x, 0:1], rstd[:, x:x + 1],
                                                   ALU.subtract, ALU.mult)
            last.then_inc(normed, 1)
            dve.wait_ge(o_in, 16)
            for c in range(UK):
                dve.wait_ge(y_turned, c + 1)
                nc.vector.scalar_tensor_tensor(yT[:, UK + c, :], ps[:, c % 4, :], vecs[:, V_GHN + c:V_GHN + c + 1],
                                               sig_o[:, c, :], ALU.mult, ALU.mult).then_inc(y_kept, 1)

        @block.tensor
        def _(pe):
            pe.wait_ge(arow_ready, 1)
            pe.wait_ge(eexp_ready, 1)
            for d in range(2):
                for b in range(TB + LB):
                    src = arow[:, d, b * P:(b + 1) * P] if b < TB else erow[:, d, (b - TB) * P:(b - TB + 1) * P]
                    c0 = (d * (TB + LB) + b) * H
                    mm = nc.tensor.transpose(ps[:, 5, c0:c0 + H], src, ident[0:H, 0:H])
            mm.then_inc(cols_turned, 1)
            pe.wait_ge(const_in, 16)
            for n in range(2 * H):
                d, h = divmod(n, H)
                if n >= 2:
                    pe.wait_ge(spread_kept, n - 1)
                nc.tensor.matmul(ps[:, 6 + n % 2, :], sel[:, h * P:(h + 1) * P], mrow[:, d, :], start=True,
                                 stop=True).then_inc(spread, 1)
            pe.wait_ge(ones_ready, 1)
            pe.wait_ge(cols_ready, 1)
            with pe.Fori(0, H // 2) as i:
                for s in range(2):
                    h = 2 * i + s
                    pe.wait_ge(head_in[s], 64 * i + 64)
                    pe.wait_ge(s_kept, TB * h)
                    for q, parts in enumerate([[(0, CTX, TOK)], [(2, 0, CTX), (1, CTX, TOK)]]):
                        for bank, a, b in parts:
                            for k in range(2):
                                mm = nc.tensor.matmul(ps[:, bank, 0:b - a], wm[:, s, q, k, :], uh[:, s, k, a:b],
                                                      start=(k == 0), stop=(k == 1))
                    mm.then_inc(qk_done, 1)
                    pe.wait_ge(qk_kept, h + 1)
                    for b in range(TB):
                        if b >= 4:
                            pe.wait_ge(s_kept, TB * h + b - 3)
                        nc.tensor.matmul(ps[:, b % 4, :], kT[:, b * P:(b + 1) * P], qT[:], start=True,
                                         stop=True).then_inc(s_done, 1)
                    for d in range(2):
                        pe.wait_ge(prob_ready, 2 * h + d + 1)
                        for t in range(LB):
                            n = 2 * LB * h + LB * d + t
                            if d or t >= 2:
                                pe.wait_ge(num_kept, n - 1)
                            else:
                                pe.wait_ge(num_kept, 2 * LB * h)
                            seen = list(range(CB)) + [CB + j for j in range(LB) if (j <= t if d == 0 else j >= t)]
                            for b in seen:
                                mm = nc.tensor.matmul(ps[:, 4 + t % 2, 0:ML_V + 1], probT[:, d, b, t * P:(t + 1) * P],
                                                      v1[:, s, b, :], start=(b == seen[0]), stop=(b == seen[-1]))
                            mm.then_inc(num_done, 1)
            pe.wait_ge(normed, 1)
            for c in range(UK):
                if c >= 4:
                    pe.wait_ge(y_kept, c - 3)
                for t in range(LB):
                    mm = nc.tensor.transpose(ps[:, c % 4, t * P:(t + 1) * P], hid[:, t, c // 2, (c % 2) * P:(c % 2 + 1) * P], ident[:])
                mm.then_inc(y_turned, 1)


def project_out(nc, io, sb, sem, psum):
    vecs, ident, ones, modR = sb["vecs"], sb["ident"], sb["ones"], sb["modR"]
    ps = psum["all"]
    yT, x1T, x1m_hi, x1m_lo = sb["yT"], sb["x1T"], sb["x1m_hi"], sb["x1m_lo"]

    def at(name, shape, dtype, kb):
        return nc.alloc_sbuf_tensor_at(name, shape, dtype, offset=SB0 + int(kb * KB))

    ada = at("e_ada", [P, 8, ADA_COLS], F32, 118)
    y_hi = at("e_y_hi", [P, KT, LAT], F32R, 54)
    y_lo = at("e_y_lo", [P, KT, LAT], F32R, 86)
    raw = at("e_raw", [P, 2, KT * P], F32, 150)
    w_hi = at("e_w_hi", [P, 2, KT * P], F32R, 166)
    w_lo = at("e_w_lo", [P, 2, KT * P], F32R, 182)
    xs = at("e_xs", [P, 2, LB, P], F32, 5)
    xa = at("e_xa", [P, 2, LAT], F32, 9)
    total = at("e_total", [P, LAT], F32, 13)
    mean = at("e_mean", [P, LAT], F32, 15)
    inv = at("e_inv", [P, LAT], F32, 17)
    sq = at("e_sq", [P, 2, LAT], F32, 118)
    x1 = at("e_x1", [P, 2, LAT], F32, 122)
    x1m = at("e_x1m", [P, 2, LAT], F32, 126)

    ada_in = sem("e_ada_in")
    raw_in = [sem(f"e_raw_in{s}") for s in range(2)]
    xs_in = [sem(f"e_xs_in{s}") for s in range(2)]
    y_hi_ready = sem("e_y_hi_ready")
    y_lo_ready = sem("e_y_lo_ready")
    ada_summed = sem("e_ada_summed")
    hi_ready = sem("e_hi_ready")
    lo_ready = sem("e_lo_ready")
    x_turned = sem("e_x_turned")
    xa_ready = sem("e_xa_ready")
    chunk_done = sem("e_chunk_done")
    x1_ready = sem("e_x1_ready")
    total_ready = sem("e_total_ready")
    mean_done = sem("e_mean_done")
    mean_ready = sem("e_mean_ready")
    centred = sem("e_centred")
    sq_ready = sem("e_sq_ready")
    var_added = sem("e_var_added")
    root_ready = sem("e_root_ready")
    scaled = sem("e_scaled")
    norm_ready = sem("e_norm_ready")
    x1m_ready = sem("e_x1m_ready")
    x1m_split = sem("e_x1m_split")
    x1_kept = sem("e_x1_kept")
    dve_own = sem("e_dve_own")

    def gate(m):
        return modR[:, m:m + 1] if isinstance(m, int) else modR[:, bass.ds(m, 1)]

    block = nc.Block()
    with block as block:
        @block.gpsimd
        def _(pool):
            sem.clear_last(pool)

        @block.sync
        def _(sp):
            sp.dma_start(ada[:], io["scratch"]["ada"].rearrange("a p m -> p a m")).then_inc(ada_in, 16)
            wv = io["w_out"][0].rearrange("(k p) m -> p k m", p=P)
            xv = io["x"][0].rearrange("(t p) m -> p t m", p=P)

            def fetch(m, s):
                sp.dma_start(xs[:, s], xv[:, :, bass.ds(m * P, P)]).then_inc(xs_in[s], 16)
                sp.dma_start(raw[:, s, :].rearrange("p (k m) -> p k m", m=P), wv[:, :, bass.ds(m * P, P)])\
                  .then_inc(raw_in[s], 16)

            for s in range(2):
                fetch(s, s)
            with sp.Fori(1, KT // 2) as i:
                for s in range(2):
                    sp.wait_ge(x_turned, 2 * i + s - 1)
                    sp.wait_ge(lo_ready, 2 * i + s - 1)
                    fetch(2 * i + s, s)

        @block.scalar
        def _(act):
            for k in range(KT):
                nc.scalar.activation(y_hi[:, k, :], yT[:, k, :], ACT.Copy).then_inc(y_hi_ready, 1)

            def hi_part(n, s):
                act.wait_ge(raw_in[s], 16 * ((n + 2) // 2) if isinstance(n, int) else n * 8 + (16 if s == 0 else 8))
                if not isinstance(n, int) or n >= 2:
                    act.wait_ge(chunk_done, n - 1)
                nc.scalar.activation(w_hi[:, s, :], raw[:, s, :], ACT.Copy).then_inc(hi_ready, 1)

            def keep_x(m, s):
                act.wait_ge(x_turned, m + 1)
                if not isinstance(m, int) or m >= 2:
                    act.wait_ge(x1_ready, m - 1)
                nc.scalar.activation(xa[:, s, :], ps[:, 2 + s, :], ACT.Copy, scale=ALPHA).then_inc(xa_ready, 1)

            hi_part(0, 0)
            for m in range(2):
                hi_part(m + 1, 1 - m)
                keep_x(m, m)
            with act.Fori(1, KT // 2 - 1) as i:
                for s in range(2):
                    hi_part(2 * i + s + 1, 1 - s)
                    keep_x(2 * i + s, s)
            hi_part(KT - 1, 1)
            keep_x(KT - 2, 0)
            keep_x(KT - 1, 1)
            act.wait_ge(mean_done, 1)
            nc.scalar.activation(mean[:], ps[:, 4, :], ACT.Copy, scale=1.0 / D).then_inc(mean_ready, 1)
            for m in range(KT):
                act.wait_ge(centred, m + 1)
                if m >= 2:
                    act.wait_ge(var_added, m - 1)
                nc.scalar.activation(sq[:, m % 2, :], x1T[:, m, :], ACT.Square).then_inc(sq_ready, 1)
            act.wait_ge(var_added, KT)
            nc.scalar.activation(inv[:], ps[:, 5, :], ACT.Sqrt, bias=sb["eps"][:], scale=1.0 / D).then_inc(root_ready, 1)

            def split(m):
                act.wait_ge(x1m_ready, m + 1)
                nc.scalar.activation(x1m_hi[:, m, :], x1m[:, m % 2, :], ACT.Copy).then_inc(x1m_split, 1)
                nc.scalar.activation(x1T[:, m, :], x1[:, m % 2, :], ACT.Copy, scale=ALPHA).then_inc(x1_kept, 1)

            for m in range(KT):
                act.wait_ge(scaled, m + 1)
                if m >= 2:
                    act.wait_ge(x1_kept, m - 1)
                nc.scalar.activation(x1[:, m % 2, :], x1T[:, m, :], ACT.Identity, bias=vecs[:, V_LN1B + m:V_LN1B + m + 1],
                                     scale=vecs[:, V_LN1G + m:V_LN1G + m + 1]).then_inc(norm_ready, 1)
                if m:
                    split(m - 1)
            split(KT - 1)

        @block.vector
        def _(dve):
            own = Chain(dve, dve_own)
            for k in range(KT):
                dve.wait_ge(y_hi_ready, k + 1)
                nc.vector.tensor_tensor(y_lo[:, k, :], yT[:, k, :], y_hi[:, k, :].bitcast(F32), ALU.subtract)\
                  .then_inc(y_lo_ready, 1)
            dve.wait_ge(ada_summed, 1)
            own.after(nc.vector.tensor_tensor(modR[:], ps[:, 7, 0:4 * KT], vecs[:, V_ADA + 2 * KT:V_ADA + 6 * KT], ALU.add))
            own.after(nc.vector.tensor_scalar(modR[:, 2 * KT:3 * KT], modR[:, 2 * KT:3 * KT], 1.0, None, ALU.add))
            own.after(nc.vector.memset(total[:], 0.0))
            base = own.n
            dve.wait_ge(y_lo_ready, KT)

            def lo_part(n, s):
                dve.wait_ge(hi_ready, n + 1)
                nc.vector.tensor_tensor(w_lo[:, s, :], raw[:, s, :], w_hi[:, s, :].bitcast(F32), ALU.subtract)\
                  .then_inc(lo_ready, 1)

            def add_x(m, s):
                own.at(base + m)
                dve.wait_ge(chunk_done, m + 1)
                dve.wait_ge(xa_ready, m + 1)
                row = x1T[:, m:m + 1, :] if isinstance(m, int) else x1T[:, bass.ds(m, 1), :]
                nc.vector.scalar_tensor_tensor(row, ps[:, s:s + 1, :], gate(m), xa[:, s:s + 1, :], ALU.mult, ALU.add)\
                  .then_inc(x1_ready, 1)
                dve.wait_ge(x1_ready, m + 1)
                own.after(nc.vector.tensor_tensor(total[:], total[:], row[:, 0], ALU.add))

            lo_part(0, 0)
            with dve.Fori(0, KT // 2 - 1) as i:
                for s in range(2):
                    lo_part(2 * i + s + 1, 1 - s)
                    add_x(2 * i + s, s)
            lo_part(KT - 1, 1)
            add_x(KT - 2, 0)
            add_x(KT - 1, 1)
            nc.vector.tensor_copy(total[:, 0:1], total[:, 0:1]).then_inc(total_ready, 1)
            dve.wait_ge(mean_ready, 1)
            for m in range(KT):
                nc.vector.tensor_tensor(x1T[:, m, :], x1T[:, m, :], mean[:], ALU.subtract).then_inc(centred, 1)
            dve.wait_ge(root_ready, 1)
            own.at(base + KT)
            own.after(nc.vector.reciprocal(inv[:], inv[:]))
            dve.wait_ge(centred, KT)

            def lo_x(m):
                dve.wait_ge(x1m_split, m + 1)
                last = nc.vector.tensor_tensor(x1m_lo[:, m, :], x1m[:, m % 2, :], x1m_hi[:, m, :].bitcast(F32), ALU.subtract)
                own.after(last)

            def modulate(m):
                dve.wait_ge(norm_ready, m + 1)
                nc.vector.tensor_scalar(x1m[:, m % 2, :], x1[:, m % 2, :], modR[:, 2 * KT + m:2 * KT + m + 1],
                                        modR[:, KT + m:KT + m + 1], ALU.mult, ALU.add).then_inc(x1m_ready, 1)

            for m in range(KT + 2):
                if m < KT:
                    nc.vector.tensor_tensor(x1T[:, m, :], x1T[:, m, :], inv[:], ALU.mult).then_inc(scaled, 1)
                if m >= 2:
                    lo_x(m - 2)
                if 1 <= m < KT + 1:
                    modulate(m - 1)

        @block.tensor
        def _(pe):
            pe.wait_ge(ada_in, 16)
            for c in range(4 * KT):
                mm = nc.tensor.matmul(ps[:, 7, c:c + 1], ada[:, c // 8, c % 8 * P:(c % 8 + 1) * P], ones[:, 0:1],
                                      start=True, stop=True)
            mm.then_inc(ada_summed, 1)
            pe.wait_ge(y_lo_ready, KT)

            def chunk(m, s):
                pe.wait_ge(xs_in[s], 8 * (m - s) + 16)
                if not isinstance(m, int) or m >= 2:
                    pe.wait_ge(x1_ready, m - 1)
                for t in range(LB):
                    mm = nc.tensor.transpose(ps[:, 2 + s, t * P:(t + 1) * P], xs[:, s, t, :], ident[:])
                mm.then_inc(x_turned, 1)
                pe.wait_ge(lo_ready, m + 1)
                for k in range(KT):
                    for p, (w, y) in enumerate([(w_hi, y_hi), (w_hi, y_lo), (w_lo, y_hi)]):
                        mm = nc.tensor.matmul(ps[:, s, :], w[:, s, k * P:(k + 1) * P], y[:, k, :],
                                              start=(k == 0 and p == 0), stop=(k == KT - 1 and p == 2))
                mm.then_inc(chunk_done, 1)

            for s in range(2):
                chunk(s, s)
            with pe.Fori(1, KT // 2) as i:
                for s in range(2):
                    chunk(2 * i + s, s)
            pe.wait_ge(total_ready, 1)
            pe.wait_ge(dve_own, 3 + KT)
            nc.tensor.matmul(ps[:, 4, :], ones[:], total[:], start=True, stop=True).then_inc(mean_done, 1)
            for m in range(KT):
                pe.wait_ge(sq_ready, m + 1)
                nc.tensor.matmul(ps[:, 5, :], ones[:], sq[:, m % 2, :], start=(m == 0), stop=(m == KT - 1)).then_inc(var_added, 1)


def gated_mlp(nc, io, sb, sem, psum):
    vecs, modR = sb["vecs"], sb["modR"]
    ps = psum["all"]
    x1T, x1m_hi, x1m_lo = sb["x1T"], sb["x1m_hi"], sb["x1m_lo"]

    def at(name, shape, dtype, kb):
        return nc.alloc_sbuf_tensor_at(name, shape, dtype, offset=SB0 + int(kb * KB))

    SLOT = KT * P
    raw = at("f_raw", [P, 3, SLOT], F32, 134)
    w_hi = at("f_w_hi", [P, 2, SLOT], F32R, 158)
    w_lo = at("f_w_lo", [P, 2, SLOT], F32R, 174)
    h_hi = at("f_h_hi", [P, 4, LAT], F32R, 118)
    h_lo = at("f_h_lo", [P, 4, LAT], F32R, 126)
    conv = at("f_conv", [P, LAT], F32, 5)
    act_out = at("f_act_out", [P, LAT], F32, 7)
    h = at("f_h", [P, LAT], F32, 9)

    raw_in = [sem(f"f_raw_in{s}") for s in range(3)]
    hi_ready = sem("f_hi_ready")
    lo_ready = sem("f_lo_ready")
    slot_done = sem("f_slot_done")
    conv_ready = sem("f_conv_ready")
    silu_ready = sem("f_silu_ready")
    h_ready = sem("f_h_ready")
    h_hi_ready = sem("f_h_hi_ready")
    h_lo_ready = sem("f_h_lo_ready")
    down_done = sem("f_down_done")
    down_kept = sem("f_down_kept")
    dve_own = sem("f_dve_own")

    G = 4
    GROUPS = FC // G
    BODY = 3 * G
    N = 3 * FC
    FIRST = [("up", j, half) for j in range(G) for half in range(2)]
    TURN = FIRST[0:2] + [("down", q, None) for q in range(4)] + FIRST[2:]
    LAST = [("down", q, None) for q in range(4)]
    assert BODY % 6 == 0 and N == len(FIRST) + (GROUPS - 1) * BODY + 4
    TURN0 = len(FIRST)
    LAST0 = TURN0 + (GROUPS - 1) * BODY

    block = nc.Block()
    with block as block:
        @block.gpsimd
        def _(pool):
            sem.clear_last(pool)

        @block.sync
        def _(sp):
            up = io["w_up"][0].rearrange("(k p) m -> p k m", p=P)
            down = io["w_down"][0].rearrange("(f p) m -> p f m", p=P)

            def fetch(n, what, group, it=0):
                kind, j, half = what
                if not isinstance(it, int) or n >= 3:
                    sp.wait_ge(lo_ready, it * BODY + n - 2)
                if kind == "up":
                    src = up[:, :, bass.ds(group * (G * P) + (half * D_FF + j * P), P)]
                    dst = raw[:, n % 3, :].rearrange("p (k m) -> p k m", m=P)
                else:
                    src = down[:, bass.ds(group * G, G), j * 512:(j + 1) * 512]
                    dst = raw[:, n % 3, :].rearrange("p (k m) -> p k m", m=512)
                sp.dma_start(dst, src).then_inc(raw_in[n % 3], 16)

            for n, what in enumerate(FIRST):
                fetch(n, what, 0)
            with sp.Fori(0, GROUPS - 1) as i:
                for k, what in enumerate(TURN):
                    fetch(TURN0 + k, what, i + 1 if what[0] == "up" else i, i)
            for k, what in enumerate(LAST):
                fetch(LAST0 + k, what, GROUPS - 1)

        @block.scalar
        def _(act):
            def hi_part(n, it=0):
                act.wait_ge(raw_in[n % 3], 16 * (it * (BODY // 3) + n // 3 + 1))
                if not isinstance(it, int) or n >= 2:
                    act.wait_ge(slot_done, it * BODY + n - 1)
                nc.scalar.activation(w_hi[:, n % 2, :], raw[:, n % 3, :], ACT.Copy).then_inc(hi_ready, 1)

            def chunk(c, j, down_slots):
                act.wait_ge(conv_ready, c + 1)
                nc.scalar.activation(act_out[:], conv[:], ACT.Silu).then_inc(silu_ready, 1)
                act.wait_ge(h_ready, c + 1)
                if down_slots is not None:
                    act.wait_ge(slot_done, down_slots)
                nc.scalar.activation(h_hi[:, j, :], h[:], ACT.Copy).then_inc(h_hi_ready, 1)

            hi_part(0)
            for n, (kind, j, half) in enumerate(FIRST):
                hi_part(n + 1)
                if half == 1:
                    chunk(j, j, None)
            with act.Fori(0, GROUPS - 1) as i:
                for k, (kind, j, half) in enumerate(TURN):
                    if k == 6:
                        chunk(G * i + G, 0, i * BODY + TURN0 + 6)
                    hi_part(TURN0 + k + 1, i)
                    if half == 1 and j > 0:
                        chunk(G * i + G + j, j, None)
            for k in range(3):
                hi_part(LAST0 + k + 1)

        @block.vector
        def _(dve):
            own = Chain(dve, dve_own)

            def lo_part(n, it=0):
                dve.wait_ge(hi_ready, it * BODY + n + 1)
                nc.vector.tensor_tensor(w_lo[:, n % 2, :], raw[:, n % 3, :], w_hi[:, n % 2, :].bitcast(F32),
                                        ALU.subtract).then_inc(lo_ready, 1)

            def chunk(c, j, slots):
                own.at(2 * c)
                dve.wait_ge(slot_done, slots)
                g = ps[:, 2 * (j % 2), :]
                up = ps[:, 2 * (j % 2) + 1, :]

                def col(v):
                    return vecs[:, bass.ds(c + v, 1)]

                dve.wait_ge(silu_ready, c)
                own.after(nc.vector.tensor_scalar(conv[:], g, col(V_FW + FC), col(V_FB), ALU.mult, ALU.add))
                own.after(nc.vector.scalar_tensor_tensor(conv[:, 1:LAT], g[:, 0:LAT - 1], col(V_FW), conv[:, 1:LAT],
                                                         ALU.mult, ALU.add))
                nc.vector.scalar_tensor_tensor(conv[:, 0:LAT - 1], g[:, 1:LAT], col(V_FW + 2 * FC), conv[:, 0:LAT - 1],
                                               ALU.mult, ALU.add).then_inc(conv_ready, 1)
                dve.wait_ge(silu_ready, c + 1)
                dve.wait_ge(h_lo_ready, c)
                nc.vector.tensor_tensor(h[:], act_out[:], up, ALU.mult).then_inc(h_ready, 1)
                dve.wait_ge(h_hi_ready, c + 1)
                nc.vector.tensor_tensor(h_lo[:, j, :], h[:], h_hi[:, j, :].bitcast(F32), ALU.subtract)\
                  .then_inc(h_lo_ready, 1)

            def add_down(n, q, group, it=0):
                for e in range(4):
                    m = 4 * q + e
                    if e < 3:
                        dve.wait_ge(down_done, group * (KT - 4) + 3 * q + e + 1)
                    else:
                        dve.wait_ge(slot_done, it * BODY + n + 1)
                    nc.vector.scalar_tensor_tensor(x1T[:, m, :], ps[:, 4 + e, :], modR[:, 3 * KT + m:3 * KT + m + 1],
                                                   x1T[:, m, :], ALU.mult, ALU.add).then_inc(down_kept, 1)

            lo_part(0)
            for n, (kind, j, half) in enumerate(FIRST):
                lo_part(n + 1)
                if half == 1:
                    chunk(j, j, n + 1)
            with dve.Fori(0, GROUPS - 1) as i:
                for k, (kind, j, half) in enumerate(TURN):
                    if k == 6:
                        chunk(G * i + G, 0, i * BODY + TURN0 + 6)
                    lo_part(TURN0 + k + 1, i)
                    if kind == "down":
                        add_down(TURN0 + k, j, i, i)
                    elif half == 1 and j > 0:
                        chunk(G * i + G + j, j, i * BODY + TURN0 + k + 1)
            for k in range(4):
                if k < 3:
                    lo_part(LAST0 + k + 1)
                add_down(LAST0 + k, k, GROUPS - 1)

        @block.tensor
        def _(pe):
            passes = [(w_hi, x1m_hi, h_hi), (w_hi, x1m_lo, h_lo), (w_lo, x1m_hi, h_hi)]

            def up_slot(n, j, half, c, it=0):
                if half == 0 and (not isinstance(c, int) or c >= 2):
                    pe.wait_ge(h_ready, c - 1)
                pe.wait_ge(lo_ready, it * BODY + n + 1)
                for k in range(KT):
                    for p, (w, x, _) in enumerate(passes):
                        mm = nc.tensor.matmul(ps[:, 2 * (j % 2) + half, :], w[:, n % 2, k * P:(k + 1) * P], x[:, k, :],
                                              start=(k == 0 and p == 0), stop=(k == KT - 1 and p == 2))
                mm.then_inc(slot_done, 1)

            def down_slot(n, q, group, it=0):
                pe.wait_ge(h_lo_ready, G * group + G)
                pe.wait_ge(lo_ready, it * BODY + n + 1)
                for e in range(4):
                    m = 4 * q + e
                    if q or not isinstance(group, int) or group:
                        pe.wait_ge(down_kept, group * KT + (m - 3 if q else 0))
                    for k in range(G):
                        for p, (w, _, hh) in enumerate(passes):
                            mm = nc.tensor.matmul(ps[:, 4 + e, :], w[:, n % 2, k * 512 + e * P:k * 512 + (e + 1) * P],
                                                  hh[:, k, :], start=(k == 0 and p == 0), stop=(k == G - 1 and p == 2))
                    mm.then_inc(down_done if e < 3 else slot_done, 1)

            for n, (kind, j, half) in enumerate(FIRST):
                up_slot(n, j, half, j)
            with pe.Fori(0, GROUPS - 1) as i:
                for k, (kind, j, half) in enumerate(TURN):
                    if kind == "up":
                        up_slot(TURN0 + k, j, half, G * i + G + j, i)
                    else:
                        down_slot(TURN0 + k, j, i, i)
            for k in range(4):
                down_slot(LAST0 + k, k, GROUPS - 1)


def final_norm(nc, io, sb, sem, psum):
    ident, x1T = sb["ident"], sb["x1T"]
    ps = psum["all"]

    def at(name, shape, kb):
        return nc.alloc_sbuf_tensor_at(name, shape, F32, offset=SB0 + int(kb * KB))

    gain = at("g_gain", [P, D], 54)
    shift = at("g_shift", [P, D], 62)
    out = at("g_out", [P, 2, D], 70)
    stats = at("g_stats", [P, 2, 4, 6], 5)
    mv = at("g_mv", [P, 2, 2], 6)
    inv = at("g_inv", [P, 2], 6.5)

    vec_in = sem("g_vec_in")
    turned = sem("g_turned")
    var_ready = sem("g_var_ready")
    root_ready = sem("g_root_ready")
    normed = sem("g_normed")
    out_ready = sem("g_out_ready")
    out_sent = [sem(f"g_out_sent{s}") for s in range(2)]
    dve_own = sem("g_dve_own")

    block = nc.Block()
    with block as block:
        @block.gpsimd
        def _(pool):
            sem.clear_last(pool)

        @block.sync
        def _(sp):
            sp.dma_start(gain[:], io["ln2_g"][0].partition_broadcast(P)).then_inc(vec_in, 16)
            sp.dma_start(shift[:], io["ln2_b"][0].partition_broadcast(P)).then_inc(vec_in, 16)
            for t in range(LB):
                sp.wait_ge(out_ready, t + 1)
                sp.dma_start(io["out"][0, t * P:(t + 1) * P, :], out[:, t % 2, :]).then_inc(out_sent[t % 2], 16)
            for s in range(2):
                sp.wait_ge(out_sent[s], 32)

        @block.scalar
        def _(act):
            for t in range(LB):
                act.wait_ge(var_ready, t + 1)
                nc.scalar.activation(inv[:, t % 2:t % 2 + 1], mv[:, t % 2, 1:2], ACT.Sqrt, bias=sb["eps"][:]).then_inc(root_ready, 1)

        @block.vector
        def _(dve):
            own = Chain(dve, dve_own)

            def stats_of(t):
                dve.wait_ge(turned, t + 1)
                for b in range(4):
                    last = nc.vector.bn_stats(stats[:, t % 2, b, :], ps[:, 4 * (t % 2) + b, :])
                own.after(last)
                nc.vector.bn_aggr(mv[:, t % 2, :], stats[:, t % 2, :, :].rearrange("p a b -> p (a b)")).then_inc(var_ready, 1)

            stats_of(0)
            for t in range(LB):
                s = t % 2
                dve.wait_ge(root_ready, t + 1)
                own.after(nc.vector.reciprocal(inv[:, s:s + 1], inv[:, s:s + 1]))
                if t >= 2:
                    dve.wait_ge(out_sent[s], 16)
                own.after(nc.vector.tensor_scalar(out[:, s, :], ps[:, 4 * s:4 * s + 4, :].rearrange("p a b -> p (a b)"),
                                                  mv[:, s, 0:1], inv[:, s:s + 1], ALU.subtract, ALU.mult))
                nc.vector.tensor_copy(inv[:, s:s + 1], inv[:, s:s + 1]).then_inc(normed, 1)
                if t + 1 < LB:
                    stats_of(t + 1)
                dve.wait_ge(vec_in, 32)
                own.after(nc.vector.tensor_tensor(out[:, s, :], out[:, s, :], gain[:], ALU.mult))
                nc.vector.tensor_tensor(out[:, s, :], out[:, s, :], shift[:], ALU.add).then_inc(out_ready, 1)

        @block.tensor
        def _(pe):
            for t in range(LB):
                if t >= 2:
                    pe.wait_ge(normed, t - 1)
                for m in range(KT):
                    mm = nc.tensor.transpose(ps[:, 4 * (t % 2) + m // 4, m % 4 * P:(m % 4 + 1) * P],
                                             x1T[:, m, t * P:(t + 1) * P], ident[:])
                mm.then_inc(turned, 1)


IN_NAMES = ["x", "c", "ctx", "c_ctx", "w_ada", "b_ada", "w_in", "g_q", "w_uq", "g_kv", "w_ukv", "ml_conv_w",
            "ml_conv_b", "w_mq", "w_mk", "b_gate", "g_hn", "w_out", "ln1_g", "ln1_b", "w_up", "ffn_conv_w",
            "ffn_conv_b", "w_down", "ln2_g", "ln2_b"]


def trunk_layer(nc, io, last_stage="g"):
    with ExitStack() as stack:
        def at(name, shape, dtype, kb):
            return nc.alloc_sbuf_tensor_at(name, shape, dtype, offset=SB0 + int(kb * KB))

        ps = stack.enter_context(nc.psum_tensor("ps", [P, 8, 512], F32))
        psum = {"all": ps}
        sb = {
            "ident": at("ident", [P, P], F32, 0),
            "ones": at("ones", [P, P], F32, 0.5),
            "vecs": at("vecs", [P, V_ALL], F32, 1),
            "cT": at("cT", [P, 2 * KT], F32, 3),
            "modT": at("modT", [P, 2 * KT, 2], F32, 3.25),
            "modR": at("modR", [P, 4 * KT], F32, 3.5),
            "eps": at("eps", [P, 1], F32, 3.75),
            "zq": at("zq", [P, QK, LAT], F32, 5),
            "zkv": at("zkv", [P, KVK, TOK], F32, 13),
            "krg": at("krg", [P, TOK], F32, 19),
            "hT_hi": at("hT_hi", [P, KT, TOK], F32R, 22),
            "hT_lo": at("hT_lo", [P, KT, TOK], F32R, 70),
            "yT": at("yT", [P, KT, LAT], F32, 22),
            "x1T": at("x1T", [P, KT, LAT], F32, 22),
            "x1m_hi": at("x1m_hi", [P, KT, LAT], F32R, 54),
            "x1m_lo": at("x1m_lo", [P, KT, LAT], F32R, 86),
        }
        scratch = {
            "u": nc.dram_tensor("scratch_u", [UK, P, TOK], F32).ap(),
            "v": nc.dram_tensor("scratch_v", [TB, P, ML_INNER], F32).ap(),
            "o": nc.dram_tensor("scratch_o", [UK, P, LAT], F32).ap(),
            "ada": nc.dram_tensor("scratch_ada", [8, P, 1024], F32).ap(),
        }
        stages = [load_and_modulate, project_in, attention, matrix_memory, project_out, gated_mlp, final_norm]
        sems = [StageSems(nc) for _ in stages]
        for n, (name, stage) in enumerate(zip("abcdefg", stages)):
            sems[n].last = sems[n - 1] if n else None
            stage(nc, io | {"scratch": scratch}, sb, sems[n], psum)
            if n:
                sems[n - 1].close()
            if name == last_stage:
                break
        sems[n].close()


def kernel(**inputs):
    import concourse.bacc as bacc
    from concourse.bass_utils import run_bass_kernel_spmd

    nc = bacc.Bacc("TRN2", target_bir_lowering=False, num_devices=1)
    consts, ident = host_constants()
    arrays, io = {}, {}
    for name, a in [(n, inputs[n]) for n in IN_NAMES] + [("consts", consts), ("ident", ident)]:
        a = np.ascontiguousarray(a)
        arrays[f"in_{name}"] = a
        io[name] = nc.dram_tensor(f"in_{name}", a.shape, F32, kind="ExternalInput").ap()
    io["out"] = nc.dram_tensor("out", [1, LAT, D], F32, kind="ExternalOutput").ap()
    trunk_layer(nc, io)
    r = run_bass_kernel_spmd(nc, [arrays], core_ids=[0])
    return r.results[0]["out"]
```

```python
from contextlib import ExitStack

import numpy as np

import concourse.bass as bass
from concourse import mybir

F32 = mybir.dt.float32
F32R = mybir.dt.float32r
ALU = mybir.AluOpType
ACT = mybir.ActivationFunctionType
AX = mybir.AxisListType

P = 128
D = 2048
KT = D // P
LAT = 512
CTX = 256
TOK = CTX + LAT
GRID_W = 64
HEADS = 8
NOPE = 128
ROPE = 64
VD = 128
QD = NOPE + ROPE
Q_LORA = 512
KV_LORA = 256
QK = 4
KVK = 2
ML_HEADS = 4
ML_QK = 128
ML_V = 256
ML_INNER = ML_HEADS * ML_V
UK = ML_INNER // P
N_GATES = 16
D_FF = 5632
FC = D_FF // P
OFF_CKV = Q_LORA
OFF_KR = Q_LORA + KV_LORA
OFF_U = OFF_KR + ROPE
OFF_V = OFF_U + ML_INNER
OFF_O = OFF_V + ML_INNER
OFF_G = OFF_O + ML_INNER
TB = TOK // P
LB = LAT // P
CB = CTX // P
ALPHA = 2.0 ** 0.25
EPS = 1e-6
ATT_SCALE = float(QD) ** -0.5
ML_SCALE = float(ML_QK) ** -0.5
EXP_MAX = 87.0

V_ADA = 0
V_GQ = 96
V_GKV = 100
V_GHN = 102
V_MLW = 128
V_MLB = 152
V_LN1G = 160
V_LN1B = 176
V_FB = 192
V_FW = 256
V_ALL = V_FW + 3 * FC

C_SWAP = 0
C_KDUP = 128
C_KSWAP = 256
C_COS = 384
C_SIN = C_COS + LAT
C_MASKF = C_SIN + LAT
C_MASKB = C_MASKF + P
C_SEL = C_MASKB + P
C_ALL = C_SEL + ML_HEADS * P


def host_constants():
    c = np.zeros((P, C_ALL), np.float32)
    part = np.array([r + 16 if r % 32 < 16 else r - 16 for r in range(ROPE)])
    for m in range(P):
        h, r = divmod(m, ROPE)
        c[h * ROPE + part[r], C_SWAP + m] = 1.0
        c[ROPE + r, C_KDUP + m] = 1.0
        c[ROPE + part[r], C_KSWAP + m] = 1.0
    inv = np.float32(10000.0) ** (-np.arange(16, dtype=np.float32) / 16)
    t = np.arange(LAT)
    pos = np.stack([t // GRID_W, t % GRID_W]).astype(np.float32)
    for m in range(P):
        r = m % ROPE
        ang = (pos[r // 32] * inv[r % 16]).astype(np.float32)
        c[m, C_COS:C_COS + LAT] = np.cos(ang)
        c[m, C_SIN:C_SIN + LAT] = np.sin(ang) * (-1.0 if r % 32 < 16 else 1.0)
    s, q = np.meshgrid(np.arange(P), np.arange(P), indexing="ij")
    c[:, C_MASKF:C_MASKF + P] = s <= q
    c[:, C_MASKB:C_MASKB + P] = s >= q
    for h in range(ML_HEADS):
        c[h, C_SEL + h * P:C_SEL + (h + 1) * P] = 1.0
    return c, np.eye(P, dtype=np.float32)


KB = 1024
SB0 = 16512


class Chain:

    def __init__(self, eng, sem):
        self.eng, self.sem, self.n = eng, sem, 0

    def at(self, value):
        self.n = value

    def after(self, ins):
        ins.then_inc(self.sem, 1)
        self.n = self.n + 1
        self.eng.wait_ge(self.sem, self.n)


class StageSems:

    def __init__(self, nc):
        self.nc, self.stack, self.handles, self.last = nc, ExitStack(), [], None

    def __call__(self, name):
        handle = self.stack.enter_context(self.nc.semaphore(name))
        self.handles.append(handle)
        return handle

    def clear_last(self, pool):
        for handle in self.last.handles:
            pool.sem_clear(handle)

    def close(self):
        self.stack.close()


def load_and_modulate(nc, io, sb, sem, psum):
    ident, ones, vecs, cT, modT = sb["ident"], sb["ones"], sb["vecs"], sb["cT"], sb["modT"]
    ps = psum["all"]
    vrows = nc.alloc_sbuf_tensor_at("a_vrows", [P, 5, P], F32, offset=SB0 + 204 * KB)
    ccrow = nc.alloc_sbuf_tensor_at("a_ccrow", [32, P], F32, offset=SB0 + 207 * KB)
    wada = nc.alloc_sbuf_tensor_at("a_wada", [P, 4, 4, 512], F32, offset=SB0 + 118 * KB)
    xnat = nc.alloc_sbuf_tensor_at("a_xnat", [P, TB, D], F32, offset=SB0 + 150 * KB)
    mrows = nc.alloc_sbuf_tensor_at("a_mrows", [2, 8, 512], F32, offset=SB0 + 22 * KB)
    xmod = nc.alloc_sbuf_tensor_at("a_xmod", [P, 2, TOK], F32, offset=SB0 + 198 * KB)
    hT_hi, hT_lo = sb["hT_hi"], sb["hT_lo"]
    NJ = 2 * D // 512

    small_in = sem("a_small_in")
    x_in = sem("a_x_in")
    w_in = [sem(f"a_w_in{s}") for s in range(4)]
    zeroed = sem("a_zeroed")
    silu_done = sem("a_silu_done")
    turned = sem("a_turned")
    turned_kept = sem("a_turned_kept")
    w_used = sem("a_w_used")
    rows_kept = sem("a_rows_kept")
    mod_turned = sem("a_mod_turned")
    mod_ready = sem("a_mod_ready")
    x_turned = sem("a_x_turned")
    xmod_ready = sem("a_xmod_ready")
    hi_ready = sem("a_hi_ready")
    lo_ready = sem("a_lo_ready")
    dve_own = sem("a_dve_own")

    def rows(ap):
        return ap.rearrange("(r p) -> r p", p=P)

    block = nc.Block()
    with block as block:
        @block.sync
        def _(sp):
            sp.dma_start(ident[:], io["ident"]).then_inc(small_in, 16)
            sp.dma_start(ccrow[0:16, :], rows(io["c"][0])).then_inc(small_in, 16)
            sp.dma_start(ccrow[16:32, :], rows(io["c_ctx"])).then_inc(small_in, 16)
            at = [(0, V_ADA, rows(io["b_ada"][0])), (0, V_GQ, rows(io["g_q"][0])), (0, V_GKV, rows(io["g_kv"][0])),
                  (0, V_GHN, io["g_hn"][0].rearrange("h (a p) -> (h a) p", p=P)),
                  (1, V_MLW, io["ml_conv_w"][0].rearrange("w (a p) -> (w a) p", p=P)),
                  (1, V_MLB, rows(io["ml_conv_b"][0])), (1, V_LN1G, rows(io["ln1_g"][0])),
                  (1, V_LN1B, rows(io["ln1_b"][0])), (1, V_FB, rows(io["ffn_conv_b"][0]))]
            for b, v, src in at:
                r = v - b * P
                sp.wait_ge(zeroed, 1)
                sp.dma_start(vrows[r:r + src.shape[0], b, :], src).then_inc(small_in, 16)
            fw = io["ffn_conv_w"][0].rearrange("w (a p) -> (w a) p", p=P)
            sp.dma_start(vrows[:, 2, :], fw[0:P]).then_inc(small_in, 16)
            sp.dma_start(vrows[0:3 * FC - P, 3, :], fw[P:3 * FC]).then_inc(small_in, 16)
            wv = io["w_ada"][0].rearrange("(k p) m -> p k m", p=P)
            for s in range(4):
                sp.dma_start(wada[:, s], wv[:, 4 * s:4 * s + 4, 0:512]).then_inc(w_in[s], 16)
            for b in range(TB):
                src = io["ctx"][0, b * P:(b + 1) * P, :] if b < CB else io["x"][0, (b - CB) * P:(b - CB + 1) * P, :]
                sp.dma_start(xnat[:, b, :], src).then_inc(x_in, 16)
            with sp.Fori(1, NJ) as j:
                for s in range(4):
                    sp.wait_ge(w_used, 4 * j + s - 3)
                    sp.dma_start(wada[:, s], wv[:, 4 * s:4 * s + 4, bass.ds(j * 512, 512)]).then_inc(w_in[s], 16)

        @block.gpsimd
        def _(pool):
            nc.gpsimd.memset(vrows[:], 0.0).then_inc(zeroed, 1)

        @block.scalar
        def _(act):
            act.wait_ge(small_in, 16 * 14)
            nc.scalar.activation(ccrow[:], ccrow[:], ACT.Silu).then_inc(silu_done, 1)
            with act.Fori(0, NJ // 2) as i:
                for e in range(2):
                    act.wait_ge(w_used, 8 * i + 4 * e + 4)
                    nc.scalar.activation(mrows[:, bass.ds(2 * i + e, 1), :], ps[0:2, e:e + 1, :],
                                         ACT.Copy).then_inc(rows_kept, 1)
            for k in range(KT):
                act.wait_ge(xmod_ready, k + 1)
                nc.scalar.activation(hT_hi[:, k, :], xmod[:, k % 2, :], ACT.Copy).then_inc(hi_ready, 1)

        @block.vector
        def _(dve):
            own = Chain(dve, dve_own)
            nc.vector.memset(ones[:], 1.0)
            nc.vector.memset(sb["eps"][:], EPS)
            dve.wait_ge(turned, 1)
            nc.vector.tensor_copy(cT[:], ps[:, 7, 0:32]).then_inc(turned_kept, 1)
            dve.wait_ge(turned, 2)
            own.after(nc.vector.tensor_copy(vecs[:], ps[:, 6, 0:V_ALL]))
            dve.wait_ge(mod_turned, 1)
            mt = ps[:, 4, 0:64].rearrange("p (a b) -> p a b", b=2)
            for b in range(2):
                last = nc.vector.tensor_tensor(modT[:, :, b], mt[:, :, b], vecs[:, V_ADA:V_ADA + 32], ALU.add)
            own.after(last)
            own.after(nc.vector.tensor_scalar(modT[:, KT:2 * KT, :], modT[:, KT:2 * KT, :], 1.0, None, ALU.add))
            def lo_part(k):
                dve.wait_ge(hi_ready, k + 1)
                nc.vector.tensor_tensor(hT_lo[:, k, :], xmod[:, k % 2, :], hT_hi[:, k, :].bitcast(F32),
                                        ALU.subtract).then_inc(lo_ready, 1)

            for k in range(KT):
                dve.wait_ge(x_turned, k + 1)
                if k >= 2:
                    dve.wait_ge(lo_ready, k - 1)
                pst = ps[:, 2 * (k % 2):2 * (k % 2) + 2, :].rearrange("p a b -> p (a b)")
                nc.vector.tensor_scalar(xmod[:, k % 2, 0:CTX], pst[:, 0:CTX], modT[:, k + KT, 1:2],
                                        modT[:, k, 1:2], ALU.mult, ALU.add)
                nc.vector.tensor_scalar(xmod[:, k % 2, CTX:TOK], pst[:, CTX:TOK], modT[:, k + KT, 0:1],
                                        modT[:, k, 0:1], ALU.mult, ALU.add).then_inc(xmod_ready, 1)
                if k >= 1:
                    lo_part(k - 1)
            lo_part(KT - 1)

        @block.tensor
        def _(pe):
            pe.wait_ge(silu_done, 1)
            nc.tensor.transpose(ps[:, 7, 0:32], ccrow[:], ident[0:32, 0:32]).then_inc(turned, 1)
            for b in range(3):
                nc.tensor.transpose(ps[:, 6, b * P:(b + 1) * P], vrows[:, b, :], ident[:])
            nc.tensor.transpose(ps[:, 6, 3 * P:V_ALL], vrows[0:V_ALL - 3 * P, 3, :], ident[0:V_ALL - 3 * P, 0:V_ALL - 3 * P]).then_inc(turned, 1)
            pe.wait_ge(turned_kept, 1)
            pe.wait_ge(dve_own, 1)
            with pe.Fori(0, NJ // 2) as i:
                for e in range(2):
                    pe.wait_ge(rows_kept, 2 * i)
                    for s in range(4):
                        pe.wait_ge(w_in[s], 32 * i + 16 * e + 16)
                        for k in range(4):
                            kt = 4 * s + k
                            mm = nc.tensor.matmul(ps[0:2, e, :], cT[:, kt:kt + KT + 1:KT], wada[:, s, k, :],
                                                  start=(kt == 0), stop=(kt == KT - 1))
                        mm.then_inc(w_used, 1)
            pe.wait_ge(rows_kept, NJ)
            for n in range(32):
                mm = nc.tensor.transpose(ps[:, 4, 2 * n:2 * n + 2], mrows[:, n // 4, (n % 4) * P:(n % 4 + 1) * P], ident[0:2, 0:2])
            mm.then_inc(mod_turned, 1)
            pe.wait_ge(x_in, 16 * TB)
            pe.wait_ge(dve_own, 3)
            for k in range(KT):
                if k >= 2:
                    pe.wait_ge(xmod_ready, k - 1)
                for b in range(TB):
                    mm = nc.tensor.transpose(ps[:, 2 * (k % 2) + b // 4, (b % 4) * P:(b % 4 + 1) * P],
                                             xnat[:, b, k * P:(k + 1) * P], ident[:])
                mm.then_inc(x_turned, 1)


def project_in(nc, io, sb, sem, psum):
    vecs, cT, ones = sb["vecs"], sb["cT"], sb["ones"]
    ps = psum["all"]
    hT_hi, hT_lo, zq, zkv, krg = sb["hT_hi"], sb["hT_lo"], sb["zq"], sb["zkv"], sb["krg"]
    scratch = io["scratch"]

    def at(name, shape, dtype, kb):
        return nc.alloc_sbuf_tensor_at(name, shape, dtype, offset=SB0 + int(kb * KB))

    raw = at("b_raw", [P, 4, 8 * P], F32, 118)
    w_hi = at("b_w_hi", [P, 2, 8 * P], F32R, 134)
    w_lo = at("b_w_lo", [P, 2, 8 * P], F32R, 142)
    conv = at("b_conv", [P, 2, TOK], F32, 150)
    u_out = at("b_u_out", [P, 2, TOK], F32, 156)
    o_out = at("b_o_out", [P, 2, LAT], F32, 162)
    sq = at("b_sq", [P, QK, TOK], F32, 150)
    v_out = at("b_v_out", [P, 4, 512], F32, 162)
    rms = at("b_rms", [P, LAT + TOK], F32, 170)
    kr_raw = at("b_kr_raw", [P, KT, ROPE], F32, 170)
    g_raw = at("b_g_raw", [P, KT, N_GATES], F32, 174)

    Q0 = 2
    KV0 = Q0 + 2 * QK
    U0 = KV0 + 2 * KVK
    O0 = U0 + 2 * UK
    V0 = O0 + 2 * UK
    N = V0 + 16

    kr_in = sem("b_kr_in")
    raw_in = [sem(f"b_raw_in{s}") for s in range(4)]
    zeroed = sem("b_zeroed")
    hi_ready = sem("b_hi_ready")
    lo_ready = sem("b_lo_ready")
    half_done = sem("b_half_done")
    psum_kept = sem("b_psum_kept")
    conv_ready = sem("b_conv_ready")
    silu_ready = sem("b_silu_ready")
    u_sent = [sem(f"b_u_sent{s}") for s in range(2)]
    o_ready = sem("b_o_ready")
    o_sent = [sem(f"b_o_sent{s}") for s in range(2)]
    v_ready = sem("b_v_ready")
    v_sent = sb["v_sent"]
    normed = sem("b_normed")
    sq_ready = sem("b_sq_ready")
    sum_ready = sem("b_sum_ready")
    root_ready = sem("b_root_ready")
    norm_own = sem("b_norm_own")
    dve_own = sem("b_dve_own")

    def fetched(eng, n, it=0):
        eng.wait_ge(raw_in[(n - 2) % 4], 16 * (it + (n - 2) // 4 + 1))

    def hi_part(act, n, it=0):
        fetched(act, n, it)
        act.wait_ge(half_done, 4 * it + n - 1)
        nc.scalar.activation(w_hi[:, n % 2, :], raw[:, (n - 2) % 4, :], ACT.Copy).then_inc(hi_ready, 1)

    def lo_part(dve, n, it=0):
        dve.wait_ge(hi_ready, 4 * it + n + 1)
        nc.vector.tensor_tensor(w_lo[:, n % 2, :], raw[:, (n - 2) % 4, :], w_hi[:, n % 2, :].bitcast(F32),
                                ALU.subtract).then_inc(lo_ready, 1)

    def krg_parts():
        both = [(64, 64 + ROPE, kr_raw[:, :, :])]
        for d in range(2):
            for g in range(2):
                c0 = (2 * d + g) * ML_HEADS
                both.append((32 * g + 4 * d, 32 * g + 4 * d + 4, g_raw[:, :, c0:c0 + ML_HEADS]))
        return both

    w_hi_full = w_hi[:].rearrange("p s (k m) -> p (s k) m", m=P)
    w_lo_full = w_lo[:].rearrange("p s (k m) -> p (s k) m", m=P)

    block = nc.Block()
    with block as block:
        @block.sync
        def _(sp):
            wv = io["w_in"][0].rearrange("(k p) m -> p k m", p=P)
            sp.dma_start(kr_raw[:], wv[:, :, OFF_KR:OFF_U]).then_inc(kr_in, 16)
            sp.dma_start(g_raw[:], wv[:, :, OFF_G:OFF_G + N_GATES]).then_inc(kr_in, 16)

            def fetch(n, col, half, it=0):
                s = (n - 2) % 4
                sp.dma_start(raw[:, s, :].rearrange("p (k m) -> p k m", m=P),
                             wv[:, 8 * half:8 * half + 8, bass.ds(col, P)]).then_inc(raw_in[s], 16)

            for n in range(4):
                fetch(Q0 + n, n // 2 * P, n % 2)
            for n0, n1, col0 in [(Q0 + 4, KV0, 2 * P), (KV0, U0, OFF_CKV), (U0, O0, OFF_U), (O0, V0, OFF_O)]:
                with sp.Fori(0, (n1 - n0) // 4) as i:
                    for s in range(4):
                        sp.wait_ge(lo_ready, 4 * i + n0 + s - 3)
                        fetch(n0 + s, col0 + i * 2 * P + s // 2 * P, s % 2)
            for c in range(2):
                with sp.Fori(0, 2) as i:
                    for s in range(4):
                        sp.wait_ge(lo_ready, 4 * i + V0 + 8 * c + s - 3)
                        sp.dma_start(raw[:, s, :].rearrange("p (k m) -> p k m", m=512),
                                     wv[:, bass.ds(i * 8 + 2 * s, 2), OFF_V + 512 * c:OFF_V + 512 * (c + 1)])\
                          .then_inc(raw_in[s], 16)
            sp.wait_ge(normed, 2)
            sb["first_c"].fetch_first(sp, io)

        @block.gpsimd
        def _(pool):
            sem.clear_last(pool)
            nc.gpsimd.memset(w_hi[:].bitcast(F32), 0.0)
            nc.gpsimd.memset(w_lo[:].bitcast(F32), 0.0).then_inc(zeroed, 1)
            sum_ada(nc, io, sb, sem, pool, range(0, 5))

        @block.scalar
        def _(act):
            act.wait_ge(kr_in, 32)
            act.wait_ge(zeroed, 1)
            for a, b, src in krg_parts():
                last = nc.scalar.activation(w_hi_full[:, :, a:b], src, ACT.Copy)
            last.then_inc(hi_ready, 2)
            hi_part(act, Q0)
            act.wait_ge(half_done, 2)
            nc.scalar.activation(krg[:, 0:CTX], ps[:, 2, 0:CTX], ACT.Copy)
            nc.scalar.activation(krg[:, CTX:TOK], ps[:, 0, :], ACT.Copy).then_inc(psum_kept, 1)

            def chunks(n0, n1, keep):
                with act.Fori(0, (n1 - n0) // 4) as i:
                    for s in range(4):
                        hi_part(act, n0 + s + 1, i)
                        if s % 2:
                            keep(i, s // 2)

            def keep_q(i, e):
                act.wait_ge(half_done, 4 * i + Q0 + 2 * e + 2)
                nc.scalar.activation(zq[:, bass.ds(2 * i + e, 1), :], ps[:, 1 - e:2 - e, :], ACT.Copy).then_inc(psum_kept, 1)

            def keep_kv(i, e):
                act.wait_ge(half_done, 4 * i + KV0 + 2 * e + 2)
                nc.scalar.activation(zkv[:, e, 0:CTX], ps[:, 3 - e, 0:CTX], ACT.Copy)
                nc.scalar.activation(zkv[:, e, CTX:TOK], ps[:, 1 - e, :], ACT.Copy).then_inc(psum_kept, 1)

            def keep_u(i, e):
                act.wait_ge(conv_ready, 2 * i + e + 1)
                if not isinstance(i, int) or i:
                    act.wait_ge(u_sent[e], 16 * i)
                nc.scalar.activation(u_out[:, e, :], conv[:, e, :], ACT.Silu).then_inc(silu_ready, 1)
                act.wait_ge(silu_ready, 2 * i + e + 1)
                act.dma_start(scratch["u"][bass.ds(2 * i + e, 1)].rearrange("a p t -> p a t"), u_out[:, e:e + 1, :])\
                   .then_inc(u_sent[e], 16)

            def keep_o(i, e):
                act.wait_ge(half_done, 4 * i + O0 + 2 * e + 2)
                act.wait_ge(o_sent[e], 16 * i)
                nc.scalar.activation(o_out[:, e, :], ps[:, 1 - e, :], ACT.Sigmoid).then_inc(o_ready, 1)
                act.wait_ge(o_ready, 2 * i + e + 1)
                act.dma_start(scratch["o"][bass.ds(2 * i + e, 1)].rearrange("a p t -> p a t"), o_out[:, e:e + 1, :])\
                   .then_inc(o_sent[e], 16)

            chunks(Q0, KV0, keep_q)
            chunks(KV0, U0, keep_kv)
            for s in range(4):
                hi_part(act, U0 + s + 1)
                if s == 2:
                    keep_u(0, 0)
            with act.Fori(1, UK // 2) as i:
                for s in range(4):
                    hi_part(act, U0 + s + 1, i)
                    if s == 0:
                        keep_u(i - 1, 1)
                    elif s == 2:
                        keep_u(i, 0)
            keep_u(UK // 2 - 1, 1)
            chunks(O0, V0, keep_o)
            for e in range(2):
                act.wait_ge(u_sent[e], 16 * UK // 2)
                act.wait_ge(o_sent[e], 16 * UK // 2)
            for c in range(2):
                for s in range(8):
                    n = V0 + 8 * c + s
                    if n + 1 < N:
                        hi_part(act, n + 1)
                    if (c, s) == (0, 1):
                        nc.scalar.activation(sq[:, :, 0:LAT], zq[:], ACT.Square).then_inc(sq_ready, 1)
                    elif (c, s) == (0, 3):
                        act.wait_ge(sum_ready, 1)
                        nc.scalar.activation(rms[:, 0:LAT], ps[:, 0, :], ACT.Sqrt, bias=sb["eps"][:],
                                             scale=1.0 / Q_LORA).then_inc(root_ready, 1)
                    elif (c, s) == (0, 4):
                        nc.scalar.activation(sq[:, 0:KVK, :], zkv[:], ACT.Square).then_inc(sq_ready, 1)
                    elif (c, s) == (0, 6):
                        act.wait_ge(sum_ready, 2)
                        nc.scalar.activation(rms[:, LAT:], ps[:, 0:2, :].rearrange("p a b -> p (a b)")[:, 0:TOK],
                                             ACT.Sqrt, bias=sb["eps"][:], scale=1.0 / KV_LORA).then_inc(root_ready, 1)
                act.wait_ge(half_done, V0 + 8 * c + 8)
                for t in range(TB):
                    e = (TB * c + t) % 4
                    if TB * c + t >= 4:
                        act.wait_ge(v_sent[e], 16 * ((TB * c + t) // 4))
                    nc.scalar.activation(v_out[:, e, :], ps[:, 2 + t, :], ACT.Copy).then_inc(v_ready, 1)
                    act.wait_ge(v_ready, 6 * c + t + 1)
                    act.dma_start(scratch["v"][t, :, 512 * c:512 * (c + 1)], v_out[:, e, :]).then_inc(v_sent[e], 16)

        @block.vector
        def _(dve):
            dve.wait_ge(hi_ready, 2)
            for a, b, src in krg_parts():
                last = nc.vector.tensor_tensor(w_lo_full[:, :, a:b], src, w_hi_full[:, :, a:b].bitcast(F32), ALU.subtract)
            last.then_inc(lo_ready, 2)
            lo_part(dve, Q0)
            own = Chain(dve, dve_own)
            norm = Chain(dve, norm_own)

            def chunks(n0, n1, then=None):
                with dve.Fori(0, (n1 - n0) // 4) as i:
                    for s in range(4):
                        lo_part(dve, n0 + s + 1, i)
                        if then and s % 2:
                            then(i, s // 2)

            def convolve(i, e):
                dve.wait_ge(half_done, 4 * i + U0 + 2 * e + 2)
                dve.wait_ge(silu_ready, 2 * i)
                own.at(2 * (2 * i + e))
                parts = [(ps[:, 3 - e, 0:CTX], conv[:, e, 0:CTX], CTX), (ps[:, 1 - e, :], conv[:, e, CTX:TOK], LAT)]

                def w(j):
                    return vecs[:, bass.ds(2 * i + (V_MLW + 8 * j + e), 1)]

                for src, dst, n in parts:
                    last = nc.vector.tensor_scalar(dst, src, w(1), vecs[:, bass.ds(2 * i + (V_MLB + e), 1)],
                                                   ALU.mult, ALU.add)
                own.after(last)
                for src, dst, n in parts:
                    last = nc.vector.scalar_tensor_tensor(dst[:, 1:n], src[:, 0:n - 1], w(0), dst[:, 1:n],
                                                          ALU.mult, ALU.add)
                own.after(last)
                for src, dst, n in parts:
                    last = nc.vector.scalar_tensor_tensor(dst[:, 0:n - 1], src[:, 1:n], w(2), dst[:, 0:n - 1],
                                                          ALU.mult, ALU.add)
                last.then_inc(conv_ready, 1)

            chunks(Q0, KV0)
            chunks(KV0, U0)
            chunks(U0, O0, convolve)
            chunks(O0, V0)
            for n in range(V0, N - 1):
                lo_part(dve, n + 1)
                if n in (V0 + 4, V0 + 7):
                    r, z, nk, v, cols = [(0, zq, QK, V_GQ, slice(0, LAT)), (1, zkv, KVK, V_GKV, slice(LAT, LAT + TOK))][n == V0 + 7]
                    dve.wait_ge(root_ready, r + 1)
                    norm.after(nc.vector.reciprocal(rms[:, cols], rms[:, cols]))
                    for k in range(nk):
                        last = nc.vector.scalar_tensor_tensor(z[:, k, :], z[:, k, :], vecs[:, v + k:v + k + 1],
                                                              rms[:, cols], ALU.mult, ALU.mult)
                    last.then_inc(normed, 1)

        @block.tensor
        def _(pe):
            def chunk(n, it, lat, ctx, w_step=None):
                for half in range(2):
                    pe.wait_ge(lo_ready, 4 * it + n + half + 1)
                    for k in range(8):
                        kt = 8 * half + k
                        for p, (w, h) in enumerate([(w_hi, hT_hi), (w_hi, hT_lo), (w_lo, hT_hi)]):
                            first, last = kt == 0 and p == 0, kt == KT - 1 and p == 2
                            lhs = w[:, (n + half) % 2, k * P:(k + 1) * P]
                            if ctx is not None:
                                nc.tensor.matmul(ps[:, ctx, 0:CTX], lhs, h[:, kt, 0:CTX], start=first, stop=last)
                            mm = nc.tensor.matmul(ps[:, lat, :], lhs, h[:, kt, CTX:TOK], start=first, stop=last)
                    mm.then_inc(half_done, 1)

            chunk(0, 0, 0, 2)
            with pe.Fori(0, QK // 2) as i:
                for e in range(2):
                    pe.wait_ge(psum_kept, 2 * i + e)
                    chunk(Q0 + 2 * e, i, 1 - e, None)
            for e in range(2):
                pe.wait_ge(psum_kept, QK + e)
                chunk(KV0 + 2 * e, 0, 1 - e, 3 - e)
            X0 = 1 + QK + KVK
            for n0, kept, before in [(U0, conv_ready, (psum_kept, X0)), (O0, o_ready, (conv_ready, UK))]:
                ctx = 3 if n0 == U0 else None
                for e in range(2):
                    pe.wait_ge(before[0], before[1] - 1 + e)
                    chunk(n0 + 2 * e, 0, 1 - e, ctx and ctx - e)
                with pe.Fori(1, UK // 2) as i:
                    for e in range(2):
                        pe.wait_ge(kept, 2 * i + e - 1)
                        chunk(n0 + 2 * e, i, 1 - e, ctx and ctx - e)
            for c in range(2):
                for s in range(8):
                    n = V0 + 8 * c + s
                    if (c, s) == (0, 3):
                        pe.wait_ge(sq_ready, 1)
                        for k in range(QK):
                            mm = nc.tensor.matmul(ps[:, 0, :], ones[:], sq[:, k, 0:LAT], start=(k == 0), stop=(k == QK - 1))
                        mm.then_inc(sum_ready, 1)
                    elif (c, s) == (0, 6):
                        pe.wait_ge(sq_ready, 2)
                        pe.wait_ge(root_ready, 1)
                        for k in range(KVK):
                            nc.tensor.matmul(ps[:, 0, :], ones[:], sq[:, k, 0:512], start=(k == 0), stop=(k == KVK - 1))
                            mm = nc.tensor.matmul(ps[:, 1, 0:TOK - 512], ones[:], sq[:, k, 512:TOK], start=(k == 0),
                                                  stop=(k == KVK - 1))
                        mm.then_inc(sum_ready, 1)
                    pe.wait_ge(lo_ready, n + 1)
                    for k in range(2):
                        kt = 2 * s + k
                        for t in range(TB):
                            if c and kt == 0:
                                pe.wait_ge(v_ready, t + 1)
                            for p, (w, h) in enumerate([(w_hi, hT_hi), (w_hi, hT_lo), (w_lo, hT_hi)]):
                                mm = nc.tensor.matmul(ps[:, 2 + t, :], h[:, kt, t * P:(t + 1) * P],
                                                      w[:, n % 2, k * 512:(k + 1) * 512],
                                                      start=(kt == 0 and p == 0), stop=(kt == KT - 1 and p == 2))
                    mm.then_inc(half_done, 1)


ADA_COLS = 1024


def sum_ada(nc, io, sb, sem, pool, parts):
    cT = sb["cT"]
    tag = f"ada{parts[0]}"

    def at(name, shape, kb):
        return nc.alloc_sbuf_tensor_at(f"{tag}_{name}", shape, F32, offset=SB0 + int(kb * KB))

    w = at("w", [P, 4, ADA_COLS], 179)
    acc = at("acc", [P, ADA_COLS], 195)
    prod = at("prod", [P, 2, ADA_COLS], 199)
    w_in = [sem(f"{tag}_w_in{s}") for s in range(4)]
    own_sem = sem(f"{tag}_own")
    sent = sem(f"{tag}_sent")
    wv = io["w_ada"][0].rearrange("(k p) m -> p k m", p=P)
    own = Chain(pool, own_sem)

    def fetch(part, k):
        c0 = 2 * D + part * ADA_COLS
        pool.dma_start(w[:, k % 4, :], wv[:, k, c0:c0 + ADA_COLS] if isinstance(part, int) else
                       wv[:, k, bass.ds(c0, ADA_COLS)]).then_inc(w_in[k % 4], 16)

    with pool.Fori(0, len(parts)) as i:
        part = i + parts[0]
        own.at((2 * KT - 1) * i)
        for k in range(3):
            fetch(part, k)
        pool.wait_ge(sent, 16 * i)
        for k in range(KT):
            pool.wait_ge(w_in[k % 4], 64 * i + 16 * (k // 4 + 1))
            out = acc[:] if k == 0 else prod[:, k % 2, :]
            own.after(nc.gpsimd.tensor_tensor(out, w[:, k % 4, :], cT[:, k:k + 1].to_broadcast([P, ADA_COLS]), ALU.mult))
            if k + 3 < KT:
                fetch(part, k + 3)
            if k:
                own.after(nc.gpsimd.tensor_tensor(acc[:], acc[:], prod[:, k % 2, :], ALU.add))
        pool.dma_start(io["scratch"]["ada"][bass.ds(part, 1)].rearrange("a p m -> p a m"), acc[:]).then_inc(sent, 16)
    pool.wait_ge(sent, 16 * len(parts))


class GateRows:

    def __init__(self, nc):
        def at(name, shape, kb):
            return nc.alloc_sbuf_tensor_at(name, shape, F32, offset=SB0 + int(kb * KB))

        H = ML_HEADS
        self.arow = at("gr_arow", [H, 2, TOK], 38)
        self.mrow = at("gr_mrow", [H, 2, LAT], 44)
        self.erow = at("gr_erow", [H, 2, LAT], 48)
        self.gate = at("gr_gate", [H, 4, TOK], 136)
        self.soft = at("gr_soft", [H, 2, TOK], 64)
        self.runs = at("gr_runs", [H, 2, TOK], 73)
        self.init = at("gr_init", [H, 2, 2], 52)
        self.bias = at("gr_bias", [H, 4], 52.25)
        self.f = self.gate[:].rearrange("h (d g) t -> h g d t", g=2)[:, 1]


def gate_scans(nc, dve, own, rows, step, arow_ready, erow_ready):
    gate, soft, runs, arow, mrow, erow, init = rows.gate, rows.soft, rows.runs, rows.arow, rows.mrow, rows.erow, rows.init
    ctx, lat = slice(0, CTX), slice(CTX, TOK)

    def back(x):
        return x[:, ::-1]

    order = [(back, lambda x: x), (lambda x: x, back)]
    if step == 0:
        own.after(nc.vector.scalar_tensor_tensor(rows.f, rows.f, 0.0, soft[:], ALU.min, ALU.subtract))
        for d in range(2):
            for part, turn in zip((ctx, lat), order[d]):
                x = turn(gate[:, 2 * d + 1, part])
                last = nc.vector.tensor_tensor_scan(turn(runs[:, d, part]), x, x, 0.0, ALU.add, ALU.bypass)
        own.after(last)
    elif step == 1:
        for d in range(2):
            i_row = gate[:, 2 * d, :]
            nc.vector.tensor_tensor(arow[:, d, lat], i_row[:, lat], runs[:, d, lat], ALU.subtract)
            if d == 0:
                nc.vector.tensor_tensor(arow[:, d, 0:CTX - 1], i_row[:, 0:CTX - 1], runs[:, d, 1:CTX], ALU.add)
                last = nc.vector.tensor_copy(arow[:, d, CTX - 1:CTX], i_row[:, CTX - 1:CTX])
            else:
                nc.vector.tensor_tensor(arow[:, d, 1:CTX], i_row[:, 1:CTX], runs[:, d, 0:CTX - 1], ALU.add)
                last = nc.vector.tensor_copy(arow[:, d, 0:1], i_row[:, 0:1])
        last.then_inc(arow_ready, 1)
        dve.wait_ge(arow_ready, 1)
        own.after(nc.vector.tensor_reduce(init[:, :, 0:1], arow[:, :, ctx], AX.X, ALU.max))
        for d, t in [(0, 0), (1, CTX - 1)]:
            last = nc.vector.tensor_tensor(init[:, d, 1:2], init[:, d, 0:1], runs[:, d, t:t + 1], ALU.max)
        own.after(last)
    else:
        for d in range(2):
            turn = order[d][1]
            x = turn(arow[:, d, lat])
            last = nc.vector.tensor_tensor_scan(turn(mrow[:, d, :]), x, x, init[:, d, 1:2], ALU.max, ALU.max)
        own.after(last)
        own.after(nc.vector.tensor_tensor(erow[:], mrow[:], runs[:, :, lat], ALU.add))
        nc.vector.tensor_scalar(erow[:], erow[:], -1.0, EXP_MAX, ALU.mult, ALU.min)
        nc.vector.tensor_scalar(mrow[:], mrow[:], -1.0, None, ALU.mult).then_inc(erow_ready, 1)


def matrix_memory(nc, io, sb, sem, psum):
    vecs, ident = sb["vecs"], sb["ident"]
    ps = psum["all"]
    yT, rows = sb["yT"], sb["rows"]
    scratch = io["scratch"]

    def at(name, shape, kb):
        return nc.alloc_sbuf_tensor_at(name, shape, F32, offset=SB0 + int(kb * KB))

    H = ML_HEADS
    arow, mrow, erow = rows.arow, rows.mrow, rows.erow
    mask = at("d_mask", [P, 2, P], 21)
    negmb = at("d_negmb", [P, H, 2, LAT], 5)
    cols = at("d_cols", [P, 2, TB + LB, H], 207)
    sel = at("d_sel", [H, H * P], 52)
    uh = at("d_uh", [P, 2, 2, TOK], 54)
    v1 = at("d_v1", [P, 2, TB, ML_V + 1], 66)
    wm = at("d_wm", [P, 2, 2, 2, P], 79)
    qT = at("d_qT", [P, LAT], 83)
    kT = at("d_kT", [P, TOK], 85)
    sT = at("d_sT", [P, 2, TB, LAT], 136)
    decay = at("d_decay", [P, 2, TB, LAT], 112)
    probT = at("d_probT", [P, 2, TB, LAT], 88)
    hid = at("d_hid", [P, 2, LB, ML_V], 160)
    sig_o = at("d_sig_o", [P, 2, 2, LAT], 168)
    small = at("d_small", [P, 2, LB], 176)
    stats = at("d_stats", [P, LB, 6], 176.25)
    mv = at("d_mv", [P, 2, LB, 2], 176.5)
    rstd = at("d_rstd", [P, 2, LB], 176.75)

    const_in = sem("d_const_in")
    mask_in = sem("d_mask_in")
    qk_in = [sem(f"d_qk_in{s}") for s in range(2)]
    v_in = [sem(f"d_v_in{s}") for s in range(2)]
    o_in = [sem(f"d_o_in{s}") for s in range(2)]
    ones_ready = sem("d_ones_ready")
    cols_turned = sem("d_cols_turned")
    cols_ready = sem("d_cols_ready")
    spread = sem("d_spread")
    spread_kept = sem("d_spread_kept")
    qk_done = sem("d_qk_done")
    qk_kept = sem("d_qk_kept")
    s_done = sem("d_s_done")
    s_kept = sem("d_s_kept")
    expo_ready = sem("d_expo_ready")
    decay_ready = sem("d_decay_ready")
    prob_ready = sem("d_prob_ready")
    num_done = sem("d_num_done")
    num_kept = sem("d_num_kept")
    var_ready = sem("d_var_ready")
    root_ready = sem("d_root_ready")
    normed = sem("d_normed")
    y_turned = sem("d_y_turned")
    y_kept = sem("d_y_kept")
    dve_own = sem("d_dve_own")
    ada_in = sem("d_ada_in")
    ada_summed = sem("d_ada_summed")
    ada = at("d_ada", [P, 4, ADA_COLS], 5)
    modR, ones = sb["modR"], sb["ones"]

    def span(d, j):
        return (j * P, LAT) if d == 0 else (0, (j + 1) * P)

    block = nc.Block()
    with block as block:
        @block.sync
        def _(sp):
            u_v = scratch["u"].rearrange("c p t -> p c t")
            v_v = scratch["v"].rearrange("t p m -> p t m")
            o_v = scratch["o"].rearrange("c p t -> p c t")

            def fetch_qk(h):
                sp.dma_start(uh[:, h % 2], u_v[:, 2 * h:2 * h + 2, :]).then_inc(qk_in[h % 2], 16)
                for q, w in enumerate([io["w_mq"], io["w_mk"]]):
                    sp.dma_start(wm[:, h % 2, q], w[0, h].rearrange("(k p) m -> p k m", p=P)).then_inc(qk_in[h % 2], 16)

            def fetch_v(h):
                sp.dma_start(v1[:, h % 2, :, 0:ML_V], v_v[:, :, h * ML_V:(h + 1) * ML_V]).then_inc(v_in[h % 2], 16)

            def fetch_o(h):
                sp.dma_start(sig_o[:, h % 2], o_v[:, 2 * h:2 * h + 2, :]).then_inc(o_in[h % 2], 16)

            sp.dma_start(sel[:], io["consts"][0:H, C_SEL:C_SEL + H * P]).then_inc(const_in, 16)
            fetch_qk(0)
            sp.dma_start(mask[:].rearrange("p a b -> p (a b)"), io["consts"][:, C_MASKF:C_MASKF + 2 * P]).then_inc(mask_in, 16)
            fetch_qk(1)
            for e in range(4):
                sp.wait_ge(sb["v_sent"][e], 16 * 2 * TB // 4)
            for h in range(2):
                fetch_v(h)
            for h in range(2):
                fetch_o(h)
            for h in range(2, H):
                sp.wait_ge(qk_done, h - 1)
                fetch_qk(h)
            for h in range(2, H):
                sp.wait_ge(num_done, 2 * LB * (h - 1))
                fetch_v(h)
            for h in range(2, H):
                sp.wait_ge(y_kept, 2 * (h - 1))
                fetch_o(h)
            sp.wait_ge(prob_ready, 2 * H)
            sb["first_e"].fetch_first(sp, io)
            sp.dma_start(ada[:], scratch["ada"][0:4].rearrange("a p m -> p a m")).then_inc(ada_in, 16)

        @block.gpsimd
        def _(pool):
            sem.clear_last(pool)
            nc.gpsimd.memset(v1[:, :, :, ML_V:ML_V + 1], 1.0).then_inc(ones_ready, 1)
            sum_ada(nc, io, sb, sem, pool, range(7, 8))

        @block.scalar
        def _(act):
            def keep_spread(n):
                act.wait_ge(spread, n + 1)
                nc.scalar.activation(negmb[:, n // 2, n % 2, :], ps[:, 6 + n % 2, :], ACT.Copy).then_inc(spread_kept, 1)

            def keep_front(h):
                act.wait_ge(qk_done, h + 1)
                nc.scalar.activation(qT[:], ps[:, 0, :], ACT.Copy, scale=ML_SCALE)
                nc.scalar.activation(kT[:, 0:CTX], ps[:, 2, 0:CTX], ACT.Copy)
                nc.scalar.activation(kT[:, CTX:TOK], ps[:, 1, :], ACT.Copy).then_inc(qk_kept, 1)
                for b in range(TB):
                    act.wait_ge(s_done, TB * h + b + 1)
                    if b == 0 and h >= 2:
                        act.wait_ge(prob_ready, 2 * (h - 1))
                    nc.scalar.activation(sT[:, h % 2, b, :], ps[:, b % 4, :], ACT.Copy).then_inc(s_kept, 1)

            def make_decay(h):
                for d in range(2):
                    act.wait_ge(expo_ready, 2 * h + d + 1)
                    nc.scalar.activation(decay[:, d, 0:CB, :], decay[:, d, 0:CB, :], ACT.Exp)
                    for j in range(LB):
                        a, c = span(d, j)
                        last = nc.scalar.activation(decay[:, d, CB + j, a:c], decay[:, d, CB + j, a:c], ACT.Exp)
                    last.then_inc(decay_ready, 1)

            def root(h):
                act.wait_ge(var_ready, h + 1)
                nc.scalar.activation(rstd[:, h % 2, :], mv[:, h % 2, :, 1], ACT.Sqrt, bias=sb["eps"][:]).then_inc(root_ready, 1)

            for n in range(2):
                keep_spread(n)
            keep_front(0)
            make_decay(0)
            for n in range(2, 2 * H):
                keep_spread(n)
            for h in range(1, H + 2):
                if h < H:
                    keep_front(h)
                if h >= 2:
                    root(h - 2)
                if h < H:
                    make_decay(h)

        @block.vector
        def _(dve):
            own = Chain(dve, dve_own)

            def exponents(h):
                dve.wait_ge(spread_kept, 2 if h == 0 else 2 * H)
                if h:
                    dve.wait_ge(prob_ready, 2 * h)
                for d in range(2):
                    for b in range(TB):
                        a, c = (0, LAT) if b < CB else span(d, b - CB)
                        last = nc.vector.tensor_scalar(decay[:, d, b, a:c], negmb[:, h, d, a:c], cols[:, d, b, h:h + 1],
                                                       0.0, ALU.add, ALU.min)
                    last.then_inc(expo_ready, 1)

            def weights(h, d):
                dve.wait_ge(decay_ready, 2 * h + d + 1)
                dve.wait_ge(s_kept, TB * (h + 1))
                if h:
                    dve.wait_ge(num_done, 2 * LB * (h - 1) + LB * (d + 1))
                nc.vector.tensor_tensor(probT[:, d, 0:CB, :], decay[:, d, 0:CB, :], sT[:, h % 2, 0:CB, :], ALU.mult)
                for j in range(LB):
                    a, c = span(d, j)
                    last = nc.vector.tensor_tensor(probT[:, d, CB + j, a:c], decay[:, d, CB + j, a:c],
                                                   sT[:, h % 2, CB + j, a:c], ALU.mult)
                own.after(last)
                for j in range(LB):
                    x = probT[:, d, CB + j, j * P:(j + 1) * P]
                    last = nc.vector.tensor_tensor(x, x, mask[:, d, :], ALU.mult)
                last.then_inc(prob_ready, 1)

            def divide(h, d):
                if d == 0 and h >= 2:
                    dve.wait_ge(y_turned, 2 * (h - 1))
                for t in range(LB):
                    src = ps[:, 4 + t % 2, :]
                    dve.wait_ge(num_done, 2 * LB * h + LB * d + t + 1)
                    x, inv = small[:, 0, t:t + 1], small[:, 1, t:t + 1]
                    own.after(nc.vector.tensor_scalar(x, src[:, ML_V:ML_V + 1], -1.0, cols[:, d, TB + t, h:h + 1],
                                                      ALU.mult, ALU.max))
                    own.after(nc.vector.tensor_tensor(x, x, src[:, ML_V:ML_V + 1], ALU.max))
                    own.after(nc.vector.reciprocal(inv, x))
                    out = hid[:, h % 2, t, :]
                    if d == 0:
                        nc.vector.tensor_scalar(out, src[:, 0:ML_V], inv, None, ALU.mult).then_inc(num_kept, 1)
                    else:
                        nc.vector.scalar_tensor_tensor(out, src[:, 0:ML_V], inv, out, ALU.mult, ALU.add).then_inc(num_kept, 1)

            def variance(h):
                dve.wait_ge(num_kept, 2 * LB * (h + 1))
                for t in range(LB):
                    last = nc.vector.bn_stats(stats[:, t, :], hid[:, h % 2, t, :])
                own.after(last)
                for t in range(LB):
                    last = nc.vector.bn_aggr(mv[:, h % 2, t, :], stats[:, t, :])
                last.then_inc(var_ready, 1)

            def norm(h):
                dve.wait_ge(root_ready, h + 1)
                own.after(nc.vector.reciprocal(rstd[:, h % 2, :], rstd[:, h % 2, :]))
                for t in range(LB):
                    last = nc.vector.tensor_scalar(hid[:, h % 2, t, :], hid[:, h % 2, t, :], mv[:, h % 2, t, 0:1],
                                                   rstd[:, h % 2, t:t + 1], ALU.subtract, ALU.mult)
                last.then_inc(normed, 1)

            def gate_out(h):
                dve.wait_ge(o_in[h % 2], 16 * (h // 2 + 1))
                for e in range(2):
                    c = 2 * h + e
                    dve.wait_ge(y_turned, c + 1)
                    nc.vector.scalar_tensor_tensor(yT[:, UK + c, :], ps[:, 6 + e, :], vecs[:, V_GHN + c:V_GHN + c + 1],
                                                   sig_o[:, h % 2, e, :], ALU.mult, ALU.mult).then_inc(y_kept, 1)

            dve.wait_ge(cols_turned, 1)
            nc.vector.tensor_copy(cols[:].rearrange("p a b c -> p (a b c)"), ps[:, 5, 0:2 * (TB + LB) * H]).then_inc(cols_ready, 1)
            dve.wait_ge(cols_ready, 1)
            exponents(0)
            dve.wait_ge(mask_in, 16)
            for d in range(2):
                weights(0, d)
            for h in range(1, H + 2):
                if h < H:
                    exponents(h)
                if h >= 2:
                    norm(h - 2)
                for d in range(2):
                    if h <= H:
                        divide(h - 1, d)
                    if h < H:
                        weights(h, d)
                if h <= H:
                    variance(h - 1)
                if h >= 2:
                    gate_out(h - 2)
            dve.wait_ge(ada_summed, 1)
            nc.vector.tensor_tensor(modR[:, 0:2 * KT], ps[:, 3, 0:2 * KT], vecs[:, V_ADA + 2 * KT:V_ADA + 4 * KT], ALU.add)

        @block.tensor
        def _(pe):
            def spread_row(n):
                h, d = divmod(n, 2)
                if n >= 2:
                    pe.wait_ge(spread_kept, n - 1)
                nc.tensor.matmul(ps[:, 6 + n % 2, :], sel[:, h * P:(h + 1) * P], mrow[:, d, :], start=True,
                                 stop=True).then_inc(spread, 1)

            def front(h):
                pe.wait_ge(qk_in[h % 2], 48 * (h // 2 + 1))
                if h:
                    pe.wait_ge(s_kept, TB * h)
                for q, parts in enumerate([[(0, CTX, TOK)], [(2, 0, CTX), (1, CTX, TOK)]]):
                    for bank, a, b in parts:
                        for k in range(2):
                            mm = nc.tensor.matmul(ps[:, bank, 0:b - a], wm[:, h % 2, q, k, :], uh[:, h % 2, k, a:b],
                                                  start=(k == 0), stop=(k == 1))
                mm.then_inc(qk_done, 1)
                pe.wait_ge(qk_kept, h + 1)
                for b in range(TB):
                    if b >= 4:
                        pe.wait_ge(s_kept, TB * h + b - 3)
                    nc.tensor.matmul(ps[:, b % 4, :], kT[:, b * P:(b + 1) * P], qT[:], start=True,
                                     stop=True).then_inc(s_done, 1)

            def back(h):
                pe.wait_ge(v_in[h % 2], 16 * (h // 2 + 1))
                for d in range(2):
                    pe.wait_ge(prob_ready, 2 * h + d + 1)
                    for t in range(LB):
                        n = 2 * LB * h + LB * d + t
                        if n >= 2:
                            pe.wait_ge(num_kept, n - 1)
                        seen = list(range(CB)) + [CB + j for j in range(LB) if (j <= t if d == 0 else j >= t)]
                        for b in seen:
                            mm = nc.tensor.matmul(ps[:, 4 + t % 2, 0:ML_V + 1], probT[:, d, b, t * P:(t + 1) * P],
                                                  v1[:, h % 2, b, :], start=(b == seen[0]), stop=(b == seen[-1]))
                        mm.then_inc(num_done, 1)

            def turn(h):
                pe.wait_ge(normed, h + 1)
                for e in range(2):
                    if h:
                        pe.wait_ge(y_kept, 2 * h + e - 1)
                    for t in range(LB):
                        mm = nc.tensor.transpose(ps[:, 6 + e, t * P:(t + 1) * P], hid[:, h % 2, t, e * P:(e + 1) * P], ident[:])
                    mm.then_inc(y_turned, 1)

            for d in range(2):
                for b in range(TB + LB):
                    src = arow[:, d, b * P:(b + 1) * P] if b < TB else erow[:, d, (b - TB) * P:(b - TB + 1) * P]
                    c0 = (d * (TB + LB) + b) * H
                    mm = nc.tensor.transpose(ps[:, 5, c0:c0 + H], src, ident[0:H, 0:H])
            mm.then_inc(cols_turned, 1)
            pe.wait_ge(const_in, 16)
            for n in range(2):
                spread_row(n)
            front(0)
            for n in range(2, 2 * H):
                spread_row(n)
            pe.wait_ge(cols_ready, 1)
            pe.wait_ge(ones_ready, 1)
            pe.wait_ge(spread_kept, 2 * H)
            for h in range(1, H + 2):
                if h < H:
                    front(h)
                if h <= H:
                    back(h - 1)
                if h >= 2:
                    turn(h - 2)
                if h == H:
                    pe.wait_ge(ada_in, 16)
                    for c in range(2 * KT):
                        mm = nc.tensor.matmul(ps[:, 3, c:c + 1], ada[:, c // 8, c % 8 * P:(c % 8 + 1) * P], ones[:, 0:1],
                                              start=True, stop=True)
                    mm.then_inc(ada_summed, 1)


class FirstLoadsC:

    def __init__(self, nc, stack):
        def at(name, shape, kb):
            return nc.alloc_sbuf_tensor_at(name, shape, F32, offset=SB0 + int(kb * KB))

        self.wq = [at(f"c_wq{s}", [P, QK, 2 * QD], kb) for s, kb in enumerate((150, 54))]
        self.wkv = [at(f"c_wkv{s}", [P, KVK, 4 * P], kb) for s, kb in enumerate((156, 60))]
        self.cst = at("c_cst", [P, C_MASKF], 173)
        self.cst_in = stack.enter_context(nc.semaphore("c_cst_in"))
        self.w_in = [stack.enter_context(nc.semaphore(f"c_w_in{s}")) for s in range(2)]

    def fetch(self, sp, io, pair, s):
        uq = io["w_uq"][0].rearrange("(k p) m -> p k m", p=P)
        ukv = io["w_ukv"][0].rearrange("(k p) m -> p k m", p=P)
        for e in range(2):
            c0 = pair * 2 * QD + e * QD
            sp.dma_start(self.wq[s][:, :, e * NOPE:(e + 1) * NOPE], uq[:, :, bass.ds(c0, NOPE)]).then_inc(self.w_in[s], 16)
            sp.dma_start(self.wq[s][:, :, 2 * NOPE + e * ROPE:2 * NOPE + (e + 1) * ROPE],
                         uq[:, :, bass.ds(c0 + NOPE, ROPE)]).then_inc(self.w_in[s], 16)
        sp.dma_start(self.wkv[s][:], ukv[:, :, bass.ds(pair * 4 * P, 4 * P)]).then_inc(self.w_in[s], 16)

    def fetch_first(self, sp, io):
        sp.dma_start(self.cst[:], io["consts"][:, 0:C_MASKF]).then_inc(self.cst_in, 16)
        self.fetch(sp, io, 0, 0)


def attention(nc, io, sb, sem, psum):
    vecs, ident, ones = sb["vecs"], sb["ident"], sb["ones"]
    ps = psum["all"]
    zq, zkv, krg, yT, rows = sb["zq"], sb["zkv"], sb["krg"], sb["yT"], sb["rows"]

    def at(name, shape, kb):
        return nc.alloc_sbuf_tensor_at(name, shape, F32, offset=SB0 + int(kb * KB))

    first_c = sb["first_c"]
    wq, wkv, cst = first_c.wq, first_c.wkv, first_c.cst
    kr2 = at("c_kr2", [P, TOK], 70)
    qn = at("c_qn", [P, 2, LAT], 83)
    qr = at("c_qr", [P, LAT], 87)
    qr_raw = at("c_qr_raw", [P, LAT], 89)
    rot = at("c_rot", [P, LAT], 91)
    kn = at("c_kn", [P, 2, TOK], 93)
    vv = at("c_v", [P, TB, 2 * VD], 99)
    prob = at("c_prob", [P, 2, TOK], 106)
    probT = at("c_probT", [P, 2, TB, LAT], 112)
    stat = at("c_stat", [P, 4, 2 * LB * 2], 79.5)

    cst_in, w_in = first_c.cst_in, first_c.w_in
    kr_turned = sem("c_kr_turned")
    kr_ready = sem("c_kr_ready")
    proj_done = sem("c_proj_done")
    proj_kept = sem("c_proj_kept")
    swap_done = sem("c_swap_done")
    qr_ready = sem("c_qr_ready")
    scores_done = sem("c_scores_done")
    negmax_ready = sem("c_negmax_ready")
    exp_ready = sem("c_exp_ready")
    prob_ready = sem("c_prob_ready")
    turned = sem("c_turned")
    turned_kept = sem("c_turned_kept")
    out_done = sem("c_out_done")
    out_kept = sem("c_out_kept")
    dve_own = sem("c_dve_own")
    gate_in = sem("c_gate_in")
    biased = sem("c_biased")
    soft_own = sem("c_soft_own")
    soft_ready = sem("c_soft_ready")
    arow_ready = sem("c_arow_ready")
    erow_ready = sem("c_erow_ready")
    gate_own = sem("c_gate_own")

    PAIRS = HEADS // 2
    U = 2 * LB
    def scores(u):
        return ps[:, 2 * (u % 2):2 * (u % 2) + 2, :].rearrange("p a b -> p (a b)")[:, 0:TOK]

    turned_ps = ps[:, 4:6, :].rearrange("p a b -> p (a b)")[:, 0:TOK]

    block = nc.Block()
    with block as block:
        @block.sync
        def _(sp):
            first_c.fetch(sp, io, 1, 1)
            H = ML_HEADS
            for d in range(2):
                for g in range(2):
                    r = 32 * g + H * d
                    sp.dma_start(rows.gate[:, 2 * d + g, :], krg[r:r + H, :]).then_inc(gate_in, 16)
            sp.dma_start(rows.bias[:], io["b_gate"][0].rearrange("(g h) -> h g", h=H),
                         allow_slow_non_contiguous=True).then_inc(gate_in, 16)
            with sp.Fori(1, PAIRS // 2) as i:
                for s in range(2):
                    sp.wait_ge(proj_done, 10 * (2 * i + s))
                    first_c.fetch(sp, io, 2 * i + s, s)

        @block.gpsimd
        def _(pool):
            sem.clear_last(pool)
            sum_ada(nc, io, sb, sem, pool, range(5, 7))

        first = lambda pair: isinstance(pair, int)

        def keep_turned(act, pair, u):
            act.wait_ge(turned, U * pair + u + 1)
            e, b = divmod(u, LB)
            nc.scalar.activation(probT[:, e, :, b * P:(b + 1) * P], turned_ps.rearrange("p (a b) -> p a b", b=P),
                                 ACT.Copy).then_inc(turned_kept, 1)

        @block.scalar
        def _(act):
            soft = Chain(act, soft_own)

            def attend(pair):
                for n in range(10):
                    act.wait_ge(proj_done, 10 * pair + n + 1)
                    bank = 6 + n % 2
                    if n == 0:
                        if not first(pair):
                            act.wait_ge(qr_ready, 1 * pair)
                        dst, src = qr_raw[:], ps[:, bank, :]
                    elif n < 3:
                        dst, src = qn[:, n - 1, :], ps[:, bank, :]
                    elif n < 7:
                        e, half = divmod(n - 3, 2)
                        cols = slice(0, CTX) if half == 0 else slice(CTX, TOK)
                        dst, src = kn[:, e, cols], ps[:, bank, 0:cols.stop - cols.start]
                    else:
                        t = 2 * (n - 7)
                        dst, src = vv[:, t:t + 2, :], ps[:, bank, :].rearrange("p (a b) -> p a b", a=2)
                    nc.scalar.activation(dst, src, ACT.Copy).then_inc(proj_kept, 1)
                for u in range(U):
                    act.wait_ge(negmax_ready, U * pair + u + 1)
                    if u >= 2:
                        act.wait_ge(turned, U * pair + u - 1)
                    nc.scalar.activation(prob[:, u % 2, :], scores(u), ACT.Exp, bias=stat[:, 0, u:u + 1],
                                         scale=ATT_SCALE, accum_out=stat[:, 1, u:u + 1]).then_inc(exp_ready, 1)
                    if u >= 1:
                        keep_turned(act, pair, u - 1)
                    if first(pair) and u == 1:
                        act.wait_ge(biased, 1)
                        soft.after(nc.scalar.activation(rows.soft[:], rows.f, ACT.Abs))
                        soft.after(nc.scalar.activation(rows.soft[:], rows.soft[:], ACT.Exp, scale=-1.0))
                        nc.scalar.activation(rows.soft[:], rows.soft[:], ACT.Ln, bias=1.0).then_inc(soft_ready, 1)
                    if first(pair) and u == U - 1:
                        act.wait_ge(erow_ready, 1)
                        nc.scalar.activation(rows.erow[:], rows.erow[:], ACT.Exp)
                keep_turned(act, pair, U - 1)
                for e in range(2):
                    act.wait_ge(out_done, 2 * pair + e + 1)
                    nc.scalar.activation(yT[:, bass.ds(2 * pair + e, 1), :], ps[:, 6 + e:7 + e, :],
                                         ACT.Copy).then_inc(out_kept, 1)

            attend(0)
            with act.Fori(1, PAIRS) as pair:
                attend(pair)

        @block.vector
        def _(dve):
            own = Chain(dve, dve_own)
            gates = Chain(dve, gate_own)
            dve.wait_ge(kr_turned, 1)
            dve.wait_ge(cst_in, 16)
            nc.vector.tensor_copy(kr2[:, 0:CTX], ps[:, 4, 0:CTX])
            nc.vector.tensor_tensor(kr2[:, CTX:TOK], ps[:, 5, :], cst[:, C_COS:C_COS + LAT], ALU.mult)
            own.after(nc.vector.tensor_tensor(rot[:], ps[:, 3, :], cst[:, C_SIN:C_SIN + LAT], ALU.mult))
            nc.vector.tensor_tensor(kr2[:, CTX:TOK], kr2[:, CTX:TOK], rot[:], ALU.add).then_inc(kr_ready, 1)
            base = own.n
            dve.wait_ge(gate_in, 80)
            for g in range(4):
                last = nc.vector.tensor_scalar(rows.gate[:, g, :], rows.gate[:, g, :], rows.bias[:, g:g + 1], None, ALU.add)
            last.then_inc(biased, 1)

            def attend(pair):
                own.at(base + (1 + 2 * U) * pair)
                dve.wait_ge(swap_done, pair + 1)
                dve.wait_ge(proj_kept, 10 * pair + 10)
                if not first(pair):
                    dve.wait_ge(scores_done, U * pair)
                nc.vector.tensor_tensor(rot[:], ps[:, 5, :], cst[:, C_SIN:C_SIN + LAT], ALU.mult)
                own.after(nc.vector.tensor_tensor(qr[:], qr_raw[:], cst[:, C_COS:C_COS + LAT], ALU.mult))
                nc.vector.tensor_tensor(qr[:], qr[:], rot[:], ALU.add).then_inc(qr_ready, 1)
                for u in range(U):
                    dve.wait_ge(scores_done, U * pair + u + 1)
                    own.after(nc.vector.tensor_reduce(stat[:, 2, u:u + 1], scores(u), AX.X, ALU.max))
                    nc.vector.tensor_scalar(stat[:, 0, u:u + 1], stat[:, 2, u:u + 1], -ATT_SCALE, None, ALU.mult)\
                      .then_inc(negmax_ready, 1)
                    dve.wait_ge(exp_ready, U * pair + u + 1)
                    own.after(nc.vector.reciprocal(stat[:, 2, U + u:U + u + 1], stat[:, 1, u:u + 1]))
                    nc.vector.tensor_scalar(prob[:, u % 2, :], prob[:, u % 2, :], stat[:, 2, U + u:U + u + 1], None,
                                            ALU.mult).then_inc(prob_ready, 1)
                    if first(pair) and 2 <= u < 5:
                        if u == 2:
                            dve.wait_ge(soft_ready, 1)
                        gate_scans(nc, dve, gates, rows, u - 2, arow_ready, erow_ready)

            attend(0)
            with dve.Fori(1, PAIRS) as pair:
                attend(pair)

        @block.tensor
        def _(pe):
            pe.wait_ge(cst_in, 16)
            kr = krg[ROPE:P, :]
            nc.tensor.matmul(ps[:, 4, 0:CTX], cst[ROPE:P, C_KDUP:C_KDUP + P], kr[:, 0:CTX], start=True, stop=True)
            nc.tensor.matmul(ps[:, 5, :], cst[ROPE:P, C_KDUP:C_KDUP + P], kr[:, CTX:TOK], start=True, stop=True)
            nc.tensor.matmul(ps[:, 3, :], cst[ROPE:P, C_KSWAP:C_KSWAP + P], kr[:, CTX:TOK], start=True,
                             stop=True).then_inc(kr_turned, 1)
            with pe.Fori(0, PAIRS // 2) as i:
                for s in range(2):
                    pair = 2 * i + s
                    pe.wait_ge(w_in[s], 80 * i + 80)
                    pe.wait_ge(out_kept, 2 * pair)
                    n = 0
                    wkvs = wkv[s][:].rearrange("p k (e m) -> p k e m", m=2 * P)

                    def bank_free(n):
                        if n >= 2:
                            pe.wait_ge(proj_kept, 10 * pair + n - 1)

                    for c0 in (2 * NOPE, 0, NOPE):
                        bank_free(n)
                        for k in range(QK):
                            mm = nc.tensor.matmul(ps[:, 6 + n % 2, :], wq[s][:, k, c0:c0 + P], zq[:, k, :], start=(k == 0), stop=(k == QK - 1))
                        mm.then_inc(proj_done, 1)
                        n += 1
                    pe.wait_ge(proj_kept, 10 * pair + 1)
                    pe.wait_ge(kr_ready, 1)
                    nc.tensor.matmul(ps[:, 5, :], cst[:, C_SWAP:C_SWAP + P], qr_raw[:], start=True, stop=True)\
                      .then_inc(swap_done, 1)
                    for e in range(2):
                        for a, b in [(0, CTX), (CTX, TOK)]:
                            bank_free(n)
                            for k in range(KVK):
                                mm = nc.tensor.matmul(ps[:, 6 + n % 2, 0:b - a], wkvs[:, k, e, 0:NOPE], zkv[:, k, a:b],
                                                      start=(k == 0), stop=(k == KVK - 1))
                            mm.then_inc(proj_done, 1)
                            n += 1
                    for t in range(0, TB, 2):
                        bank_free(n)
                        for tt in range(2):
                            for k in range(KVK):
                                mm = nc.tensor.matmul(ps[:, 6 + n % 2, tt * 256:(tt + 1) * 256],
                                                      zkv[:, k, (t + tt) * P:(t + tt + 1) * P], wkvs[:, k, :, NOPE:2 * P],
                                                      start=(k == 0), stop=(k == KVK - 1))
                        mm.then_inc(proj_done, 1)
                        n += 1

                    def score(u):
                        e, b = divmod(u, LB)
                        if u < 2:
                            pe.wait_ge(prob_ready, U * pair)
                        else:
                            pe.wait_ge(exp_ready, U * pair + u - 1)
                        r = slice(e * ROPE, (e + 1) * ROPE)
                        out = ps[:, 2 * (u % 2):2 * (u % 2) + 2, :]
                        for j, (a, c) in enumerate([(0, 512), (512, TOK)]):
                            nc.tensor.matmul(out[:, j, 0:c - a], qn[:, e, b * P:(b + 1) * P], kn[:, e, a:c], start=True, stop=False)
                            mm = nc.tensor.matmul(out[:, j, 0:c - a], qr[r, b * P:(b + 1) * P], kr2[r, a:c], start=False, stop=True)
                        mm.then_inc(scores_done, 1)

                    def turn(u):
                        pe.wait_ge(prob_ready, U * pair + u + 1)
                        pe.wait_ge(turned_kept, U * pair + u)
                        for t in range(TB):
                            mm = nc.tensor.transpose(ps[:, 4 + t // 4, (t % 4) * P:(t % 4 + 1) * P],
                                                     prob[:, u % 2, t * P:(t + 1) * P], ident[:])
                        mm.then_inc(turned, 1)

                    def weigh(e):
                        pe.wait_ge(turned_kept, U * pair + LB * (e + 1))
                        for t in range(TB):
                            mm = nc.tensor.matmul(ps[:, 6 + e, :], vv[:, t, e * VD:(e + 1) * VD], probT[:, e, t, :],
                                                  start=(t == 0), stop=(t == TB - 1))
                        mm.then_inc(out_done, 1)

                    pe.wait_ge(proj_kept, 10 * pair + 10)
                    pe.wait_ge(qr_ready, pair + 1)
                    for u in range(U + 1):
                        if u < U:
                            score(u)
                        if u >= 1:
                            turn(u - 1)
                        if u == LB + 2:
                            weigh(0)
                    weigh(1)


class FirstLoadsE:

    def __init__(self, nc, stack):
        self.raw = nc.alloc_sbuf_tensor_at("f_raw", [P, 3, KT * P], F32, offset=SB0 + 134 * KB)
        self.xs = nc.alloc_sbuf_tensor_at("e_xs", [P, 2, LB, P], F32, offset=SB0 + 118 * KB)
        self.raw_in = [stack.enter_context(nc.semaphore(f"f_raw_in{s}")) for s in range(3)]
        self.xs_in = [stack.enter_context(nc.semaphore(f"e_xs_in{s}")) for s in range(2)]

    def fetch_first(self, sp, io):
        out_w = io["w_out"][0].rearrange("(k p) m -> p k m", p=P)
        xv = io["x"][0].rearrange("(t p) m -> p t m", p=P)
        for n in range(2):
            cols = slice(n * P, (n + 1) * P)
            sp.dma_start(self.raw[:, n, :].rearrange("p (k m) -> p k m", m=P), out_w[:, :, cols]).then_inc(self.raw_in[n], 16)
            sp.dma_start(self.xs[:, n], xv[:, :, cols]).then_inc(self.xs_in[n], 16)


def finish(nc, io, sb, sem, psum):
    vecs, modR, ident, ones, eps = sb["vecs"], sb["modR"], sb["ident"], sb["ones"], sb["eps"]
    ps = psum["all"]
    yT, x1T, x1m_hi, x1m_lo = sb["yT"], sb["x1T"], sb["x1m_hi"], sb["x1m_lo"]

    def at(name, shape, dtype, kb):
        return nc.alloc_sbuf_tensor_at(name, shape, dtype, offset=SB0 + int(kb * KB))

    SLOT = KT * P
    first_e = sb["first_e"]
    raw, xs, raw_in, xs_in = first_e.raw, first_e.xs, first_e.raw_in, first_e.xs_in
    w_hi = at("f_w_hi", [P, 2, SLOT], F32R, 158)
    w_lo = at("f_w_lo", [P, 2, SLOT], F32R, 174)
    ada = at("e_ada", [P, 4, ADA_COLS], F32, 190)
    y_hi = at("e_y_hi", [P, KT, LAT], F32R, 54)
    y_lo = at("e_y_lo", [P, KT, LAT], F32R, 86)
    xa = at("e_xa", [P, 2, LAT], F32, 122)
    xp = at("e_xp", [P, 2, LAT], F32, 126)
    total = at("e_total", [P, LAT], F32, 130)
    pivot = at("e_pivot", [P, LAT], F32, 132)
    sqtot = at("e_sqtot", [P, LAT], F32, 196)
    sq = at("e_sq", [P, 2, LAT], F32, 192)
    diag = at("e_diag", [P, 2, LB, P], F32, 198)
    stat = at("e_stat", [P, 8, LB], F32, 207)
    fold = at("e_fold", [P, 4, KT], F32, 207.25)
    u = at("e_u", [P, 2, LAT], F32, 5)
    a = at("e_a", [P, 2, LAT], F32, 9)
    x1m = at("e_x1m", [P, 2, LAT], F32, 13)
    h_hi = at("f_h_hi", [P, 4, LAT], F32R, 118)
    h_lo = at("f_h_lo", [P, 4, LAT], F32R, 126)
    conv = at("f_conv", [P, LAT], F32, 17)
    act_out = at("f_act_out", [P, LAT], F32, 19)
    h = at("f_h", [P, LAT], F32, 190)
    xnat = at("g_xnat", [P, LB, D], F32, 54)
    gain = at("g_gain", [P, D], F32, 86)
    shift = at("g_shift", [P, D], F32, 94)
    stats = at("g_stats", [P, LB, 4, 6], F32, 192)
    mv = at("g_mv", [P, LB, 2], F32, 193)
    ginv = at("g_inv", [P, 2, LB], F32, 193.5)

    ada_in = sem("e_ada_in")
    y_hi_ready = sem("e_y_hi_ready")
    y_lo_ready = sem("e_y_lo_ready")
    ada_summed = sem("e_ada_summed")
    hi_ready = sem("f_hi_ready")
    lo_ready = sem("f_lo_ready")
    slot_done = sem("f_slot_done")
    x_turned = sem("e_x_turned")
    xa_ready = sem("e_xa_ready")
    xp_ready = sem("e_xp_ready")
    pivot_done = sem("e_pivot_done")
    pivot_ready = sem("e_pivot_ready")
    x1_ready = sem("e_x1_ready")
    sq_ready = sem("e_sq_ready")
    sq_added = sem("e_sq_added")
    total_ready = sem("e_total_ready")
    sums_done = sem("e_sums_done")
    var_ready = sem("e_var_ready")
    root_ready = sem("e_root_ready")
    diag_ready = sem("e_diag_ready")
    spread = sem("e_spread")
    u_ready = sem("e_u_ready")
    a_ready = sem("e_a_ready")
    x1m_ready = sem("e_x1m_ready")
    x1m_hi_ready = sem("e_x1m_hi_ready")
    x1m_lo_ready = sem("e_x1m_lo_ready")
    u2_ready = sem("e_u2_ready")
    alpha_ready = sem("e_alpha_ready")
    conv_ready = sem("f_conv_ready")
    silu_ready = sem("f_silu_ready")
    h_ready = sem("f_h_ready")
    h_hi_ready = sem("f_h_hi_ready")
    h_lo_ready = sem("f_h_lo_ready")
    down_done = sem("f_down_done")
    down_kept = sem("f_down_kept")
    vec_in = sem("g_vec_in")
    turned = sem("g_turned")
    turned_kept = sem("g_turned_kept")
    turned_seen = sem("g_turned_seen")
    gvar_ready = sem("g_var_ready")
    groot_ready = sem("g_root_ready")
    gfold_ready = sem("g_fold_ready")
    normed = sem("g_normed")
    gained = sem("g_gained")
    out_a_ready = sem("g_out_a_ready")
    out_b_ready = sem("g_out_b_ready")
    out_sent = sem("g_out_sent")
    dve_own = sem("f_dve_own")
    ln_own = sem("e_ln_own")
    pool_own = sem("e_pool_own")

    G = 4
    GROUPS = FC // G
    BODY = 3 * G
    FIRST = [("up", j, half) for j in range(G) for half in range(2)]
    TURN = FIRST[0:2] + [("down", q, None) for q in range(4)] + FIRST[2:]
    LAST = [("down", q, None) for q in range(4)]
    E0 = KT - 12
    FIRST0 = KT
    TURN0 = FIRST0 + len(FIRST)
    LAST0 = TURN0 + (GROUPS - 1) * BODY
    assert BODY % 6 == 0 and LAST0 + 4 == KT + 3 * FC
    GP, NBP, AG, NAB = range(4)

    block = nc.Block()
    with block as block:
        @block.gpsimd
        def _(pool):
            sem.clear_last(pool)

            def pivoted(m, s, it=0):
                pool.wait_ge(xa_ready, 6 * it + m + 1)
                if m >= 3 or not isinstance(it, int):
                    pool.wait_ge(x1_ready, 6 * it + m - 1)
                nc.gpsimd.tensor_tensor(xp[:, s, :], xa[:, s, :], pivot[:], ALU.subtract).then_inc(xp_ready, 1)
                pool.wait_ge(sq_ready, 6 * it + m + 1)
                pool.wait_ge(sq_added, 6 * it + m)
                nc.gpsimd.tensor_tensor(sqtot[:], sqtot[:], sq[:, s, :], ALU.add).then_inc(sq_added, 1)

            pool.wait_ge(pivot_ready, 1)
            pool.wait_ge(ada_summed, 1)
            pool.wait_ge(sq_ready, 1)
            nc.gpsimd.tensor_copy(sqtot[:], sq[:, 0, :]).then_inc(sq_added, 1)
            for m in range(1, E0):
                pivoted(m, m % 2)
            with pool.Fori(0, 2) as i:
                for k in range(6):
                    pivoted(E0 + k, k % 2, i)
            for m in range(KT):
                pool.wait_ge(a_ready, m + 1)
                pool.wait_ge(u_ready, m + 1)
                if m >= 2:
                    pool.wait_ge(x1m_lo_ready, m - 1)
                nc.gpsimd.tensor_tensor(x1m[:, m % 2, :], a[:, m % 2, :], u[:, m % 2, :], ALU.subtract).then_inc(x1m_ready, 1)
            pool.wait_ge(vec_in, 32)
            for t in range(LB):
                pool.wait_ge(gained, t + 1)
                nc.gpsimd.tensor_tensor(xnat[:, t, 0:D // 2], xnat[:, t, 0:D // 2], shift[:, 0:D // 2], ALU.add)\
                  .then_inc(out_a_ready, 1)

        @block.sync
        def _(sp):
            out_w = io["w_out"][0].rearrange("(k p) m -> p k m", p=P)
            up = io["w_up"][0].rearrange("(k p) m -> p k m", p=P)
            down = io["w_down"][0].rearrange("(f p) m -> p f m", p=P)
            xv = io["x"][0].rearrange("(t p) m -> p t m", p=P)

            def fetch(n, src, m, it=0, body=1):
                if not isinstance(it, int) or n >= 3:
                    sp.wait_ge(lo_ready, it * body + n - 2)
                sp.dma_start(raw[:, n % 3, :].rearrange("p (k m) -> p k m", m=m), src).then_inc(raw_in[n % 3], 16)

            def fetch_out(n, it=0):
                fetch(n, out_w[:, :, bass.ds(it * 6 * P + n * P, P)], P, it, 6)
                fetch_xs(n, it)

            def fetch_xs(n, it=0):
                if not isinstance(it, int) or n >= 2:
                    sp.wait_ge(x_turned, it * 6 + n - 1)
                sp.dma_start(xs[:, n % 2], xv[:, :, bass.ds(it * 6 * P + n * P, P)]).then_inc(xs_in[n % 2], 16)

            def fetch_mlp(n, what, group, it=0):
                kind, j, half = what
                if kind == "up":
                    fetch(n, up[:, :, bass.ds(group * (G * P) + (half * D_FF + j * P), P)], P, it, BODY)
                else:
                    fetch(n, down[:, bass.ds(group * G, G), j * 512:(j + 1) * 512], 512, it, BODY)

            sp.dma_start(ada[:], io["scratch"]["ada"][4:8].rearrange("a p m -> p a m")).then_inc(ada_in, 16)
            fetch(2, out_w[:, :, 2 * P:3 * P], P)
            fetch_xs(2)
            for n in range(3, E0):
                fetch_out(n)
            with sp.Fori(0, 2) as i:
                for k in range(6):
                    fetch_out(E0 + k, i)
            for k, what in enumerate(FIRST):
                fetch_mlp(FIRST0 + k, what, 0)
            with sp.Fori(0, GROUPS - 1) as i:
                for k, what in enumerate(TURN):
                    fetch_mlp(TURN0 + k, what, i + 1 if what[0] == "up" else i, i)
            for k, what in enumerate(LAST):
                fetch_mlp(LAST0 + k, what, GROUPS - 1)
            sp.wait_ge(slot_done, LAST0)
            sp.dma_start(gain[:], io["ln2_g"][0].partition_broadcast(P)).then_inc(vec_in, 16)
            sp.dma_start(shift[:], io["ln2_b"][0].partition_broadcast(P)).then_inc(vec_in, 16)
            for t in range(LB):
                for c, ready in enumerate((out_a_ready, out_b_ready)):
                    sp.wait_ge(ready, t + 1)
                    cols = slice(c * D // 2, (c + 1) * D // 2)
                    sp.dma_start(io["out"][0, t * P:(t + 1) * P, cols], xnat[:, t, cols]).then_inc(out_sent, 16)
            sp.wait_ge(out_sent, 16 * 2 * LB)

        @block.scalar
        def _(act):
            def hi_part(n, it=0, body=1):
                if isinstance(it, int):
                    act.wait_ge(raw_in[n % 3], 16 * (n // 3 + 1))
                else:
                    act.wait_ge(raw_in[n % 3], it * (16 * body // 3) + 16 * (n // 3 + 1))
                if not isinstance(it, int) or n >= 2:
                    act.wait_ge(slot_done, it * body + n - 1)
                nc.scalar.activation(w_hi[:, n % 2, :], raw[:, n % 3, :], ACT.Copy).then_inc(hi_ready, 1)

            def keep_x(m, it=0):
                act.wait_ge(x_turned, 6 * it + m + 1)
                if m == 2:
                    act.wait_ge(x1_ready, 1)
                elif m > 2:
                    act.wait_ge(xp_ready, 6 * it + m - 2)
                nc.scalar.activation(xa[:, m % 2, :], ps[:, 2 + m % 2, :], ACT.Copy, scale=ALPHA).then_inc(xa_ready, 1)

            def square(m, it=0):
                act.wait_ge(x1_ready, 6 * it + m + 1)
                if not isinstance(it, int) or m >= 2:
                    act.wait_ge(sq_added, 6 * it + m - 1)
                row = x1T[:, m, :] if isinstance(it, int) else x1T[:, bass.ds(6 * it + m, 1), :]
                nc.scalar.activation(sq[:, m % 2, :], row, ACT.Square).then_inc(sq_ready, 1)

            nc.scalar.activation(y_hi[:, 0, :], yT[:, 0, :], ACT.Copy).then_inc(y_hi_ready, 1)
            hi_part(0)
            for k in range(1, KT):
                nc.scalar.activation(y_hi[:, k, :], yT[:, k, :], ACT.Copy).then_inc(y_hi_ready, 1)
            keep_x(0)
            hi_part(1)
            keep_x(1)
            hi_part(2)
            act.wait_ge(pivot_done, 1)
            nc.scalar.activation(pivot[:], ps[:, 4, :], ACT.Copy, scale=1.0 / P).then_inc(pivot_ready, 1)
            act.wait_ge(ada_summed, 1)
            square(0)
            square(1)
            for m in range(2, E0):
                keep_x(m)
                hi_part(m + 1)
                square(m)
            with act.Fori(0, 2) as i:
                for k in range(6):
                    keep_x(E0 + k, i)
                    hi_part(E0 + k + 1, i, 6)
                    square(E0 + k, i)
            act.wait_ge(var_ready, 1)
            nc.scalar.activation(stat[:, 4, :], stat[:, 3, :], ACT.Sqrt, bias=eps[:]).then_inc(root_ready, 1)
            hi_part(FIRST0 + 1)
            act.wait_ge(spread, 1)

            def hi_x(m):
                act.wait_ge(x1m_ready, m + 1)
                nc.scalar.activation(x1m_hi[:, m, :], x1m[:, m % 2, :], ACT.Copy).then_inc(x1m_hi_ready, 1)

            for m in range(KT):
                if m >= 2:
                    act.wait_ge(x1m_ready, m - 1)
                nc.scalar.activation(u[:, m % 2, :], ps[:, 7, :], ACT.Identity, bias=fold[:, NBP, m:m + 1],
                                     scale=fold[:, GP, m:m + 1]).then_inc(u_ready, 1)
                if m:
                    hi_x(m - 1)
            hi_x(KT - 1)

            def alpha_part(m):
                act.wait_ge(alpha_ready, m - 1) if m >= 2 else act.wait_ge(x1m_ready, KT)
                nc.scalar.activation(u[:, m % 2, :], ps[:, 7, :], ACT.Identity, bias=fold[:, NAB, m:m + 1],
                                     scale=fold[:, AG, m:m + 1]).then_inc(u2_ready, 1)

            def chunk(c, j, down_slots):
                act.wait_ge(conv_ready, c + 1)
                nc.scalar.activation(act_out[:], conv[:], ACT.Silu).then_inc(silu_ready, 1)
                act.wait_ge(h_ready, c + 1)
                if down_slots is not None:
                    act.wait_ge(slot_done, down_slots)
                nc.scalar.activation(h_hi[:, j, :], h[:], ACT.Copy).then_inc(h_hi_ready, 1)

            for k, (kind, j, half) in enumerate(FIRST):
                if k:
                    hi_part(FIRST0 + k + 1)
                for m in (2 * k, 2 * k + 1):
                    alpha_part(m)
                if half == 1:
                    chunk(j, j, None)
            with act.Fori(0, GROUPS - 1) as i:
                for k, (kind, j, half) in enumerate(TURN):
                    if k == 6:
                        chunk(G * i + G, 0, i * BODY + TURN0 + 6)
                    hi_part(TURN0 + k + 1, i, BODY)
                    if half == 1 and j > 0:
                        chunk(G * i + G + j, j, None)

            def keep_turned(q):
                act.wait_ge(turned, q + 1)
                for t in range(LB):
                    last = nc.scalar.activation(xnat[:, t, q * 512:(q + 1) * 512], ps[:, t, :], ACT.Copy)
                last.then_inc(turned_kept, 1)

            for k in range(4):
                if k < 3:
                    hi_part(LAST0 + k + 1)
                if k >= 2:
                    keep_turned(k - 2)
            keep_turned(2)
            keep_turned(3)
            act.wait_ge(gvar_ready, 1)
            nc.scalar.activation(ginv[:, 0, :], mv[:, :, 1], ACT.Sqrt, bias=eps[:]).then_inc(groot_ready, 1)
            act.wait_ge(gfold_ready, 1)
            for t in range(LB):
                nc.scalar.activation(xnat[:, t, :], xnat[:, t, :], ACT.Identity, bias=ginv[:, 1, t:t + 1],
                                     scale=ginv[:, 0, t:t + 1]).then_inc(normed, 1)

        @block.vector
        def _(dve):
            own = Chain(dve, dve_own)
            ln = Chain(dve, ln_own)

            def lo_part(n, it=0, body=1):
                dve.wait_ge(hi_ready, it * body + n + 1)
                nc.vector.tensor_tensor(w_lo[:, n % 2, :], raw[:, n % 3, :], w_hi[:, n % 2, :].bitcast(F32),
                                        ALU.subtract).then_inc(lo_ready, 1)

            def y_part(k):
                dve.wait_ge(y_hi_ready, k + 1)
                nc.vector.tensor_tensor(y_lo[:, k, :], yT[:, k, :], y_hi[:, k, :].bitcast(F32), ALU.subtract)\
                  .then_inc(y_lo_ready, 1)

            y_part(0)
            lo_part(0)
            for k in range(1, KT):
                y_part(k)
            dve.wait_ge(ada_summed, 1)
            ln.after(nc.vector.tensor_tensor(modR[:, 2 * KT:], ps[:, 7, 0:2 * KT],
                                             vecs[:, V_ADA + 4 * KT:V_ADA + 6 * KT], ALU.add))
            scale = modR[:, 2 * KT:3 * KT]
            ln.after(nc.vector.tensor_scalar(scale, scale, 1.0, None, ALU.add))
            gain1, shift1 = vecs[:, V_LN1G:V_LN1G + KT], vecs[:, V_LN1B:V_LN1B + KT]
            nc.vector.tensor_tensor(fold[:, GP, :], gain1, scale, ALU.mult)
            nc.vector.tensor_scalar(fold[:, AG, :], gain1, ALPHA, None, ALU.mult)
            nc.vector.tensor_scalar(fold[:, NAB, :], shift1, -ALPHA, None, ALU.mult)
            ln.after(nc.vector.tensor_tensor(fold[:, NBP, :], shift1, scale, ALU.mult))
            ln.after(nc.vector.scalar_tensor_tensor(fold[:, NBP, :], fold[:, NBP, :], -1.0, modR[:, KT:2 * KT],
                                                    ALU.mult, ALU.subtract))
            dve.wait_ge(y_lo_ready, KT)
            lo_part(1)

            def add_x(m, it=0):
                dve.wait_ge(slot_done, 6 * it + m + 1)
                dve.wait_ge(xp_ready, 6 * it + m)
                row = x1T[:, m:m + 1, :] if isinstance(it, int) else x1T[:, bass.ds(6 * it + m, 1), :]
                gate = modR[:, m:m + 1] if isinstance(it, int) else modR[:, bass.ds(6 * it + m, 1)]
                nc.vector.scalar_tensor_tensor(row, ps[:, m % 2:m % 2 + 1, :], gate, xp[:, m % 2:m % 2 + 1, :],
                                               ALU.mult, ALU.add).then_inc(x1_ready, 1)
                dve.wait_ge(x1_ready, 6 * it + m + 1)
                dve.wait_ge(total_ready, 6 * it + m)
                nc.vector.tensor_tensor(total[:], total[:], row[:, 0], ALU.add).then_inc(total_ready, 1)

            dve.wait_ge(slot_done, 1)
            dve.wait_ge(xa_ready, 1)
            ln.after(nc.vector.scalar_tensor_tensor(x1T[:, 0, :], ps[:, 0, :], modR[:, 0:1], xa[:, 0, :], ALU.mult, ALU.add))
            lo_part(2)
            dve.wait_ge(pivot_ready, 1)
            nc.vector.tensor_tensor(x1T[:, 0, :], x1T[:, 0, :], pivot[:], ALU.subtract).then_inc(x1_ready, 1)
            dve.wait_ge(x1_ready, 1)
            nc.vector.tensor_copy(total[:], x1T[:, 0, :]).then_inc(total_ready, 1)
            add_x(1)
            for m in range(2, E0):
                lo_part(m + 1)
                add_x(m)
            with dve.Fori(0, 2) as i:
                for k in range(6):
                    lo_part(E0 + k + 1, i, 6)
                    add_x(E0 + k, i)
            dve.wait_ge(sums_done, 1)
            ln.after(nc.vector.tensor_scalar(stat[:, 0:2, :], ps[:, 5, 0:2 * LB].rearrange("p (a b) -> p a b", a=2), 1.0 / D,
                                             None, ALU.mult))
            ln.after(nc.vector.tensor_tensor(stat[:, 2, :], stat[:, 0, :], stat[:, 0, :], ALU.mult))
            ln.after(nc.vector.tensor_tensor(stat[:, 3, :], stat[:, 1, :], stat[:, 2, :], ALU.subtract))
            nc.vector.tensor_scalar(stat[:, 3, :], stat[:, 3, :], 0.0, None, ALU.max).then_inc(var_ready, 1)
            dve.wait_ge(root_ready, 1)
            ln.after(nc.vector.reciprocal(stat[:, 5, :], stat[:, 4, :]))
            ln.after(nc.vector.tensor_tensor(stat[:, 6, :], stat[:, 0, :], stat[:, 5, :], ALU.mult))
            for r in range(2):
                for t in range(LB):
                    last = nc.vector.tensor_scalar(diag[:, r, t, :], ident[:], stat[:, 5 + r, t:t + 1], None, ALU.mult)
            last.then_inc(diag_ready, 1)
            lo_part(FIRST0 + 1)
            dve.wait_ge(spread, 1)

            def lo_x(m):
                dve.wait_ge(x1m_hi_ready, m + 1)
                nc.vector.tensor_tensor(x1m_lo[:, m, :], x1m[:, m % 2, :], x1m_hi[:, m, :].bitcast(F32), ALU.subtract)\
                  .then_inc(x1m_lo_ready, 1)

            for m in range(KT + 2):
                if m < KT:
                    if m >= 2:
                        dve.wait_ge(x1m_ready, m - 1)
                    nc.vector.scalar_tensor_tensor(a[:, m % 2, :], x1T[:, m, :], fold[:, GP, m:m + 1], ps[:, 6, :],
                                                   ALU.mult, ALU.mult).then_inc(a_ready, 1)
                if m >= 2:
                    lo_x(m - 2)

            def alpha_part(m):
                ln.after(nc.vector.scalar_tensor_tensor(x1T[:, m, :], x1T[:, m, :], fold[:, AG, m:m + 1], ps[:, 6, :],
                                                        ALU.mult, ALU.mult))
                dve.wait_ge(u2_ready, m + 1)
                nc.vector.tensor_tensor(x1T[:, m, :], x1T[:, m, :], u[:, m % 2, :], ALU.subtract).then_inc(alpha_ready, 1)

            def chunk(c, j, slots):
                own.at(2 * c)
                dve.wait_ge(slot_done, slots)
                g = ps[:, 2 * (j % 2), :]
                up = ps[:, 2 * (j % 2) + 1, :]

                def col(v):
                    return vecs[:, c + v:c + v + 1] if isinstance(c, int) else vecs[:, bass.ds(c + v, 1)]

                if not isinstance(c, int) or c:
                    dve.wait_ge(silu_ready, c)
                own.after(nc.vector.tensor_scalar(conv[:], g, col(V_FW + FC), col(V_FB), ALU.mult, ALU.add))
                own.after(nc.vector.scalar_tensor_tensor(conv[:, 1:LAT], g[:, 0:LAT - 1], col(V_FW), conv[:, 1:LAT],
                                                         ALU.mult, ALU.add))
                nc.vector.scalar_tensor_tensor(conv[:, 0:LAT - 1], g[:, 1:LAT], col(V_FW + 2 * FC), conv[:, 0:LAT - 1],
                                               ALU.mult, ALU.add).then_inc(conv_ready, 1)
                dve.wait_ge(silu_ready, c + 1)
                if not isinstance(c, int) or c:
                    dve.wait_ge(h_lo_ready, c)
                nc.vector.tensor_tensor(h[:], act_out[:], up, ALU.mult).then_inc(h_ready, 1)
                dve.wait_ge(h_hi_ready, c + 1)
                nc.vector.tensor_tensor(h_lo[:, j, :], h[:], h_hi[:, j, :].bitcast(F32), ALU.subtract)\
                  .then_inc(h_lo_ready, 1)

            def add_down(n, q, group, it=0):
                for e in range(4):
                    m = 4 * q + e
                    if e < 3:
                        dve.wait_ge(down_done, group * (KT - 4) + 3 * q + e + 1)
                    else:
                        dve.wait_ge(slot_done, it * BODY + n + 1)
                    nc.vector.scalar_tensor_tensor(x1T[:, m, :], ps[:, 4 + e, :], modR[:, 3 * KT + m:3 * KT + m + 1],
                                                   x1T[:, m, :], ALU.mult, ALU.add).then_inc(down_kept, 1)

            for k, (kind, j, half) in enumerate(FIRST):
                if k:
                    lo_part(FIRST0 + k + 1)
                for m in (2 * k, 2 * k + 1):
                    alpha_part(m)
                if half == 1:
                    chunk(j, j, FIRST0 + k + 1)
            dve.wait_ge(alpha_ready, KT)
            with dve.Fori(0, GROUPS - 1) as i:
                for k, (kind, j, half) in enumerate(TURN):
                    if k == 6:
                        chunk(G * i + G, 0, i * BODY + TURN0 + 6)
                    lo_part(TURN0 + k + 1, i, BODY)
                    if kind == "down":
                        add_down(TURN0 + k, j, i, i)
                    elif half == 1 and j > 0:
                        chunk(G * i + G + j, j, i * BODY + TURN0 + k + 1)

            def see_turned(q):
                dve.wait_ge(turned_kept, q + 1)
                for t in range(LB):
                    last = nc.vector.bn_stats(stats[:, t, q, :], xnat[:, t, q * 512:(q + 1) * 512])
                last.then_inc(turned_seen, 1)

            for k in range(4):
                if k < 3:
                    lo_part(LAST0 + k + 1)
                add_down(LAST0 + k, k, GROUPS - 1)
                if k >= 2:
                    see_turned(k - 2)
            see_turned(2)
            see_turned(3)
            dve.wait_ge(turned_seen, 4)
            for t in range(LB):
                last = nc.vector.bn_aggr(mv[:, t, :], stats[:, t, :, :].rearrange("p a b -> p (a b)"))
            last.then_inc(gvar_ready, 1)
            dve.wait_ge(groot_ready, 1)
            ln.after(nc.vector.reciprocal(ginv[:, 0, :], ginv[:, 0, :]))
            nc.vector.scalar_tensor_tensor(ginv[:, 1, :], mv[:, :, 0], -1.0, ginv[:, 0, :], ALU.mult, ALU.mult)\
              .then_inc(gfold_ready, 1)
            dve.wait_ge(vec_in, 32)
            for t in range(LB):
                dve.wait_ge(normed, t + 1)
                nc.vector.tensor_tensor(xnat[:, t, :], xnat[:, t, :], gain[:], ALU.mult).then_inc(gained, 1)
                dve.wait_ge(gained, t + 1)
                nc.vector.tensor_tensor(xnat[:, t, D // 2:D], xnat[:, t, D // 2:D], shift[:, D // 2:D], ALU.add)\
                  .then_inc(out_b_ready, 1)

        @block.tensor
        def _(pe):
            passes = [(w_hi, y_hi, x1m_hi, h_hi), (w_hi, y_lo, x1m_lo, h_lo), (w_lo, y_hi, x1m_hi, h_hi)]

            def out_slot(m, it=0):
                pe.wait_ge(xs_in[m % 2], it * 48 + 16 * (m // 2 + 1))
                if not isinstance(it, int) or m >= 2:
                    pe.wait_ge(x1_ready, 6 * it + m - 1)
                for t in range(LB):
                    mm = nc.tensor.transpose(ps[:, 2 + m % 2, t * P:(t + 1) * P], xs[:, m % 2, t, :], ident[:])
                mm.then_inc(x_turned, 1)
                pe.wait_ge(lo_ready, 6 * it + m + 1)
                for k in range(KT):
                    if m == 0:
                        pe.wait_ge(y_lo_ready, k + 1)
                    for p, (w, y, _, _) in enumerate(passes):
                        mm = nc.tensor.matmul(ps[:, m % 2, :], w[:, m % 2, k * P:(k + 1) * P], y[:, k, :],
                                              start=(k == 0 and p == 0), stop=(k == KT - 1 and p == 2))
                mm.then_inc(slot_done, 1)

            def up_slot(n, j, half, c, it=0):
                if half == 0 and (not isinstance(c, int) or c >= 2):
                    pe.wait_ge(h_ready, c - 1)
                pe.wait_ge(lo_ready, it * BODY + n + 1)
                for k in range(KT):
                    if n == FIRST0 and isinstance(it, int):
                        pe.wait_ge(x1m_lo_ready, k + 1)
                    for p, (w, _, x, _) in enumerate(passes):
                        mm = nc.tensor.matmul(ps[:, 2 * (j % 2) + half, :], w[:, n % 2, k * P:(k + 1) * P], x[:, k, :],
                                              start=(k == 0 and p == 0), stop=(k == KT - 1 and p == 2))
                mm.then_inc(slot_done, 1)

            def down_slot(n, q, group, first=False, it=0):
                pe.wait_ge(h_lo_ready, G * group + G)
                pe.wait_ge(lo_ready, it * BODY + n + 1)
                for e in range(4):
                    m = 4 * q + e
                    if q:
                        pe.wait_ge(down_kept, group * KT + m - 3)
                    elif e == 0:
                        pe.wait_ge(h_lo_ready, G * group + G) if first else pe.wait_ge(down_kept, group * KT)
                    for k in range(G):
                        for p, (w, _, _, hh) in enumerate(passes):
                            mm = nc.tensor.matmul(ps[:, 4 + e, :], w[:, n % 2, k * 512 + e * P:k * 512 + (e + 1) * P],
                                                  hh[:, k, :], start=(k == 0 and p == 0), stop=(k == G - 1 and p == 2))
                    mm.then_inc(down_done if e < 3 else slot_done, 1)

            out_slot(0)
            pe.wait_ge(ada_in, 16)
            for c in range(2 * KT):
                mm = nc.tensor.matmul(ps[:, 7, c:c + 1], ada[:, c // 8, c % 8 * P:(c % 8 + 1) * P], ones[:, 0:1],
                                      start=True, stop=True)
            mm.then_inc(ada_summed, 1)
            out_slot(1)
            pe.wait_ge(ln_own, 5)
            nc.tensor.matmul(ps[:, 4, :], ones[:], x1T[:, 0, :], start=True, stop=True).then_inc(pivot_done, 1)
            for m in range(2, E0):
                out_slot(m)
            with pe.Fori(0, 2) as i:
                for k in range(6):
                    out_slot(E0 + k, i)
            pe.wait_ge(total_ready, KT)
            pe.wait_ge(sq_added, KT)
            for r, src in enumerate((total, sqtot)):
                for t in range(LB):
                    mm = nc.tensor.matmul(ps[:, 5, r * LB + t:r * LB + t + 1], src[:, t * P:(t + 1) * P], ones[:, 0:1],
                                          start=True, stop=True)
            mm.then_inc(sums_done, 1)
            pe.wait_ge(diag_ready, 1)
            for r in range(2):
                mm = nc.tensor.matmul(ps[:, 6 + r, :], ones[:], diag[:, r, :, :].rearrange("p a b -> p (a b)"), start=True, stop=True)
            mm.then_inc(spread, 1)
            for k, (kind, j, half) in enumerate(FIRST):
                up_slot(FIRST0 + k, j, half, j)
            pe.wait_ge(alpha_ready, KT)
            with pe.Fori(0, GROUPS - 1) as i:
                for k, (kind, j, half) in enumerate(TURN):
                    if kind == "up":
                        up_slot(TURN0 + k, j, half, G * i + G + j, i)
                    else:
                        down_slot(TURN0 + k, j, i, False, i)

            def turn(q):
                pe.wait_ge(down_kept, GROUPS * KT - KT + 4 * q + 4)
                if q:
                    pe.wait_ge(turned_kept, q)
                for t in range(LB):
                    for e in range(4):
                        mm = nc.tensor.transpose(ps[:, t, e * P:(e + 1) * P], x1T[:, 4 * q + e, t * P:(t + 1) * P], ident[:])
                mm.then_inc(turned, 1)

            for k in range(4):
                down_slot(LAST0 + k, k, GROUPS - 1)
                if k:
                    turn(k - 1)
            turn(3)


IN_NAMES = ["x", "c", "ctx", "c_ctx", "w_ada", "b_ada", "w_in", "g_q", "w_uq", "g_kv", "w_ukv", "ml_conv_w",
            "ml_conv_b", "w_mq", "w_mk", "b_gate", "g_hn", "w_out", "ln1_g", "ln1_b", "w_up", "ffn_conv_w",
            "ffn_conv_b", "w_down", "ln2_g", "ln2_b"]


def trunk_layer(nc, io, last_stage="g"):
    with ExitStack() as stack:
        def at(name, shape, dtype, kb):
            return nc.alloc_sbuf_tensor_at(name, shape, dtype, offset=SB0 + int(kb * KB))

        ps = stack.enter_context(nc.psum_tensor("ps", [P, 8, 512], F32))
        psum = {"all": ps}
        sb = {
            "ident": at("ident", [P, P], F32, 0),
            "ones": at("ones", [P, P], F32, 0.5),
            "vecs": at("vecs", [P, V_ALL], F32, 1),
            "cT": at("cT", [P, 2 * KT], F32, 3),
            "modT": at("modT", [P, 2 * KT, 2], F32, 3.25),
            "modR": at("modR", [P, 4 * KT], F32, 3.5),
            "eps": at("eps", [P, 1], F32, 3.75),
            "zq": at("zq", [P, QK, LAT], F32, 5),
            "zkv": at("zkv", [P, KVK, TOK], F32, 13),
            "krg": at("krg", [P, TOK], F32, 19),
            "hT_hi": at("hT_hi", [P, KT, TOK], F32R, 22),
            "hT_lo": at("hT_lo", [P, KT, TOK], F32R, 70),
            "yT": at("yT", [P, KT, LAT], F32, 22),
            "x1T": at("x1T", [P, KT, LAT], F32, 22),
            "x1m_hi": at("x1m_hi", [P, KT, LAT], F32R, 54),
            "x1m_lo": at("x1m_lo", [P, KT, LAT], F32R, 86),
        }
        sb["rows"] = GateRows(nc)
        sb["first_c"] = FirstLoadsC(nc, stack)
        sb["first_e"] = FirstLoadsE(nc, stack)
        sb["v_sent"] = [stack.enter_context(nc.semaphore(f"v_sent{s}")) for s in range(4)]
        scratch = {
            "u": nc.dram_tensor("scratch_u", [UK, P, TOK], F32).ap(),
            "v": nc.dram_tensor("scratch_v", [TB, P, ML_INNER], F32).ap(),
            "o": nc.dram_tensor("scratch_o", [UK, P, LAT], F32).ap(),
            "ada": nc.dram_tensor("scratch_ada", [8, P, 1024], F32).ap(),
        }
        stages = [load_and_modulate, project_in, attention, matrix_memory, finish]
        sems = [StageSems(nc) for _ in stages]
        for n, (name, stage) in enumerate(zip("abcdg", stages)):
            sems[n].last = sems[n - 1] if n else None
            stage(nc, io | {"scratch": scratch}, sb, sems[n], psum)
            if n:
                sems[n - 1].close()
            if name == last_stage:
                break
        sems[n].close()


def kernel(**inputs):
    import concourse.bacc as bacc
    from concourse.bass_utils import run_bass_kernel_spmd

    nc = bacc.Bacc("TRN2", target_bir_lowering=False, num_devices=1)
    consts, ident = host_constants()
    arrays, io = {}, {}
    for name, a in [(n, inputs[n]) for n in IN_NAMES] + [("consts", consts), ("ident", ident)]:
        a = np.ascontiguousarray(a)
        arrays[f"in_{name}"] = a
        io[name] = nc.dram_tensor(f"in_{name}", a.shape, F32, kind="ExternalInput").ap()
    io["out"] = nc.dram_tensor("out", [1, LAT, D], F32, kind="ExternalOutput").ap()
    trunk_layer(nc, io)
    r = run_bass_kernel_spmd(nc, [arrays], core_ids=[0])
    return r.results[0]["out"]
```

```python
from contextlib import ExitStack

import numpy as np

import concourse.bass as bass
from concourse import mybir

F32 = mybir.dt.float32
F32R = mybir.dt.float32r
ALU = mybir.AluOpType
ACT = mybir.ActivationFunctionType
AX = mybir.AxisListType

P = 128
D = 2048
KT = D // P
LAT = 512
CTX = 256
TOK = CTX + LAT
GRID_W = 64
HEADS = 8
NOPE = 128
ROPE = 64
VD = 128
QD = NOPE + ROPE
Q_LORA = 512
KV_LORA = 256
QK = 4
KVK = 2
ML_HEADS = 4
ML_QK = 128
ML_V = 256
ML_INNER = ML_HEADS * ML_V
UK = ML_INNER // P
N_GATES = 16
D_FF = 5632
FC = D_FF // P
OFF_CKV = Q_LORA
OFF_KR = Q_LORA + KV_LORA
OFF_U = OFF_KR + ROPE
OFF_V = OFF_U + ML_INNER
OFF_O = OFF_V + ML_INNER
OFF_G = OFF_O + ML_INNER
TB = TOK // P
LB = LAT // P
CB = CTX // P
ALPHA = 2.0 ** 0.25
EPS = 1e-6
ATT_SCALE = float(QD) ** -0.5
ML_SCALE = float(ML_QK) ** -0.5
EXP_MAX = 87.0

V_ADA = 0
V_GQ = 96
V_GKV = 100
V_GHN = 102
V_MLW = 128
V_MLB = 152
V_LN1G = 160
V_LN1B = 176
V_FB = 192
V_FW = 256
V_ALL = V_FW + 3 * FC

C_SWAP = 0
C_KDUP = 128
C_KSWAP = 256
C_COS = 384
C_SIN = C_COS + LAT
C_MASKF = C_SIN + LAT
C_MASKB = C_MASKF + P
C_SEL = C_MASKB + P
C_ALL = C_SEL + ML_HEADS * P


def host_constants():
    c = np.zeros((P, C_ALL), np.float32)
    part = np.array([r + 16 if r % 32 < 16 else r - 16 for r in range(ROPE)])
    for m in range(P):
        h, r = divmod(m, ROPE)
        c[h * ROPE + part[r], C_SWAP + m] = 1.0
        c[ROPE + r, C_KDUP + m] = 1.0
        c[ROPE + part[r], C_KSWAP + m] = 1.0
    inv = np.float32(10000.0) ** (-np.arange(16, dtype=np.float32) / 16)
    t = np.arange(LAT)
    pos = np.stack([t // GRID_W, t % GRID_W]).astype(np.float32)
    for m in range(P):
        r = m % ROPE
        ang = (pos[r // 32] * inv[r % 16]).astype(np.float32)
        c[m, C_COS:C_COS + LAT] = np.cos(ang)
        c[m, C_SIN:C_SIN + LAT] = np.sin(ang) * (-1.0 if r % 32 < 16 else 1.0)
    s, q = np.meshgrid(np.arange(P), np.arange(P), indexing="ij")
    c[:, C_MASKF:C_MASKF + P] = s <= q
    c[:, C_MASKB:C_MASKB + P] = s >= q
    for h in range(ML_HEADS):
        c[h, C_SEL + h * P:C_SEL + (h + 1) * P] = 1.0
    return c, np.eye(P, dtype=np.float32)


KB = 1024
SB0 = 16512


class Chain:

    def __init__(self, eng, sem):
        self.eng, self.sem, self.n = eng, sem, 0

    def at(self, value):
        self.n = value

    def after(self, ins):
        ins.then_inc(self.sem, 1)
        self.n = self.n + 1
        self.eng.wait_ge(self.sem, self.n)


class StageSems:

    def __init__(self, nc):
        self.nc, self.stack, self.handles, self.last = nc, ExitStack(), [], None

    def __call__(self, name):
        handle = self.stack.enter_context(self.nc.semaphore(name))
        self.handles.append(handle)
        return handle

    def clear_last(self, pool):
        for handle in self.last.handles:
            pool.sem_clear(handle)

    def close(self):
        self.stack.close()


def enter(nc, io, sb, sem, psum):
    vecs, cT, ones, ident, modT = sb["vecs"], sb["cT"], sb["ones"], sb["ident"], sb["modT"]
    ps = psum["all"]
    hT_hi, hT_lo, zq, zkv, krg = sb["hT_hi"], sb["hT_lo"], sb["zq"], sb["zkv"], sb["krg"]
    scratch = io["scratch"]

    def at(name, shape, dtype, kb):
        return nc.alloc_sbuf_tensor_at(name, shape, dtype, offset=SB0 + int(kb * KB))

    raw = at("b_raw", [P, 4, 8 * P], F32, 118)
    w_hi = at("b_w_hi", [P, 2, 8 * P], F32R, 134)
    w_lo = at("b_w_lo", [P, 2, 8 * P], F32R, 142)
    conv = at("b_conv", [P, 2, TOK], F32, 150)
    u_out = at("b_u_out", [P, 2, TOK], F32, 156)
    o_out = at("b_o_out", [P, 2, LAT], F32, 162)
    sq = at("b_sq", [P, QK, TOK], F32, 150)
    v_out = at("b_v_out", [P, 4, 512], F32, 162)
    rms = at("b_rms", [P, LAT + TOK], F32, 170)
    kr_raw = at("b_kr_raw", [P, KT, ROPE], F32, 170)
    g_raw = at("b_g_raw", [P, KT, N_GATES], F32, 174)

    vrows = at("a_vrows", [P, 5, P], F32, 166)
    ccrow = at("a_ccrow", [32, P], F32, 169)
    wada = at("a_wada", [P, 4, 4, 512], F32, 175)
    xnat = at("a_xnat", [P, TB, D], F32, 22)
    xT = at("a_xT", [P, KT, TOK], F32, 70)
    mrows = at("a_mrows", [2, 8, 512], F32, 150)
    xmod = at("a_xmod", [P, 2, TOK], F32, 150)
    NJ = 2 * D // 512

    Q0 = 2
    KV0 = Q0 + 2 * QK
    U0 = KV0 + 2 * KVK
    O0 = U0 + 2 * UK
    V0 = O0 + 2 * UK
    N = V0 + 16

    small_in = sem("a_small_in")
    x_in = [sem(f"a_x_in{b}") for b in range(TB)]
    w_in = [sem(f"a_w_in{s}") for s in range(4)]
    rows_zeroed = sem("a_rows_zeroed")
    silu_done = sem("a_silu_done")
    turned = sem("a_turned")
    turned_kept = sem("a_turned_kept")
    w_used = sem("a_w_used")
    rows_kept = sem("a_rows_kept")
    x_turned = sem("a_x_turned")
    x_kept = sem("a_x_kept")
    mod_turned = sem("a_mod_turned")
    mod_ready = sem("a_mod_ready")
    ctx_ready = sem("a_ctx_ready")
    xmod_ready = sem("a_xmod_ready")
    h_hi_ready = sem("a_h_hi_ready")
    h_lo_ready = sem("a_h_lo_ready")
    vec_own = sem("a_vec_own")
    kr_in = sem("b_kr_in")
    raw_in = [sem(f"b_raw_in{s}") for s in range(4)]
    zeroed = sem("b_zeroed")
    hi_ready = sem("b_hi_ready")
    lo_ready = sem("b_lo_ready")
    half_done = sem("b_half_done")
    psum_kept = sem("b_psum_kept")
    conv_ready = sem("b_conv_ready")
    silu_ready = sem("b_silu_ready")
    u_sent = [sem(f"b_u_sent{s}") for s in range(2)]
    o_ready = sem("b_o_ready")
    o_sent = [sem(f"b_o_sent{s}") for s in range(2)]
    v_ready = sem("b_v_ready")
    v_sent = sb["v_sent"]
    normed = sem("b_normed")
    sq_ready = sem("b_sq_ready")
    sum_ready = sem("b_sum_ready")
    root_ready = sem("b_root_ready")
    norm_own = sem("b_norm_own")
    dve_own = sem("b_dve_own")

    def fetched(eng, n, it=0):
        eng.wait_ge(raw_in[(n - 2) % 4], 16 * (it + (n - 2) // 4 + 1))

    def hi_part(act, n, it=0):
        fetched(act, n, it)
        act.wait_ge(half_done, 4 * it + n - 1)
        nc.scalar.activation(w_hi[:, n % 2, :], raw[:, (n - 2) % 4, :], ACT.Copy).then_inc(hi_ready, 1)

    def lo_part(dve, n, it=0):
        dve.wait_ge(hi_ready, 4 * it + n + 1)
        nc.vector.tensor_tensor(w_lo[:, n % 2, :], raw[:, (n - 2) % 4, :], w_hi[:, n % 2, :].bitcast(F32),
                                ALU.subtract).then_inc(lo_ready, 1)

    def krg_parts():
        both = [(64, 64 + ROPE, kr_raw[:, :, :])]
        for d in range(2):
            for g in range(2):
                c0 = (2 * d + g) * ML_HEADS
                both.append((32 * g + 4 * d, 32 * g + 4 * d + 4, g_raw[:, :, c0:c0 + ML_HEADS]))
        return both

    w_hi_full = w_hi[:].rearrange("p s (k m) -> p (s k) m", m=P)
    w_lo_full = w_lo[:].rearrange("p s (k m) -> p (s k) m", m=P)

    block = nc.Block()
    with block as block:
        @block.sync
        def _(sp):
            def rows(ap):
                return ap.rearrange("(r p) -> r p", p=P)

            ada = io["w_ada"][0].rearrange("(k p) m -> p k m", p=P)
            wv = io["w_in"][0].rearrange("(k p) m -> p k m", p=P)
            sp.dma_start(ident[:], io["ident"]).then_inc(small_in, 16)
            sp.dma_start(ccrow[0:16, :], rows(io["c"][0])).then_inc(small_in, 16)
            sp.dma_start(ccrow[16:32, :], rows(io["c_ctx"])).then_inc(small_in, 16)
            sp.dma_start(wada[:, 0], ada[:, 0:4, 0:512]).then_inc(w_in[0], 16)
            vectors = [(0, V_ADA, rows(io["b_ada"][0])), (0, V_GQ, rows(io["g_q"][0])), (0, V_GKV, rows(io["g_kv"][0])),
                       (0, V_GHN, io["g_hn"][0].rearrange("h (a p) -> (h a) p", p=P)),
                       (1, V_MLW, io["ml_conv_w"][0].rearrange("w (a p) -> (w a) p", p=P)),
                       (1, V_MLB, rows(io["ml_conv_b"][0])), (1, V_LN1G, rows(io["ln1_g"][0])),
                       (1, V_LN1B, rows(io["ln1_b"][0])), (1, V_FB, rows(io["ffn_conv_b"][0]))]
            for b, v, src in vectors:
                r = v - b * P
                sp.wait_ge(rows_zeroed, 1)
                sp.dma_start(vrows[r:r + src.shape[0], b, :], src).then_inc(small_in, 16)
            fw = io["ffn_conv_w"][0].rearrange("w (a p) -> (w a) p", p=P)
            sp.dma_start(vrows[:, 2, :], fw[0:P]).then_inc(small_in, 16)
            sp.dma_start(vrows[0:3 * FC - P, 3, :], fw[P:3 * FC]).then_inc(small_in, 16)
            for s in range(1, 4):
                sp.dma_start(wada[:, s], ada[:, 4 * s:4 * s + 4, 0:512]).then_inc(w_in[s], 16)
            for j in range(1, NJ):
                if j <= TB:
                    b = j - 1
                    src = io["ctx"][0, b * P:(b + 1) * P, :] if b < CB else io["x"][0, (b - CB) * P:(b - CB + 1) * P, :]
                    sp.dma_start(xnat[:, b, :], src).then_inc(x_in[b], 16)
                else:
                    sp.dma_start(kr_raw[:], wv[:, :, OFF_KR:OFF_U]).then_inc(kr_in, 16)
                    sp.dma_start(g_raw[:], wv[:, :, OFF_G:OFF_G + N_GATES]).then_inc(kr_in, 16)
                for s in range(4):
                    sp.wait_ge(w_used, 4 * j + s - 3)
                    sp.dma_start(wada[:, s], ada[:, 4 * s:4 * s + 4, j * 512:(j + 1) * 512]).then_inc(w_in[s], 16)

            def fetch(n, col, half, it=0):
                s = (n - 2) % 4
                sp.dma_start(raw[:, s, :].rearrange("p (k m) -> p k m", m=P),
                             wv[:, 8 * half:8 * half + 8, bass.ds(col, P)]).then_inc(raw_in[s], 16)

            for n in range(4):
                fetch(Q0 + n, n // 2 * P, n % 2)
            for n0, n1, col0 in [(Q0 + 4, KV0, 2 * P), (KV0, U0, OFF_CKV), (U0, O0, OFF_U), (O0, V0, OFF_O)]:
                with sp.Fori(0, (n1 - n0) // 4) as i:
                    for s in range(4):
                        sp.wait_ge(lo_ready, 4 * i + n0 + s - 3)
                        fetch(n0 + s, col0 + i * 2 * P + s // 2 * P, s % 2)
            for c in range(2):
                with sp.Fori(0, 2) as i:
                    for s in range(4):
                        sp.wait_ge(lo_ready, 4 * i + V0 + 8 * c + s - 3)
                        sp.dma_start(raw[:, s, :].rearrange("p (k m) -> p k m", m=512),
                                     wv[:, bass.ds(i * 8 + 2 * s, 2), OFF_V + 512 * c:OFF_V + 512 * (c + 1)])\
                          .then_inc(raw_in[s], 16)
            sp.wait_ge(normed, 2)
            sb["first_c"].fetch_first(sp, io)

        @block.gpsimd
        def _(pool):
            nc.gpsimd.memset(vrows[:], 0.0).then_inc(rows_zeroed, 1)
            nc.gpsimd.memset(w_hi[:].bitcast(F32), 0.0)
            nc.gpsimd.memset(w_lo[:].bitcast(F32), 0.0).then_inc(zeroed, 1)
            pool.wait_ge(w_used, 4 * NJ)
            sum_ada(nc, io, sb, sem, pool, range(0, 5))

        @block.scalar
        def _(act):
            act.wait_ge(small_in, 16 * 14)
            nc.scalar.activation(ccrow[:], ccrow[:], ACT.Silu).then_inc(silu_done, 1)
            for j in range(NJ):
                act.wait_ge(w_used, 4 * j + 4)
                nc.scalar.activation(mrows[:, j, :], ps[0:2, j % 2, :], ACT.Copy).then_inc(rows_kept, 1)
            act.wait_ge(kr_in, 32)
            act.wait_ge(zeroed, 1)
            for a, b, src in krg_parts():
                last = nc.scalar.activation(w_hi_full[:, :, a:b], src, ACT.Copy)
            last.then_inc(hi_ready, 2)
            act.wait_ge(mod_ready, 1)
            for k in range(KT):
                if k >= 2:
                    act.wait_ge(h_lo_ready, k - 1)
                nc.scalar.activation(xmod[:, k % 2, 0:CTX], xT[:, k, 0:CTX], ACT.Identity, bias=modT[:, k, 1:2],
                                     scale=modT[:, k + KT, 1:2]).then_inc(ctx_ready, 1)
                act.wait_ge(ctx_ready, k + 1)
                act.wait_ge(xmod_ready, k + 1)
                nc.scalar.activation(hT_hi[:, k, :], xmod[:, k % 2, :], ACT.Copy).then_inc(h_hi_ready, 1)
            act.wait_ge(half_done, 1)
            hi_part(act, Q0)
            act.wait_ge(half_done, 2)
            nc.scalar.activation(krg[:, 0:CTX], ps[:, 2, 0:CTX], ACT.Copy)
            nc.scalar.activation(krg[:, CTX:TOK], ps[:, 0, :], ACT.Copy).then_inc(psum_kept, 1)

            def chunks(n0, n1, keep):
                with act.Fori(0, (n1 - n0) // 4) as i:
                    for s in range(4):
                        hi_part(act, n0 + s + 1, i)
                        if s % 2:
                            keep(i, s // 2)

            def keep_q(i, e):
                act.wait_ge(half_done, 4 * i + Q0 + 2 * e + 2)
                nc.scalar.activation(zq[:, bass.ds(2 * i + e, 1), :], ps[:, 1 - e:2 - e, :], ACT.Copy).then_inc(psum_kept, 1)

            def keep_kv(i, e):
                act.wait_ge(half_done, 4 * i + KV0 + 2 * e + 2)
                nc.scalar.activation(zkv[:, e, 0:CTX], ps[:, 3 - e, 0:CTX], ACT.Copy)
                nc.scalar.activation(zkv[:, e, CTX:TOK], ps[:, 1 - e, :], ACT.Copy).then_inc(psum_kept, 1)

            def keep_u(i, e):
                act.wait_ge(conv_ready, 2 * i + e + 1)
                if not isinstance(i, int) or i:
                    act.wait_ge(u_sent[e], 16 * i)
                nc.scalar.activation(u_out[:, e, :], conv[:, e, :], ACT.Silu).then_inc(silu_ready, 1)
                act.wait_ge(silu_ready, 2 * i + e + 1)
                act.dma_start(scratch["u"][bass.ds(2 * i + e, 1)].rearrange("a p t -> p a t"), u_out[:, e:e + 1, :])\
                   .then_inc(u_sent[e], 16)

            def keep_o(i, e):
                act.wait_ge(half_done, 4 * i + O0 + 2 * e + 2)
                if not isinstance(i, int):
                    act.wait_ge(o_sent[e], 16 * i)
                nc.scalar.activation(o_out[:, e, :], ps[:, 1 - e, :], ACT.Sigmoid).then_inc(o_ready, 1)
                act.wait_ge(o_ready, 2 * i + e + 1)
                act.dma_start(scratch["o"][bass.ds(2 * i + e, 1)].rearrange("a p t -> p a t"), o_out[:, e:e + 1, :])\
                   .then_inc(o_sent[e], 16)

            chunks(Q0, KV0, keep_q)
            chunks(KV0, U0, keep_kv)
            for s in range(4):
                hi_part(act, U0 + s + 1)
                if s == 2:
                    keep_u(0, 0)
            with act.Fori(1, UK // 2) as i:
                for s in range(4):
                    hi_part(act, U0 + s + 1, i)
                    if s == 0:
                        keep_u(i - 1, 1)
                    elif s == 2:
                        keep_u(i, 0)
            for s in range(4):
                hi_part(act, O0 + s + 1)
                if s == 0:
                    keep_u(UK // 2 - 1, 1)
                elif s % 2:
                    keep_o(0, s // 2)
            with act.Fori(1, UK // 2) as i:
                for s in range(4):
                    hi_part(act, O0 + s + 1, i)
                    if s % 2:
                        keep_o(i, s // 2)
            for e in range(2):
                act.wait_ge(u_sent[e], 16 * UK // 2)
                act.wait_ge(o_sent[e], 16 * UK // 2)
            for c in range(2):
                for s in range(8):
                    n = V0 + 8 * c + s
                    if n + 1 < N:
                        hi_part(act, n + 1)
                    if (c, s) == (0, 1):
                        nc.scalar.activation(sq[:, :, 0:LAT], zq[:], ACT.Square).then_inc(sq_ready, 1)
                    elif (c, s) == (0, 3):
                        act.wait_ge(sum_ready, 1)
                        nc.scalar.activation(rms[:, 0:LAT], ps[:, 0, :], ACT.Sqrt, bias=sb["eps"][:],
                                             scale=1.0 / Q_LORA).then_inc(root_ready, 1)
                    elif (c, s) == (0, 4):
                        nc.scalar.activation(sq[:, 0:KVK, :], zkv[:], ACT.Square).then_inc(sq_ready, 1)
                    elif (c, s) == (0, 6):
                        act.wait_ge(sum_ready, 2)
                        nc.scalar.activation(rms[:, LAT:], ps[:, 0:2, :].rearrange("p a b -> p (a b)")[:, 0:TOK],
                                             ACT.Sqrt, bias=sb["eps"][:], scale=1.0 / KV_LORA).then_inc(root_ready, 1)
                act.wait_ge(half_done, V0 + 8 * c + 8)
                for t in range(TB):
                    e = (TB * c + t) % 4
                    if TB * c + t >= 4:
                        act.wait_ge(v_sent[e], 16 * ((TB * c + t) // 4))
                    nc.scalar.activation(v_out[:, e, :], ps[:, 2 + t, :], ACT.Copy).then_inc(v_ready, 1)
                    act.wait_ge(v_ready, 6 * c + t + 1)
                    act.dma_start(scratch["v"][t, :, 512 * c:512 * (c + 1)], v_out[:, e, :]).then_inc(v_sent[e], 16)

        @block.vector
        def _(dve):
            vec = Chain(dve, vec_own)
            nc.vector.memset(ones[:], 1.0)
            nc.vector.memset(sb["eps"][:], EPS)
            dve.wait_ge(turned, 1)
            nc.vector.tensor_copy(cT[:], ps[:, 7, 0:32]).then_inc(turned_kept, 1)
            dve.wait_ge(turned, 2)
            vec.after(nc.vector.tensor_copy(vecs[:], ps[:, 6, 0:V_ALL]))
            for b in range(TB):
                for q in range(4):
                    dve.wait_ge(x_turned, 4 * b + q + 1)
                    nc.vector.tensor_copy(xT[:, 4 * q:4 * q + 4, b * P:(b + 1) * P],
                                          ps[:, 2 + q, :].rearrange("p (k t) -> p k t", t=P)).then_inc(x_kept, 1)
            dve.wait_ge(hi_ready, 2)
            for a, b, src in krg_parts():
                last = nc.vector.tensor_tensor(w_lo_full[:, :, a:b], src, w_hi_full[:, :, a:b].bitcast(F32), ALU.subtract)
            last.then_inc(lo_ready, 2)
            dve.wait_ge(mod_turned, 1)
            mt = ps[:, 7, 0:64].rearrange("p (a b) -> p a b", b=2)
            for b in range(2):
                last = nc.vector.tensor_tensor(modT[:, :, b], mt[:, :, b], vecs[:, V_ADA:V_ADA + 32], ALU.add)
            vec.after(last)
            dve.wait_ge(x_kept, 4 * TB)
            nc.vector.tensor_scalar(modT[:, KT:2 * KT, :], modT[:, KT:2 * KT, :], 1.0, None, ALU.add).then_inc(mod_ready, 1)
            dve.wait_ge(mod_ready, 1)

            def h_lo(k):
                dve.wait_ge(h_hi_ready, k + 1)
                nc.vector.tensor_tensor(hT_lo[:, k, :], xmod[:, k % 2, :], hT_hi[:, k, :].bitcast(F32),
                                        ALU.subtract).then_inc(h_lo_ready, 1)

            for k in range(KT + 1):
                if k < KT:
                    if k >= 2:
                        dve.wait_ge(h_lo_ready, k - 1)
                    nc.vector.tensor_scalar(xmod[:, k % 2, CTX:TOK], xT[:, k, CTX:TOK], modT[:, k + KT, 0:1],
                                            modT[:, k, 0:1], ALU.mult, ALU.add).then_inc(xmod_ready, 1)
                if k:
                    h_lo(k - 1)
            lo_part(dve, Q0)
            own = Chain(dve, dve_own)
            norm = Chain(dve, norm_own)

            def chunks(n0, n1, first=0, then=None):
                with dve.Fori(first, (n1 - n0) // 4) as i:
                    for s in range(4):
                        lo_part(dve, n0 + s + 1, i)
                        if then and s % 2:
                            then(i, s // 2)

            def convolve(i, e):
                dve.wait_ge(half_done, 4 * i + U0 + 2 * e + 2)
                if not isinstance(i, int):
                    dve.wait_ge(silu_ready, 2 * i + e - 1)
                own.at(2 * (2 * i + e))
                parts = [(ps[:, 3 - e, 0:CTX], conv[:, e, 0:CTX], CTX), (ps[:, 1 - e, :], conv[:, e, CTX:TOK], LAT)]

                def w(j):
                    return vecs[:, bass.ds(2 * i + (V_MLW + 8 * j + e), 1)]

                for src, dst, n in parts:
                    last = nc.vector.tensor_scalar(dst, src, w(1), vecs[:, bass.ds(2 * i + (V_MLB + e), 1)],
                                                   ALU.mult, ALU.add)
                own.after(last)
                for src, dst, n in parts:
                    last = nc.vector.scalar_tensor_tensor(dst[:, 1:n], src[:, 0:n - 1], w(0), dst[:, 1:n],
                                                          ALU.mult, ALU.add)
                own.after(last)
                for src, dst, n in parts:
                    last = nc.vector.scalar_tensor_tensor(dst[:, 0:n - 1], src[:, 1:n], w(2), dst[:, 0:n - 1],
                                                          ALU.mult, ALU.add)
                last.then_inc(conv_ready, 1)

            chunks(Q0, KV0)
            chunks(KV0, U0)
            for s in range(4):
                lo_part(dve, U0 + s + 1)
                if s % 2:
                    convolve(0, s // 2)
            chunks(U0, O0, 1, convolve)
            chunks(O0, V0)
            for n in range(V0, N - 1):
                lo_part(dve, n + 1)
                if n in (V0 + 4, V0 + 7):
                    r, z, nk, v, cols = [(0, zq, QK, V_GQ, slice(0, LAT)), (1, zkv, KVK, V_GKV, slice(LAT, LAT + TOK))][n == V0 + 7]
                    dve.wait_ge(root_ready, r + 1)
                    norm.after(nc.vector.reciprocal(rms[:, cols], rms[:, cols]))
                    for k in range(nk):
                        last = nc.vector.scalar_tensor_tensor(z[:, k, :], z[:, k, :], vecs[:, v + k:v + k + 1],
                                                              rms[:, cols], ALU.mult, ALU.mult)
                    last.then_inc(normed, 1)

        @block.tensor
        def _(pe):
            pe.wait_ge(silu_done, 1)
            nc.tensor.transpose(ps[:, 7, 0:32], ccrow[:], ident[0:32, 0:32]).then_inc(turned, 1)
            for b in range(3):
                nc.tensor.transpose(ps[:, 6, b * P:(b + 1) * P], vrows[:, b, :], ident[:])
            nc.tensor.transpose(ps[:, 6, 3 * P:V_ALL], vrows[0:V_ALL - 3 * P, 3, :],
                                ident[0:V_ALL - 3 * P, 0:V_ALL - 3 * P]).then_inc(turned, 1)
            pe.wait_ge(turned_kept, 1)
            for j in range(NJ):
                if j >= 2:
                    pe.wait_ge(rows_kept, j - 1)
                for s in range(4):
                    pe.wait_ge(w_in[s], 16 * (j + 1))
                    for k in range(4):
                        kt = 4 * s + k
                        mm = nc.tensor.matmul(ps[0:2, j % 2, :], cT[:, kt:kt + KT + 1:KT], wada[:, s, k, :],
                                              start=(kt == 0), stop=(kt == KT - 1))
                    mm.then_inc(w_used, 1)
                if 2 <= j:
                    b = j - 2
                    pe.wait_ge(x_in[b], 16)
                    for q in range(4):
                        if b:
                            pe.wait_ge(x_kept, 4 * (b - 1) + q + 1)
                        for k in range(4):
                            mm = nc.tensor.transpose(ps[:, 2 + q, k * P:(k + 1) * P],
                                                     xnat[:, b, (4 * q + k) * P:(4 * q + k + 1) * P], ident[:])
                        mm.then_inc(x_turned, 1)
            pe.wait_ge(rows_kept, NJ)
            for n in range(32):
                mm = nc.tensor.transpose(ps[:, 7, 2 * n:2 * n + 2], mrows[:, n // 4, (n % 4) * P:(n % 4 + 1) * P], ident[0:2, 0:2])
            mm.then_inc(mod_turned, 1)
            pe.wait_ge(x_kept, 4 * TB)

            def chunk(n, it, lat, ctx, w_step=None):
                for half in range(2):
                    pe.wait_ge(lo_ready, 4 * it + n + half + 1)
                    for k in range(8):
                        kt = 8 * half + k
                        if isinstance(it, int) and n == 0:
                            pe.wait_ge(h_lo_ready, kt + 1)
                        for p, (w, h) in enumerate([(w_hi, hT_hi), (w_hi, hT_lo), (w_lo, hT_hi)]):
                            first, last = kt == 0 and p == 0, kt == KT - 1 and p == 2
                            lhs = w[:, (n + half) % 2, k * P:(k + 1) * P]
                            if ctx is not None:
                                nc.tensor.matmul(ps[:, ctx, 0:CTX], lhs, h[:, kt, 0:CTX], start=first, stop=last)
                            mm = nc.tensor.matmul(ps[:, lat, :], lhs, h[:, kt, CTX:TOK], start=first, stop=last)
                    mm.then_inc(half_done, 1)

            chunk(0, 0, 0, 2)
            for x in range(QK):
                if x:
                    pe.wait_ge(psum_kept, x)
                chunk(Q0 + 2 * x, 0, 1 - x % 2, None)
            for e in range(2):
                pe.wait_ge(psum_kept, QK + e)
                chunk(KV0 + 2 * e, 0, 1 - e, 3 - e)
            X0 = 1 + QK + KVK
            for n0, kept, before in [(U0, conv_ready, (psum_kept, X0)), (O0, o_ready, (conv_ready, UK))]:
                ctx = 3 if n0 == U0 else None
                for e in range(2):
                    pe.wait_ge(before[0], before[1] - 1 + e)
                    chunk(n0 + 2 * e, 0, 1 - e, ctx and ctx - e)
                with pe.Fori(1, UK // 2) as i:
                    for e in range(2):
                        pe.wait_ge(kept, 2 * i + e - 1)
                        chunk(n0 + 2 * e, i, 1 - e, ctx and ctx - e)
            for c in range(2):
                for s in range(8):
                    n = V0 + 8 * c + s
                    if (c, s) == (0, 3):
                        pe.wait_ge(sq_ready, 1)
                        for k in range(QK):
                            mm = nc.tensor.matmul(ps[:, 0, :], ones[:], sq[:, k, 0:LAT], start=(k == 0), stop=(k == QK - 1))
                        mm.then_inc(sum_ready, 1)
                    elif (c, s) == (0, 6):
                        pe.wait_ge(sq_ready, 2)
                        pe.wait_ge(root_ready, 1)
                        for k in range(KVK):
                            nc.tensor.matmul(ps[:, 0, :], ones[:], sq[:, k, 0:512], start=(k == 0), stop=(k == KVK - 1))
                            mm = nc.tensor.matmul(ps[:, 1, 0:TOK - 512], ones[:], sq[:, k, 512:TOK], start=(k == 0),
                                                  stop=(k == KVK - 1))
                        mm.then_inc(sum_ready, 1)
                    pe.wait_ge(lo_ready, n + 1)
                    for k in range(2):
                        kt = 2 * s + k
                        for t in range(TB):
                            if c and kt == 0:
                                pe.wait_ge(v_ready, t + 1)
                            for p, (w, h) in enumerate([(w_hi, hT_hi), (w_hi, hT_lo), (w_lo, hT_hi)]):
                                mm = nc.tensor.matmul(ps[:, 2 + t, :], h[:, kt, t * P:(t + 1) * P],
                                                      w[:, n % 2, k * 512:(k + 1) * 512],
                                                      start=(kt == 0 and p == 0), stop=(kt == KT - 1 and p == 2))
                    mm.then_inc(half_done, 1)


ADA_COLS = 1024


def sum_ada(nc, io, sb, sem, pool, parts):
    cT = sb["cT"]
    tag = f"ada{parts[0]}"

    def at(name, shape, kb):
        return nc.alloc_sbuf_tensor_at(f"{tag}_{name}", shape, F32, offset=SB0 + int(kb * KB))

    w = at("w", [P, 4, ADA_COLS], 179)
    acc = at("acc", [P, ADA_COLS], 195)
    w_in, sent = sb["ada_in"], sb["ada_sent"]
    own_sem = sem(f"{tag}_own")
    wv = io["w_ada"][0].rearrange("(k p) m -> p k m", p=P)

    def fetch(part, k):
        c0 = 2 * D + part * ADA_COLS
        pool.dma_start(w[:, k % 4, :], wv[:, k, c0:c0 + ADA_COLS] if isinstance(part, int) else
                       wv[:, k, bass.ds(c0, ADA_COLS)]).then_inc(w_in[k % 4], 16)

    def product(part, k):
        pool.wait_ge(w_in[k % 4], 64 * part + 16 * (k // 4 + 1))
        out = acc[:] if k == 0 else w[:, k % 4, :]
        nc.gpsimd.tensor_tensor(out, w[:, k % 4, :], cT[:, k:k + 1].to_broadcast([P, ADA_COLS]), ALU.mult)\
          .then_inc(own_sem, 1)

    def one_part(part, i):
        own = (2 * KT - 1) * i
        for k in range(4):
            fetch(part, k)
        if not isinstance(part, int) or part:
            pool.wait_ge(sent, 16 * part)
        product(part, 0)
        for k in range(KT):
            if k + 1 < KT:
                product(part, k + 1)
            pool.wait_ge(own_sem, own + max(2 * k, 1))
            if k:
                nc.gpsimd.tensor_tensor(acc[:], acc[:], w[:, k % 4, :], ALU.add).then_inc(own_sem, 1)
            if k and k + 3 < KT:
                fetch(part, k + 3)
        pool.wait_ge(own_sem, own + 2 * KT - 1)
        pool.dma_start(io["scratch"]["ada"][bass.ds(part, 1)].rearrange("a p m -> p a m"), acc[:]).then_inc(sent, 16)

    one_part(parts[0], 0)
    if len(parts) > 1:
        with pool.Fori(1, len(parts)) as i:
            one_part(i + parts[0], i)
    pool.wait_ge(sent, 16 * (parts[-1] + 1))


class GateRows:

    def __init__(self, nc):
        def at(name, shape, kb):
            return nc.alloc_sbuf_tensor_at(name, shape, F32, offset=SB0 + int(kb * KB))

        H = ML_HEADS
        self.arow = at("gr_arow", [H, 2, TOK], 38)
        self.mrow = at("gr_mrow", [H, 2, LAT], 44)
        self.erow = at("gr_erow", [H, 2, LAT], 48)
        self.gate = at("gr_gate", [H, 4, TOK], 136)
        self.soft = at("gr_soft", [H, 2, TOK], 30)
        self.runs = at("gr_runs", [H, 2, TOK], 73)
        self.init = at("gr_init", [H, 2, 2], 52)
        self.bias = at("gr_bias", [H, 4], 52.25)
        self.f = self.gate[:].rearrange("h (d g) t -> h g d t", g=2)[:, 1]


def gate_scans(nc, dve, own, rows, step, arow_ready, erow_ready):
    gate, soft, runs, arow, mrow, erow, init = rows.gate, rows.soft, rows.runs, rows.arow, rows.mrow, rows.erow, rows.init
    ctx, lat = slice(0, CTX), slice(CTX, TOK)

    def back(x):
        return x[:, ::-1]

    order = [(back, lambda x: x), (lambda x: x, back)]
    if step == 0:
        own.after(nc.vector.scalar_tensor_tensor(rows.f, rows.f, 0.0, soft[:], ALU.min, ALU.subtract))
        for d in range(2):
            for part, turn in zip((ctx, lat), order[d]):
                x = turn(gate[:, 2 * d + 1, part])
                last = nc.vector.tensor_tensor_scan(turn(runs[:, d, part]), x, x, 0.0, ALU.add, ALU.bypass)
        own.after(last)
    elif step == 1:
        for d in range(2):
            i_row = gate[:, 2 * d, :]
            nc.vector.tensor_tensor(arow[:, d, lat], i_row[:, lat], runs[:, d, lat], ALU.subtract)
            if d == 0:
                nc.vector.tensor_tensor(arow[:, d, 0:CTX - 1], i_row[:, 0:CTX - 1], runs[:, d, 1:CTX], ALU.add)
                last = nc.vector.tensor_copy(arow[:, d, CTX - 1:CTX], i_row[:, CTX - 1:CTX])
            else:
                nc.vector.tensor_tensor(arow[:, d, 1:CTX], i_row[:, 1:CTX], runs[:, d, 0:CTX - 1], ALU.add)
                last = nc.vector.tensor_copy(arow[:, d, 0:1], i_row[:, 0:1])
        last.then_inc(arow_ready, 1)
        dve.wait_ge(arow_ready, 1)
        own.after(nc.vector.tensor_reduce(init[:, :, 0:1], arow[:, :, ctx], AX.X, ALU.max))
        for d, t in [(0, 0), (1, CTX - 1)]:
            last = nc.vector.tensor_tensor(init[:, d, 1:2], init[:, d, 0:1], runs[:, d, t:t + 1], ALU.max)
        own.after(last)
    else:
        for d in range(2):
            turn = order[d][1]
            x = turn(arow[:, d, lat])
            last = nc.vector.tensor_tensor_scan(turn(mrow[:, d, :]), x, x, init[:, d, 1:2], ALU.max, ALU.max)
        own.after(last)
        own.after(nc.vector.tensor_tensor(erow[:], mrow[:], runs[:, :, lat], ALU.add))
        nc.vector.tensor_scalar(erow[:], erow[:], -1.0, EXP_MAX, ALU.mult, ALU.min)
        nc.vector.tensor_scalar(mrow[:], mrow[:], -1.0, None, ALU.mult).then_inc(erow_ready, 1)


class FirstLoadsD:

    def __init__(self, nc, stack):
        self.uh = nc.alloc_sbuf_tensor_at("d_uh", [P, 2, 2, TOK], F32, offset=SB0 + 54 * KB)
        self.wm = nc.alloc_sbuf_tensor_at("d_wm", [P, 2, 2, 2, P], F32, offset=SB0 + 79 * KB)
        self.sel = nc.alloc_sbuf_tensor_at("d_sel", [ML_HEADS, ML_HEADS * P], F32, offset=SB0 + 52 * KB)
        self.const_in = stack.enter_context(nc.semaphore("d_const_in"))
        self.qk_in = [stack.enter_context(nc.semaphore(f"d_qk_in{s}")) for s in range(2)]

    def fetch(self, sp, io, h):
        s = h % 2
        u_v = io["scratch"]["u"].rearrange("c p t -> p c t")
        sp.dma_start(self.uh[:, s], u_v[:, 2 * h:2 * h + 2, :]).then_inc(self.qk_in[s], 16)
        for q, w in enumerate([io["w_mq"], io["w_mk"]]):
            sp.dma_start(self.wm[:, s, q], w[0, h].rearrange("(k p) m -> p k m", p=P)).then_inc(self.qk_in[s], 16)
        if h == 0:
            sp.dma_start(self.sel[:], io["consts"][0:ML_HEADS, C_SEL:C_SEL + ML_HEADS * P]).then_inc(self.const_in, 16)


def matrix_memory(nc, io, sb, sem, psum):
    vecs, ident = sb["vecs"], sb["ident"]
    ps = psum["all"]
    yT, rows = sb["yT"], sb["rows"]
    scratch = io["scratch"]

    def at(name, shape, kb):
        return nc.alloc_sbuf_tensor_at(name, shape, F32, offset=SB0 + int(kb * KB))

    H = ML_HEADS
    arow, mrow, erow = rows.arow, rows.mrow, rows.erow
    mask = at("d_mask", [P, 2, P], 21)
    negmb = at("d_negmb", [P, H, 2, LAT], 5)
    cols = at("d_cols", [P, 2, TB + LB, H], 207)
    first_d = sb["first_d"]
    sel, uh, wm, const_in, qk_in = first_d.sel, first_d.uh, first_d.wm, first_d.const_in, first_d.qk_in
    v1 = at("d_v1", [P, 2, TB, ML_V + 1], 66)
    qT = at("d_qT", [P, LAT], 83)
    kT = at("d_kT", [P, TOK], 85)
    sT = at("d_sT", [P, 2, TB, LAT], 136)
    decay = at("d_decay", [P, 2, TB, LAT], 112)
    probT = at("d_probT", [P, 2, TB, LAT], 88)
    hid = at("d_hid", [P, 2, LB, ML_V], 160)
    sig_o = at("d_sig_o", [P, 2, 2, LAT], 168)
    small = at("d_small", [P, 2, LB], 176)
    stats = at("d_stats", [P, LB, 6], 176.25)
    mv = at("d_mv", [P, 2, LB, 2], 176.5)
    rstd = at("d_rstd", [P, 2, LB], 176.75)

    mask_in = sem("d_mask_in")
    v_in = [sem(f"d_v_in{s}") for s in range(2)]
    o_in = [sem(f"d_o_in{s}") for s in range(2)]
    ones_ready = sem("d_ones_ready")
    cols_turned = sem("d_cols_turned")
    cols_ready = sem("d_cols_ready")
    spread = sem("d_spread")
    spread_kept = sem("d_spread_kept")
    qk_done = sem("d_qk_done")
    qk_kept = sem("d_qk_kept")
    s_done = sem("d_s_done")
    s_kept = sem("d_s_kept")
    expo_ready = sem("d_expo_ready")
    decay_ready = sem("d_decay_ready")
    prob_ready = sem("d_prob_ready")
    num_done = sem("d_num_done")
    num_kept = sem("d_num_kept")
    var_ready = sem("d_var_ready")
    root_ready = sem("d_root_ready")
    normed = sem("d_normed")
    y_turned = sem("d_y_turned")
    y_kept = sem("d_y_kept")
    dve_own = sem("d_dve_own")
    ada_in = sem("d_ada_in")
    ada_summed = sem("d_ada_summed")
    ada = at("d_ada", [P, 4, ADA_COLS], 5)
    modR, ones = sb["modR"], sb["ones"]

    S_BANK = [3, 0, 2, 1, 3, 0]
    SPREAD_BANK = [6, 7, 6, 7, 4, 5, 6, 7]

    def span(d, j):
        return (j * P, LAT) if d == 0 else (0, (j + 1) * P)

    block = nc.Block()
    with block as block:
        @block.sync
        def _(sp):
            v_v = scratch["v"].rearrange("t p m -> p t m")
            o_v = scratch["o"].rearrange("c p t -> p c t")

            def fetch_v(h):
                sp.dma_start(v1[:, h % 2, :, 0:ML_V], v_v[:, :, h * ML_V:(h + 1) * ML_V]).then_inc(v_in[h % 2], 16)

            def fetch_o(h):
                sp.dma_start(sig_o[:, h % 2], o_v[:, 2 * h:2 * h + 2, :]).then_inc(o_in[h % 2], 16)

            first_d.fetch(sp, io, 1)
            sp.dma_start(mask[:].rearrange("p a b -> p (a b)"), io["consts"][:, C_MASKF:C_MASKF + 2 * P]).then_inc(mask_in, 16)
            for e in range(4):
                sp.wait_ge(sb["v_sent"][e], 16 * 2 * TB // 4)
            for h in range(2):
                fetch_v(h)
            for h in range(2):
                fetch_o(h)
            for h in range(2, H):
                sp.wait_ge(qk_done, 3 * (h - 1))
                first_d.fetch(sp, io, h)
            for h in range(2, H):
                sp.wait_ge(num_done, 2 * LB * (h - 1))
                fetch_v(h)
            for h in range(2, H):
                sp.wait_ge(y_kept, 2 * (h - 1))
                fetch_o(h)
            sp.wait_ge(prob_ready, 2 * H)
            sb["first_e"].fetch_first(sp, io)
            sp.dma_start(ada[:], scratch["ada"][0:4].rearrange("a p m -> p a m")).then_inc(ada_in, 16)

        @block.gpsimd
        def _(pool):
            sem.clear_last(pool)
            nc.gpsimd.memset(v1[:, :, :, ML_V:ML_V + 1], 1.0).then_inc(ones_ready, 1)
            sum_ada(nc, io, sb, sem, pool, range(7, 8))

        @block.scalar
        def _(act):
            def keep_spread(n):
                act.wait_ge(spread, n + 1)
                nc.scalar.activation(negmb[:, n // 2, n % 2, :], ps[:, SPREAD_BANK[n], :], ACT.Copy).then_inc(spread_kept, 1)

            def keep_front(h):
                act.wait_ge(qk_done, 3 * h + 1)
                nc.scalar.activation(kT[:, 0:CTX], ps[:, 2, 0:CTX], ACT.Copy)
                act.wait_ge(qk_done, 3 * h + 2)
                nc.scalar.activation(qT[:], ps[:, 0, :], ACT.Copy, scale=ML_SCALE).then_inc(qk_kept, 1)
                act.wait_ge(qk_done, 3 * h + 3)
                nc.scalar.activation(kT[:, CTX:TOK], ps[:, 1, :], ACT.Copy).then_inc(qk_kept, 1)
                for b in range(TB):
                    act.wait_ge(s_done, TB * h + b + 1)
                    if b == 0 and h >= 2:
                        act.wait_ge(prob_ready, 2 * (h - 1))
                    nc.scalar.activation(sT[:, h % 2, b, :], ps[:, S_BANK[b], :], ACT.Copy).then_inc(s_kept, 1)

            def make_decay(h):
                for d in range(2):
                    act.wait_ge(expo_ready, 2 * h + d + 1)
                    nc.scalar.activation(decay[:, d, 0:CB, :], decay[:, d, 0:CB, :], ACT.Exp)
                    for j in range(LB):
                        a, c = span(d, j)
                        last = nc.scalar.activation(decay[:, d, CB + j, a:c], decay[:, d, CB + j, a:c], ACT.Exp)
                    last.then_inc(decay_ready, 1)

            def root(h):
                act.wait_ge(var_ready, h + 1)
                nc.scalar.activation(rstd[:, h % 2, :], mv[:, h % 2, :, 1], ACT.Sqrt, bias=sb["eps"][:]).then_inc(root_ready, 1)

            for n in range(2):
                keep_spread(n)
            keep_front(0)
            make_decay(0)
            for n in range(2, 6):
                keep_spread(n)
            for h in range(1, H + 2):
                if h < H:
                    keep_front(h)
                if h == 1:
                    for n in range(6, 2 * H):
                        keep_spread(n)
                if h >= 2:
                    root(h - 2)
                if h < H:
                    make_decay(h)

        @block.vector
        def _(dve):
            own = Chain(dve, dve_own)

            def exponents(h):
                dve.wait_ge(spread_kept, 2 * (h + 1))
                if h:
                    dve.wait_ge(prob_ready, 2 * h)
                for d in range(2):
                    for b in range(TB):
                        a, c = (0, LAT) if b < CB else span(d, b - CB)
                        last = nc.vector.tensor_scalar(decay[:, d, b, a:c], negmb[:, h, d, a:c], cols[:, d, b, h:h + 1],
                                                       0.0, ALU.add, ALU.min)
                    last.then_inc(expo_ready, 1)

            def weights(h, d, step):
                if step == 0:
                    dve.wait_ge(decay_ready, 2 * h + d + 1)
                    dve.wait_ge(s_kept, TB * (h + 1))
                    if h:
                        dve.wait_ge(num_done, 2 * LB * (h - 1) + LB * (d + 1))
                    nc.vector.tensor_tensor(probT[:, d, 0:CB, :], decay[:, d, 0:CB, :], sT[:, h % 2, 0:CB, :], ALU.mult)
                elif step == 1:
                    for j in range(LB):
                        a, c = span(d, j)
                        last = nc.vector.tensor_tensor(probT[:, d, CB + j, a:c], decay[:, d, CB + j, a:c],
                                                       sT[:, h % 2, CB + j, a:c], ALU.mult)
                    own.after(last)
                elif step == 2:
                    for j in range(LB):
                        x = probT[:, d, CB + j, j * P:(j + 1) * P]
                        last = nc.vector.tensor_tensor(x, x, mask[:, d, :], ALU.mult)
                    last.then_inc(prob_ready, 1)

            def divide(h, d, t):
                if (d, t) == (0, 0) and h >= 2:
                    dve.wait_ge(y_turned, 2 * (h - 1))
                src = ps[:, 4 + t % 2, :]
                dve.wait_ge(num_done, 2 * LB * h + LB * d + t + 1)
                x, inv = small[:, 0, t:t + 1], small[:, 1, t:t + 1]
                own.after(nc.vector.tensor_scalar(x, src[:, ML_V:ML_V + 1], -1.0, cols[:, d, TB + t, h:h + 1],
                                                  ALU.mult, ALU.max))
                own.after(nc.vector.tensor_tensor(x, x, src[:, ML_V:ML_V + 1], ALU.max))
                own.after(nc.vector.reciprocal(inv, x))
                out = hid[:, h % 2, t, :]
                if d == 0:
                    nc.vector.tensor_scalar(out, src[:, 0:ML_V], inv, None, ALU.mult).then_inc(num_kept, 1)
                else:
                    nc.vector.scalar_tensor_tensor(out, src[:, 0:ML_V], inv, out, ALU.mult, ALU.add).then_inc(num_kept, 1)
                    dve.wait_ge(num_kept, 2 * LB * h + LB + t + 1)
                    own.after(nc.vector.bn_stats(stats[:, t, :], out))
                    last = nc.vector.bn_aggr(mv[:, h % 2, t, :], stats[:, t, :])
                    if t == LB - 1:
                        last.then_inc(var_ready, 1)

            def norm(h):
                dve.wait_ge(root_ready, h + 1)
                own.after(nc.vector.reciprocal(rstd[:, h % 2, :], rstd[:, h % 2, :]))
                for t in range(LB):
                    last = nc.vector.tensor_scalar(hid[:, h % 2, t, :], hid[:, h % 2, t, :], mv[:, h % 2, t, 0:1],
                                                   rstd[:, h % 2, t:t + 1], ALU.subtract, ALU.mult)
                last.then_inc(normed, 1)

            def gate_out(h):
                dve.wait_ge(o_in[h % 2], 16 * (h // 2 + 1))
                for e in range(2):
                    c = 2 * h + e
                    dve.wait_ge(y_turned, c + 1)
                    nc.vector.scalar_tensor_tensor(yT[:, UK + c, :], ps[:, 6 + e, :], vecs[:, V_GHN + c:V_GHN + c + 1],
                                                   sig_o[:, h % 2, e, :], ALU.mult, ALU.mult).then_inc(y_kept, 1)

            dve.wait_ge(cols_turned, 1)
            nc.vector.tensor_copy(cols[:].rearrange("p a b c -> p (a b c)"), ps[:, 5, 0:2 * (TB + LB) * H]).then_inc(cols_ready, 1)
            dve.wait_ge(cols_ready, 1)
            exponents(0)
            dve.wait_ge(mask_in, 16)
            for d in range(2):
                for step in range(3):
                    weights(0, d, step)
            for h in range(1, H + 2):
                if h < H:
                    exponents(h)
                if h <= H:
                    for t in range(LB):
                        divide(h - 1, 0, t)
                if h >= 2:
                    norm(h - 2)
                if h <= H:
                    for t in range(LB):
                        divide(h - 1, 1, t)
                        if h < H:
                            weights(h, 0, t)
                if h < H:
                    for step in range(3):
                        weights(h, 1, step)
                if h >= 2:
                    gate_out(h - 2)
            dve.wait_ge(ada_summed, 1)
            nc.vector.tensor_tensor(modR[:, 0:2 * KT], ps[:, 3, 0:2 * KT], vecs[:, V_ADA + 2 * KT:V_ADA + 4 * KT], ALU.add)

        @block.tensor
        def _(pe):
            def spread_row(n):
                h, d = divmod(n, 2)
                if n in (2, 3):
                    pe.wait_ge(spread_kept, n - 1)
                elif n == 5:
                    pe.wait_ge(cols_ready, 1)
                elif n >= 6:
                    pe.wait_ge(spread_kept, n - 3)
                nc.tensor.matmul(ps[:, SPREAD_BANK[n], :], sel[:, h * P:(h + 1) * P], mrow[:, d, :], start=True,
                                 stop=True).then_inc(spread, 1)

            def front(h):
                pe.wait_ge(qk_in[h % 2], 48 * (h // 2 + 1))
                if h:
                    pe.wait_ge(s_kept, TB * h)
                for q, bank, a, b in [(1, 2, 0, CTX), (0, 0, CTX, TOK), (1, 1, CTX, TOK)]:
                    for k in range(2):
                        mm = nc.tensor.matmul(ps[:, bank, 0:b - a], wm[:, h % 2, q, k, :], uh[:, h % 2, k, a:b],
                                              start=(k == 0), stop=(k == 1))
                    mm.then_inc(qk_done, 1)
                for b in range(TB):
                    if b in (0, 2):
                        pe.wait_ge(qk_kept, 2 * h + 1 + b // 2)
                    if b >= 4:
                        pe.wait_ge(s_kept, TB * h + b - 3)
                    nc.tensor.matmul(ps[:, S_BANK[b], :], kT[:, b * P:(b + 1) * P], qT[:], start=True,
                                     stop=True).then_inc(s_done, 1)

            def back(h):
                pe.wait_ge(v_in[h % 2], 16 * (h // 2 + 1))
                for d in range(2):
                    pe.wait_ge(prob_ready, 2 * h + d + 1)
                    for t in range(LB):
                        n = 2 * LB * h + LB * d + t
                        if n >= 2:
                            pe.wait_ge(num_kept, n - 1)
                        seen = list(range(CB)) + [CB + j for j in range(LB) if (j <= t if d == 0 else j >= t)]
                        for b in seen:
                            mm = nc.tensor.matmul(ps[:, 4 + t % 2, 0:ML_V + 1], probT[:, d, b, t * P:(t + 1) * P],
                                                  v1[:, h % 2, b, :], start=(b == seen[0]), stop=(b == seen[-1]))
                        mm.then_inc(num_done, 1)

            def turn(h):
                pe.wait_ge(normed, h + 1)
                for e in range(2):
                    if h:
                        pe.wait_ge(y_kept, 2 * h + e - 1)
                    for t in range(LB):
                        mm = nc.tensor.transpose(ps[:, 6 + e, t * P:(t + 1) * P], hid[:, h % 2, t, e * P:(e + 1) * P], ident[:])
                    mm.then_inc(y_turned, 1)

            for d in range(2):
                for b in range(TB + LB):
                    src = arow[:, d, b * P:(b + 1) * P] if b < TB else erow[:, d, (b - TB) * P:(b - TB + 1) * P]
                    c0 = (d * (TB + LB) + b) * H
                    mm = nc.tensor.transpose(ps[:, 5, c0:c0 + H], src, ident[0:H, 0:H])
            mm.then_inc(cols_turned, 1)
            pe.wait_ge(const_in, 16)
            for n in range(2):
                spread_row(n)
            front(0)
            for n in range(2, 6):
                spread_row(n)
            for h in range(1, H + 2):
                if h < H:
                    front(h)
                if h == 1:
                    for n in range(6, 2 * H):
                        spread_row(n)
                    pe.wait_ge(ones_ready, 1)
                    pe.wait_ge(spread_kept, 6)
                if h == 2:
                    pe.wait_ge(spread_kept, 2 * H)
                if h <= H:
                    back(h - 1)
                if h >= 2:
                    turn(h - 2)
                if h == H:
                    pe.wait_ge(ada_in, 16)
                    for c in range(2 * KT):
                        mm = nc.tensor.matmul(ps[:, 3, c:c + 1], ada[:, c // 8, c % 8 * P:(c % 8 + 1) * P], ones[:, 0:1],
                                              start=True, stop=True)
                    mm.then_inc(ada_summed, 1)


class FirstLoadsC:

    def __init__(self, nc, stack):
        def at(name, shape, kb):
            return nc.alloc_sbuf_tensor_at(name, shape, F32, offset=SB0 + int(kb * KB))

        self.wq = [at(f"c_wq{s}", [P, QK, 2 * QD], kb) for s, kb in enumerate((150, 54))]
        self.wkv = [at(f"c_wkv{s}", [P, KVK, 4 * P], kb) for s, kb in enumerate((156, 60))]
        self.cst = at("c_cst", [P, C_MASKF], 173)
        self.cst_in = stack.enter_context(nc.semaphore("c_cst_in"))
        self.w_in = [stack.enter_context(nc.semaphore(f"c_w_in{s}")) for s in range(2)]

    def fetch(self, sp, io, pair, s):
        uq = io["w_uq"][0].rearrange("(k p) m -> p k m", p=P)
        ukv = io["w_ukv"][0].rearrange("(k p) m -> p k m", p=P)
        for e in range(2):
            c0 = pair * 2 * QD + e * QD
            sp.dma_start(self.wq[s][:, :, e * NOPE:(e + 1) * NOPE], uq[:, :, bass.ds(c0, NOPE)]).then_inc(self.w_in[s], 16)
            sp.dma_start(self.wq[s][:, :, 2 * NOPE + e * ROPE:2 * NOPE + (e + 1) * ROPE],
                         uq[:, :, bass.ds(c0 + NOPE, ROPE)]).then_inc(self.w_in[s], 16)
        sp.dma_start(self.wkv[s][:], ukv[:, :, bass.ds(pair * 4 * P, 4 * P)]).then_inc(self.w_in[s], 16)

    def fetch_first(self, sp, io):
        sp.dma_start(self.cst[:], io["consts"][:, 0:C_MASKF]).then_inc(self.cst_in, 16)
        self.fetch(sp, io, 0, 0)


def attention(nc, io, sb, sem, psum):
    vecs, ident = sb["vecs"], sb["ident"]
    ps = psum["all"]
    zq, zkv, krg, yT, rows = sb["zq"], sb["zkv"], sb["krg"], sb["yT"], sb["rows"]
    first_c = sb["first_c"]
    wq, wkv, cst = first_c.wq, first_c.wkv, first_c.cst

    def at(name, shape, kb):
        return nc.alloc_sbuf_tensor_at(name, shape, F32, offset=SB0 + int(kb * KB))

    kr2 = at("c_kr2", [P, TOK], 70)
    qn = [at(f"c_qn{s}", [P, 2, LAT], kb) for s, kb in enumerate((83, 64))]
    qr = [at(f"c_qr{s}", [P, LAT], kb) for s, kb in enumerate((87, 68))]
    qr_raw = at("c_qr_raw", [P, LAT], 89)
    rot = at("c_rot", [P, LAT], 91)
    kn = [at(f"c_kn{s}", [P, 2, TOK], kb) for s, kb in enumerate((93, 160))]
    vv = [at(f"c_v{s}", [P, TB, 2 * VD], kb) for s, kb in enumerate((99, 166))]
    prob = at("c_prob", [P, 2, TOK], 106)
    probT = at("c_probT", [P, 2, TB, LAT], 112)
    stat = at("c_stat", [P, 4, 2 * LB * 2], 148)

    cst_in, w_in = first_c.cst_in, first_c.w_in
    kr_turned = sem("c_kr_turned")
    kr_ready = sem("c_kr_ready")
    piece_done = sem("c_piece_done")
    piece_kept = sem("c_piece_kept")
    qr_ready = sem("c_qr_ready")
    scores_done = sem("c_scores_done")
    negmax_ready = sem("c_negmax_ready")
    exp_ready = sem("c_exp_ready")
    prob_ready = sem("c_prob_ready")
    turned = sem("c_turned")
    turned_kept = sem("c_turned_kept")
    dve_own = sem("c_dve_own")
    gate_in = sem("c_gate_in")
    biased = sem("c_biased")
    soft_own = sem("c_soft_own")
    soft_ready = sem("c_soft_ready")
    arow_ready = sem("c_arow_ready")
    erow_ready = sem("c_erow_ready")
    gate_own = sem("c_gate_own")

    PAIRS = HEADS // 2
    U = 2 * LB
    PROJECT = [("q", 0), ("q", 1), ("q", 2), ("swap", 0), ("k", 0), ("k", 1), ("k", 2), ("k", 3), ("v", 0), ("v", 1), ("v", 2)]
    BEHIND = {0: PROJECT[0:1], 2: PROJECT[1:2], 3: PROJECT[2:4], 4: PROJECT[4:6], 6: PROJECT[6:9], 7: PROJECT[9:11]}

    def pieces(pair, u):
        if u == 1:
            return [("out", 1, pair - 1)] if pair else []
        if u == 5:
            return [("out", 0, pair)]
        return [(kind, n, pair + 1) for kind, n in BEHIND[u]] if pair + 1 < PAIRS else []

    PIECES = [(kind, n, 0) for kind, n in PROJECT] + [x for pair in range(PAIRS) for u in range(U) for x in pieces(pair, u)]
    PIECES.append(("out", 1, PAIRS - 1))

    def count(kind, n, pair):
        return PIECES.index((kind, n, pair)) + 1

    def bank(piece):
        return 6 + PIECES.index(piece) % 2

    def scores(u):
        return ps[:, 2 * (u % 2):2 * (u % 2) + 2, :].rearrange("p a b -> p (a b)")[:, 0:TOK]

    turned_ps = ps[:, 4:6, :].rearrange("p a b -> p (a b)")[:, 0:TOK]

    block = nc.Block()
    with block as block:
        @block.sync
        def _(sp):
            first_c.fetch(sp, io, 1, 1)
            H = ML_HEADS
            for d in range(2):
                for g in range(2):
                    r = 32 * g + H * d
                    sp.dma_start(rows.gate[:, 2 * d + g, :], krg[r:r + H, :]).then_inc(gate_in, 16)
            sp.dma_start(rows.bias[:], io["b_gate"][0].rearrange("(g h) -> h g", h=H),
                         allow_slow_non_contiguous=True).then_inc(gate_in, 16)
            for pair in range(2, PAIRS):
                sp.wait_ge(piece_done, count("v", 2, pair - 2))
                first_c.fetch(sp, io, pair, pair % 2)
            sp.wait_ge(piece_done, count("v", 2, PAIRS - 1))
            sb["first_d"].fetch(sp, io, 0)

        @block.gpsimd
        def _(pool):
            sem.clear_last(pool)
            sum_ada(nc, io, sb, sem, pool, range(5, 7))

        @block.scalar
        def _(act):
            soft = Chain(act, soft_own)

            def keep(piece):
                kind, n, pair = piece
                act.wait_ge(piece_done, count(*piece))
                src, s = ps[:, bank(piece), :], pair % 2
                if kind == "q" and n == 0:
                    if pair:
                        act.wait_ge(qr_ready, pair)
                    dst = qr_raw[:]
                elif kind == "q":
                    dst = qn[s][:, n - 1, :]
                elif kind == "swap":
                    act.wait_ge(kr_ready, 1)
                    dst = rot[:]
                elif kind == "k":
                    cols = slice(0, CTX) if n % 2 == 0 else slice(CTX, TOK)
                    dst, src = kn[s][:, n // 2, cols], src[:, 0:cols.stop - cols.start]
                elif kind == "v":
                    dst, src = vv[s][:, 2 * n:2 * n + 2, :], src.rearrange("p (a b) -> p a b", a=2)
                else:
                    dst = yT[:, 2 * pair + n, :]
                nc.scalar.activation(dst, src, ACT.Copy).then_inc(piece_kept, 1)

            def keep_turned(v):
                act.wait_ge(turned, v + 1)
                e, b = divmod(v % U, LB)
                nc.scalar.activation(probT[:, e, :, b * P:(b + 1) * P], turned_ps.rearrange("p (a b) -> p a b", b=P),
                                     ACT.Copy).then_inc(turned_kept, 1)

            for kind, n in PROJECT:
                keep((kind, n, 0))
            for e in range(4):
                act.wait_ge(sb["v_sent"][e], 16 * 2 * TB // 4)
            for v in range(PAIRS * U):
                pair, u = divmod(v, U)
                act.wait_ge(negmax_ready, v + 1)
                if v >= 2:
                    act.wait_ge(turned, v - 1)
                nc.scalar.activation(prob[:, u % 2, :], scores(u), ACT.Exp, bias=stat[:, 0, u:u + 1],
                                     scale=ATT_SCALE, accum_out=stat[:, 1, u:u + 1]).then_inc(exp_ready, 1)
                for piece in pieces(pair, u):
                    keep(piece)
                if v:
                    keep_turned(v - 1)
                if v == 1:
                    act.wait_ge(biased, 1)
                    soft.after(nc.scalar.activation(rows.soft[:], rows.f, ACT.Abs))
                    soft.after(nc.scalar.activation(rows.soft[:], rows.soft[:], ACT.Exp, scale=-1.0))
                    nc.scalar.activation(rows.soft[:], rows.soft[:], ACT.Ln, bias=1.0).then_inc(soft_ready, 1)
                if v == U - 1:
                    act.wait_ge(erow_ready, 1)
                    nc.scalar.activation(rows.erow[:], rows.erow[:], ACT.Exp)
            keep_turned(PAIRS * U - 1)
            keep(("out", 1, PAIRS - 1))

        @block.vector
        def _(dve):
            own = Chain(dve, dve_own)
            gates = Chain(dve, gate_own)
            dve.wait_ge(kr_turned, 1)
            dve.wait_ge(cst_in, 16)
            nc.vector.tensor_copy(kr2[:, 0:CTX], ps[:, 4, 0:CTX])
            nc.vector.tensor_tensor(kr2[:, CTX:TOK], ps[:, 5, :], cst[:, C_COS:C_COS + LAT], ALU.mult)
            own.after(nc.vector.tensor_tensor(rot[:], ps[:, 3, :], cst[:, C_SIN:C_SIN + LAT], ALU.mult))
            nc.vector.tensor_tensor(kr2[:, CTX:TOK], kr2[:, CTX:TOK], rot[:], ALU.add).then_inc(kr_ready, 1)

            def rotate(pair):
                dve.wait_ge(piece_kept, count("swap", 0, pair))
                if pair >= 2:
                    dve.wait_ge(scores_done, U * (pair - 1))
                nc.vector.tensor_tensor(rot[:], rot[:], cst[:, C_SIN:C_SIN + LAT], ALU.mult)
                own.after(nc.vector.tensor_tensor(qr[pair % 2][:], qr_raw[:], cst[:, C_COS:C_COS + LAT], ALU.mult))
                nc.vector.tensor_tensor(qr[pair % 2][:], qr[pair % 2][:], rot[:], ALU.add).then_inc(qr_ready, 1)

            rotate(0)
            dve.wait_ge(gate_in, 80)
            for g in range(4):
                last = nc.vector.tensor_scalar(rows.gate[:, g, :], rows.gate[:, g, :], rows.bias[:, g:g + 1], None, ALU.add)
            last.then_inc(biased, 1)
            for v in range(PAIRS * U):
                pair, u = divmod(v, U)
                dve.wait_ge(scores_done, v + 1)
                own.after(nc.vector.tensor_reduce(stat[:, 2, u:u + 1], scores(u), AX.X, ALU.max))
                nc.vector.tensor_scalar(stat[:, 0, u:u + 1], stat[:, 2, u:u + 1], -ATT_SCALE, None, ALU.mult)\
                  .then_inc(negmax_ready, 1)
                dve.wait_ge(exp_ready, v + 1)
                own.after(nc.vector.reciprocal(stat[:, 2, U + u:U + u + 1], stat[:, 1, u:u + 1]))
                nc.vector.tensor_scalar(prob[:, u % 2, :], prob[:, u % 2, :], stat[:, 2, U + u:U + u + 1], None,
                                        ALU.mult).then_inc(prob_ready, 1)
                if 2 <= v < 5:
                    if v == 2:
                        dve.wait_ge(soft_ready, 1)
                    gate_scans(nc, dve, gates, rows, v - 2, arow_ready, erow_ready)
                if u == 4 and pair + 1 < PAIRS:
                    rotate(pair + 1)

        @block.tensor
        def _(pe):
            def do_piece(piece):
                kind, n, pair = piece
                number = PIECES.index(piece)
                if number >= 2:
                    pe.wait_ge(piece_kept, number - 1)
                out, s = ps[:, bank(piece), :], pair % 2
                if kind == "q" and n == 0:
                    pe.wait_ge(w_in[s], 80 * (pair // 2 + 1))
                weights = wkv[s][:].rearrange("p k (e m) -> p k e m", m=2 * P)
                if kind == "q":
                    c0 = (2 * NOPE, 0, NOPE)[n]
                    for k in range(QK):
                        mm = nc.tensor.matmul(out, wq[s][:, k, c0:c0 + P], zq[:, k, :], start=(k == 0), stop=(k == QK - 1))
                elif kind == "swap":
                    pe.wait_ge(piece_kept, count("q", 0, pair))
                    mm = nc.tensor.matmul(out, cst[:, C_SWAP:C_SWAP + P], qr_raw[:], start=True, stop=True)
                elif kind == "k":
                    a, b = (0, CTX) if n % 2 == 0 else (CTX, TOK)
                    for k in range(KVK):
                        mm = nc.tensor.matmul(out[:, 0:b - a], weights[:, k, n // 2, 0:NOPE], zkv[:, k, a:b],
                                              start=(k == 0), stop=(k == KVK - 1))
                elif kind == "v":
                    for t in range(2):
                        for k in range(KVK):
                            mm = nc.tensor.matmul(out[:, t * 256:(t + 1) * 256], zkv[:, k, (2 * n + t) * P:(2 * n + t + 1) * P],
                                                  weights[:, k, :, NOPE:2 * P], start=(k == 0), stop=(k == KVK - 1))
                else:
                    pe.wait_ge(turned_kept, U * pair + LB * (n + 1))
                    pe.wait_ge(piece_kept, count("v", 2, pair))
                    for t in range(TB):
                        mm = nc.tensor.matmul(out, vv[s][:, t, n * VD:(n + 1) * VD], probT[:, n, t, :],
                                              start=(t == 0), stop=(t == TB - 1))
                mm.then_inc(piece_done, 1)

            def score(v):
                pair, u = divmod(v, U)
                e, b = divmod(u, LB)
                s = pair % 2
                if u == 0:
                    pe.wait_ge(piece_kept, count("k", 3, pair))
                    pe.wait_ge(qr_ready, pair + 1)
                if v >= 2:
                    pe.wait_ge(exp_ready, v - 1)
                r = slice(e * ROPE, (e + 1) * ROPE)
                out = ps[:, 2 * (u % 2):2 * (u % 2) + 2, :]
                for j, (a, c) in enumerate([(0, 512), (512, TOK)]):
                    nc.tensor.matmul(out[:, j, 0:c - a], qn[s][:, e, b * P:(b + 1) * P], kn[s][:, e, a:c], start=True, stop=False)
                    mm = nc.tensor.matmul(out[:, j, 0:c - a], qr[s][r, b * P:(b + 1) * P], kr2[r, a:c], start=False, stop=True)
                mm.then_inc(scores_done, 1)

            def turn(v):
                pe.wait_ge(prob_ready, v + 1)
                if v:
                    pe.wait_ge(turned_kept, v)
                for t in range(TB):
                    mm = nc.tensor.transpose(ps[:, 4 + t // 4, (t % 4) * P:(t % 4 + 1) * P],
                                             prob[:, v % 2, t * P:(t + 1) * P], ident[:])
                mm.then_inc(turned, 1)

            pe.wait_ge(cst_in, 16)
            kr = krg[ROPE:P, :]
            nc.tensor.matmul(ps[:, 4, 0:CTX], cst[ROPE:P, C_KDUP:C_KDUP + P], kr[:, 0:CTX], start=True, stop=True)
            nc.tensor.matmul(ps[:, 5, :], cst[ROPE:P, C_KDUP:C_KDUP + P], kr[:, CTX:TOK], start=True, stop=True)
            nc.tensor.matmul(ps[:, 3, :], cst[ROPE:P, C_KSWAP:C_KSWAP + P], kr[:, CTX:TOK], start=True,
                             stop=True).then_inc(kr_turned, 1)
            for kind, n in PROJECT:
                do_piece((kind, n, 0))
            pe.wait_ge(kr_ready, 1)
            for v in range(PAIRS * U):
                pair, u = divmod(v, U)
                score(v)
                for piece in pieces(pair, u):
                    do_piece(piece)
                if v:
                    turn(v - 1)
            turn(PAIRS * U - 1)
            do_piece(("out", 1, PAIRS - 1))


class FirstLoadsE:

    def __init__(self, nc, stack):
        self.raw = nc.alloc_sbuf_tensor_at("f_raw", [P, 3, KT * P], F32, offset=SB0 + 134 * KB)
        self.xs = nc.alloc_sbuf_tensor_at("e_xs", [P, 2, LB, P], F32, offset=SB0 + 118 * KB)
        self.raw_in = [stack.enter_context(nc.semaphore(f"f_raw_in{s}")) for s in range(3)]
        self.xs_in = [stack.enter_context(nc.semaphore(f"e_xs_in{s}")) for s in range(2)]

    def fetch_first(self, sp, io):
        out_w = io["w_out"][0].rearrange("(k p) m -> p k m", p=P)
        xv = io["x"][0].rearrange("(t p) m -> p t m", p=P)
        for n in range(2):
            cols = slice(n * P, (n + 1) * P)
            sp.dma_start(self.raw[:, n, :].rearrange("p (k m) -> p k m", m=P), out_w[:, :, cols]).then_inc(self.raw_in[n], 16)
            sp.dma_start(self.xs[:, n], xv[:, :, cols]).then_inc(self.xs_in[n], 16)


def finish(nc, io, sb, sem, psum):
    vecs, modR, ident, ones, eps = sb["vecs"], sb["modR"], sb["ident"], sb["ones"], sb["eps"]
    ps = psum["all"]
    yT, x1T, x1m_hi, x1m_lo = sb["yT"], sb["x1T"], sb["x1m_hi"], sb["x1m_lo"]

    def at(name, shape, dtype, kb):
        return nc.alloc_sbuf_tensor_at(name, shape, dtype, offset=SB0 + int(kb * KB))

    SLOT = KT * P
    first_e = sb["first_e"]
    raw, xs, raw_in, xs_in = first_e.raw, first_e.xs, first_e.raw_in, first_e.xs_in
    w_hi = at("f_w_hi", [P, 2, SLOT], F32R, 158)
    w_lo = at("f_w_lo", [P, 2, SLOT], F32R, 174)
    ada = at("e_ada", [P, 4, ADA_COLS], F32, 190)
    y_hi = at("e_y_hi", [P, KT, LAT], F32R, 54)
    y_lo = at("e_y_lo", [P, KT, LAT], F32R, 86)
    xa = at("e_xa", [P, 2, LAT], F32, 122)
    xp = at("e_xp", [P, 2, LAT], F32, 126)
    total = at("e_total", [P, LAT], F32, 130)
    pivot = at("e_pivot", [P, LAT], F32, 132)
    sqtot = at("e_sqtot", [P, LAT], F32, 196)
    sq = at("e_sq", [P, 2, LAT], F32, 192)
    diag = at("e_diag", [P, 2, LB, P], F32, 198)
    stat = at("e_stat", [P, 8, LB], F32, 207)
    fold = at("e_fold", [P, 4, KT], F32, 207.25)
    u = at("e_u", [P, 2, LAT], F32, 5)
    a = at("e_a", [P, 2, LAT], F32, 9)
    x1m = at("e_x1m", [P, 2, LAT], F32, 13)
    h_hi = at("f_h_hi", [P, 4, LAT], F32R, 118)
    h_lo = at("f_h_lo", [P, 4, LAT], F32R, 126)
    conv = at("f_conv", [P, LAT], F32, 17)
    act_out = at("f_act_out", [P, LAT], F32, 19)
    h = at("f_h", [P, LAT], F32, 190)
    xnat = at("g_xnat", [P, LB, D], F32, 54)
    gain = at("g_gain", [P, D], F32, 86)
    shift = at("g_shift", [P, D], F32, 94)
    stats = at("g_stats", [P, LB, 4, 6], F32, 192)
    mv = at("g_mv", [P, LB, 2], F32, 193)
    ginv = at("g_inv", [P, 2, LB], F32, 193.5)

    ada_in = sem("e_ada_in")
    y_hi_ready = sem("e_y_hi_ready")
    y_lo_ready = sem("e_y_lo_ready")
    ada_summed = sem("e_ada_summed")
    hi_ready = sem("f_hi_ready")
    lo_ready = sem("f_lo_ready")
    slot_done = sem("f_slot_done")
    x_turned = sem("e_x_turned")
    xa_ready = sem("e_xa_ready")
    xp_ready = sem("e_xp_ready")
    pivot_done = sem("e_pivot_done")
    pivot_ready = sem("e_pivot_ready")
    x1_ready = sem("e_x1_ready")
    sq_ready = sem("e_sq_ready")
    sq_added = sem("e_sq_added")
    total_ready = sem("e_total_ready")
    sums_done = sem("e_sums_done")
    var_ready = sem("e_var_ready")
    root_ready = sem("e_root_ready")
    diag_ready = sem("e_diag_ready")
    spread = sem("e_spread")
    u_ready = sem("e_u_ready")
    a_ready = sem("e_a_ready")
    x1m_ready = sem("e_x1m_ready")
    x1m_hi_ready = sem("e_x1m_hi_ready")
    x1m_lo_ready = sem("e_x1m_lo_ready")
    u2_ready = sem("e_u2_ready")
    alpha_ready = sem("e_alpha_ready")
    conv_ready = sem("f_conv_ready")
    silu_ready = sem("f_silu_ready")
    h_ready = sem("f_h_ready")
    h_hi_ready = sem("f_h_hi_ready")
    h_lo_ready = sem("f_h_lo_ready")
    down_done = sem("f_down_done")
    down_kept = sem("f_down_kept")
    vec_in = sem("g_vec_in")
    turned = sem("g_turned")
    turned_kept = sem("g_turned_kept")
    turned_seen = sem("g_turned_seen")
    gvar_ready = sem("g_var_ready")
    groot_ready = sem("g_root_ready")
    gfold_ready = sem("g_fold_ready")
    normed = sem("g_normed")
    gained = sem("g_gained")
    out_a_ready = sem("g_out_a_ready")
    out_b_ready = sem("g_out_b_ready")
    out_sent = sem("g_out_sent")
    dve_own = sem("f_dve_own")
    ln_own = sem("e_ln_own")
    pool_own = sem("e_pool_own")

    G = 4
    GROUPS = FC // G
    BODY = 3 * G
    FIRST = [("up", j, half) for j in range(G) for half in range(2)]
    TURN = FIRST[0:2] + [("down", q, None) for q in range(4)] + FIRST[2:]
    LAST = [("down", q, None) for q in range(4)]
    E0 = KT - 12
    FIRST0 = KT
    TURN0 = FIRST0 + len(FIRST)
    LAST0 = TURN0 + (GROUPS - 1) * BODY
    assert BODY % 6 == 0 and LAST0 + 4 == KT + 3 * FC
    GP, NBP, AG, NAB = range(4)

    block = nc.Block()
    with block as block:
        @block.gpsimd
        def _(pool):
            sem.clear_last(pool)

            def pivoted(m, s, it=0):
                pool.wait_ge(xa_ready, 6 * it + m + 1)
                if m >= 3 or not isinstance(it, int):
                    pool.wait_ge(x1_ready, 6 * it + m - 1)
                nc.gpsimd.tensor_tensor(xp[:, s, :], xa[:, s, :], pivot[:], ALU.subtract).then_inc(xp_ready, 1)
                pool.wait_ge(sq_ready, 6 * it + m + 1)
                pool.wait_ge(sq_added, 6 * it + m)
                nc.gpsimd.tensor_tensor(sqtot[:], sqtot[:], sq[:, s, :], ALU.add).then_inc(sq_added, 1)

            pool.wait_ge(pivot_ready, 1)
            pool.wait_ge(ada_summed, 1)
            pool.wait_ge(sq_ready, 1)
            nc.gpsimd.tensor_copy(sqtot[:], sq[:, 0, :]).then_inc(sq_added, 1)
            for m in range(1, E0):
                pivoted(m, m % 2)
            with pool.Fori(0, 2) as i:
                for k in range(6):
                    pivoted(E0 + k, k % 2, i)
            for m in range(KT):
                pool.wait_ge(a_ready, m + 1)
                pool.wait_ge(u_ready, m + 1)
                if m >= 2:
                    pool.wait_ge(x1m_lo_ready, m - 1)
                nc.gpsimd.tensor_tensor(x1m[:, m % 2, :], a[:, m % 2, :], u[:, m % 2, :], ALU.subtract).then_inc(x1m_ready, 1)
            pool.wait_ge(vec_in, 32)
            for t in range(LB):
                pool.wait_ge(gained, 2 * t + 1)
                nc.gpsimd.tensor_tensor(xnat[:, t, 0:D // 2], xnat[:, t, 0:D // 2], shift[:, 0:D // 2], ALU.add)\
                  .then_inc(out_a_ready, 1)

        @block.sync
        def _(sp):
            out_w = io["w_out"][0].rearrange("(k p) m -> p k m", p=P)
            up = io["w_up"][0].rearrange("(k p) m -> p k m", p=P)
            down = io["w_down"][0].rearrange("(f p) m -> p f m", p=P)
            xv = io["x"][0].rearrange("(t p) m -> p t m", p=P)

            def fetch(n, src, m, it=0, body=1):
                if not isinstance(it, int) or n >= 3:
                    sp.wait_ge(lo_ready, it * body + n - 2)
                sp.dma_start(raw[:, n % 3, :].rearrange("p (k m) -> p k m", m=m), src).then_inc(raw_in[n % 3], 16)

            def fetch_out(n, it=0):
                fetch(n, out_w[:, :, bass.ds(it * 6 * P + n * P, P)], P, it, 6)
                fetch_xs(n, it)

            def fetch_xs(n, it=0):
                if not isinstance(it, int) or n >= 2:
                    sp.wait_ge(x_turned, it * 6 + n - 1)
                sp.dma_start(xs[:, n % 2], xv[:, :, bass.ds(it * 6 * P + n * P, P)]).then_inc(xs_in[n % 2], 16)

            def fetch_mlp(n, what, group, it=0):
                kind, j, half = what
                if kind == "up":
                    fetch(n, up[:, :, bass.ds(group * (G * P) + (half * D_FF + j * P), P)], P, it, BODY)
                else:
                    fetch(n, down[:, bass.ds(group * G, G), j * 512:(j + 1) * 512], 512, it, BODY)

            sp.dma_start(ada[:], io["scratch"]["ada"][4:8].rearrange("a p m -> p a m")).then_inc(ada_in, 16)
            fetch(2, out_w[:, :, 2 * P:3 * P], P)
            fetch_xs(2)
            for n in range(3, E0):
                fetch_out(n)
            with sp.Fori(0, 2) as i:
                for k in range(6):
                    fetch_out(E0 + k, i)
            for k, what in enumerate(FIRST):
                fetch_mlp(FIRST0 + k, what, 0)
            with sp.Fori(0, GROUPS - 1) as i:
                for k, what in enumerate(TURN):
                    fetch_mlp(TURN0 + k, what, i + 1 if what[0] == "up" else i, i)
            for k, what in enumerate(LAST):
                fetch_mlp(LAST0 + k, what, GROUPS - 1)
            sp.wait_ge(slot_done, LAST0)
            sp.dma_start(gain[:], io["ln2_g"][0].partition_broadcast(P)).then_inc(vec_in, 16)
            sp.dma_start(shift[:], io["ln2_b"][0].partition_broadcast(P)).then_inc(vec_in, 16)
            for t in range(LB):
                for c, ready in enumerate((out_a_ready, out_b_ready)):
                    sp.wait_ge(ready, t + 1)
                    cols = slice(c * D // 2, (c + 1) * D // 2)
                    sp.dma_start(io["out"][0, t * P:(t + 1) * P, cols], xnat[:, t, cols]).then_inc(out_sent, 16)
            sp.wait_ge(out_sent, 16 * 2 * LB)

        @block.scalar
        def _(act):
            def hi_part(n, it=0, body=1):
                if isinstance(it, int):
                    act.wait_ge(raw_in[n % 3], 16 * (n // 3 + 1))
                else:
                    act.wait_ge(raw_in[n % 3], it * (16 * body // 3) + 16 * (n // 3 + 1))
                if not isinstance(it, int) or n >= 2:
                    act.wait_ge(slot_done, it * body + n - 1)
                nc.scalar.activation(w_hi[:, n % 2, :], raw[:, n % 3, :], ACT.Copy).then_inc(hi_ready, 1)

            def keep_x(m, it=0):
                act.wait_ge(x_turned, 6 * it + m + 1)
                if m == 2:
                    act.wait_ge(x1_ready, 1)
                elif m > 2:
                    act.wait_ge(xp_ready, 6 * it + m - 2)
                nc.scalar.activation(xa[:, m % 2, :], ps[:, 2 + m % 2, :], ACT.Copy, scale=ALPHA).then_inc(xa_ready, 1)

            def square(m, it=0):
                act.wait_ge(x1_ready, 6 * it + m + 1)
                if not isinstance(it, int) or m >= 2:
                    act.wait_ge(sq_added, 6 * it + m - 1)
                row = x1T[:, m, :] if isinstance(it, int) else x1T[:, bass.ds(6 * it + m, 1), :]
                nc.scalar.activation(sq[:, m % 2, :], row, ACT.Square).then_inc(sq_ready, 1)

            nc.scalar.activation(y_hi[:, 0, :], yT[:, 0, :], ACT.Copy).then_inc(y_hi_ready, 1)
            hi_part(0)
            for k in range(1, KT):
                nc.scalar.activation(y_hi[:, k, :], yT[:, k, :], ACT.Copy).then_inc(y_hi_ready, 1)
            keep_x(0)
            hi_part(1)
            keep_x(1)
            hi_part(2)
            act.wait_ge(pivot_done, 1)
            nc.scalar.activation(pivot[:], ps[:, 4, :], ACT.Copy, scale=1.0 / P).then_inc(pivot_ready, 1)
            act.wait_ge(ada_summed, 1)
            square(0)
            square(1)
            for m in range(2, E0):
                keep_x(m)
                hi_part(m + 1)
                square(m)
            with act.Fori(0, 2) as i:
                for k in range(6):
                    keep_x(E0 + k, i)
                    hi_part(E0 + k + 1, i, 6)
                    square(E0 + k, i)
            act.wait_ge(var_ready, 1)
            nc.scalar.activation(stat[:, 4, :], stat[:, 3, :], ACT.Sqrt, bias=eps[:]).then_inc(root_ready, 1)
            hi_part(FIRST0 + 1)
            act.wait_ge(spread, 1)

            def hi_x(m):
                act.wait_ge(x1m_ready, m + 1)
                nc.scalar.activation(x1m_hi[:, m, :], x1m[:, m % 2, :], ACT.Copy).then_inc(x1m_hi_ready, 1)

            for m in range(KT):
                if m >= 2:
                    act.wait_ge(x1m_ready, m - 1)
                nc.scalar.activation(u[:, m % 2, :], ps[:, 7, :], ACT.Identity, bias=fold[:, NBP, m:m + 1],
                                     scale=fold[:, GP, m:m + 1]).then_inc(u_ready, 1)
                if m:
                    hi_x(m - 1)
            hi_x(KT - 1)

            def alpha_part(m):
                act.wait_ge(alpha_ready, m - 1) if m >= 2 else act.wait_ge(x1m_ready, KT)
                nc.scalar.activation(u[:, m % 2, :], ps[:, 7, :], ACT.Identity, bias=fold[:, NAB, m:m + 1],
                                     scale=fold[:, AG, m:m + 1]).then_inc(u2_ready, 1)

            def chunk(c, j, down_slots):
                act.wait_ge(conv_ready, c + 1)
                nc.scalar.activation(act_out[:], conv[:], ACT.Silu).then_inc(silu_ready, 1)
                act.wait_ge(h_ready, c + 1)
                if down_slots is not None:
                    act.wait_ge(slot_done, down_slots)
                nc.scalar.activation(h_hi[:, j, :], h[:], ACT.Copy).then_inc(h_hi_ready, 1)

            for k, (kind, j, half) in enumerate(FIRST):
                if k:
                    hi_part(FIRST0 + k + 1)
                for m in (2 * k, 2 * k + 1):
                    alpha_part(m)
                if half == 1:
                    chunk(j, j, None)
            with act.Fori(0, GROUPS - 1) as i:
                for k, (kind, j, half) in enumerate(TURN):
                    if k == 6:
                        chunk(G * i + G, 0, i * BODY + TURN0 + 6)
                    hi_part(TURN0 + k + 1, i, BODY)
                    if half == 1 and j > 0:
                        chunk(G * i + G + j, j, None)

            def keep_turned(q):
                for t in range(LB):
                    act.wait_ge(turned, LB * q + t + 1)
                    nc.scalar.activation(xnat[:, t, q * 512:(q + 1) * 512], ps[:, t, :], ACT.Copy).then_inc(turned_kept, 1)

            for k in range(4):
                if k < 3:
                    hi_part(LAST0 + k + 1)
                if k >= 2:
                    keep_turned(k - 2)
            keep_turned(2)
            keep_turned(3)
            act.wait_ge(gvar_ready, 1)
            nc.scalar.activation(ginv[:, 0, :], mv[:, :, 1], ACT.Sqrt, bias=eps[:]).then_inc(groot_ready, 1)
            act.wait_ge(gfold_ready, 1)
            for t in range(LB):
                for c in range(2):
                    x = xnat[:, t, c * D // 2:(c + 1) * D // 2]
                    nc.scalar.activation(x, x, ACT.Identity, bias=ginv[:, 1, t:t + 1], scale=ginv[:, 0, t:t + 1])\
                      .then_inc(normed, 1)

        @block.vector
        def _(dve):
            own = Chain(dve, dve_own)
            ln = Chain(dve, ln_own)

            def lo_part(n, it=0, body=1):
                dve.wait_ge(hi_ready, it * body + n + 1)
                nc.vector.tensor_tensor(w_lo[:, n % 2, :], raw[:, n % 3, :], w_hi[:, n % 2, :].bitcast(F32),
                                        ALU.subtract).then_inc(lo_ready, 1)

            def y_part(k):
                dve.wait_ge(y_hi_ready, k + 1)
                nc.vector.tensor_tensor(y_lo[:, k, :], yT[:, k, :], y_hi[:, k, :].bitcast(F32), ALU.subtract)\
                  .then_inc(y_lo_ready, 1)

            y_part(0)
            lo_part(0)
            for k in range(1, KT):
                y_part(k)
            dve.wait_ge(ada_summed, 1)
            ln.after(nc.vector.tensor_tensor(modR[:, 2 * KT:], ps[:, 7, 0:2 * KT],
                                             vecs[:, V_ADA + 4 * KT:V_ADA + 6 * KT], ALU.add))
            scale = modR[:, 2 * KT:3 * KT]
            ln.after(nc.vector.tensor_scalar(scale, scale, 1.0, None, ALU.add))
            gain1, shift1 = vecs[:, V_LN1G:V_LN1G + KT], vecs[:, V_LN1B:V_LN1B + KT]
            nc.vector.tensor_tensor(fold[:, GP, :], gain1, scale, ALU.mult)
            nc.vector.tensor_scalar(fold[:, AG, :], gain1, ALPHA, None, ALU.mult)
            nc.vector.tensor_scalar(fold[:, NAB, :], shift1, -ALPHA, None, ALU.mult)
            ln.after(nc.vector.tensor_tensor(fold[:, NBP, :], shift1, scale, ALU.mult))
            ln.after(nc.vector.scalar_tensor_tensor(fold[:, NBP, :], fold[:, NBP, :], -1.0, modR[:, KT:2 * KT],
                                                    ALU.mult, ALU.subtract))
            dve.wait_ge(y_lo_ready, KT)
            lo_part(1)

            def add_x(m, it=0):
                dve.wait_ge(slot_done, 6 * it + m + 1)
                dve.wait_ge(xp_ready, 6 * it + m)
                row = x1T[:, m:m + 1, :] if isinstance(it, int) else x1T[:, bass.ds(6 * it + m, 1), :]
                gate = modR[:, m:m + 1] if isinstance(it, int) else modR[:, bass.ds(6 * it + m, 1)]
                nc.vector.scalar_tensor_tensor(row, ps[:, m % 2:m % 2 + 1, :], gate, xp[:, m % 2:m % 2 + 1, :],
                                               ALU.mult, ALU.add).then_inc(x1_ready, 1)
                dve.wait_ge(x1_ready, 6 * it + m + 1)
                dve.wait_ge(total_ready, 6 * it + m)
                nc.vector.tensor_tensor(total[:], total[:], row[:, 0], ALU.add).then_inc(total_ready, 1)

            dve.wait_ge(slot_done, 1)
            dve.wait_ge(xa_ready, 1)
            ln.after(nc.vector.scalar_tensor_tensor(x1T[:, 0, :], ps[:, 0, :], modR[:, 0:1], xa[:, 0, :], ALU.mult, ALU.add))
            lo_part(2)
            dve.wait_ge(pivot_ready, 1)
            nc.vector.tensor_tensor(x1T[:, 0, :], x1T[:, 0, :], pivot[:], ALU.subtract).then_inc(x1_ready, 1)
            dve.wait_ge(x1_ready, 1)
            nc.vector.tensor_copy(total[:], x1T[:, 0, :]).then_inc(total_ready, 1)
            add_x(1)
            for m in range(2, E0):
                lo_part(m + 1)
                add_x(m)
            with dve.Fori(0, 2) as i:
                for k in range(6):
                    lo_part(E0 + k + 1, i, 6)
                    add_x(E0 + k, i)
            dve.wait_ge(sums_done, 1)
            ln.after(nc.vector.tensor_scalar(stat[:, 0:2, :], ps[:, 5, 0:2 * LB].rearrange("p (a b) -> p a b", a=2), 1.0 / D,
                                             None, ALU.mult))
            ln.after(nc.vector.tensor_tensor(stat[:, 2, :], stat[:, 0, :], stat[:, 0, :], ALU.mult))
            ln.after(nc.vector.tensor_tensor(stat[:, 3, :], stat[:, 1, :], stat[:, 2, :], ALU.subtract))
            nc.vector.tensor_scalar(stat[:, 3, :], stat[:, 3, :], 0.0, None, ALU.max).then_inc(var_ready, 1)
            dve.wait_ge(root_ready, 1)
            ln.after(nc.vector.reciprocal(stat[:, 5, :], stat[:, 4, :]))
            ln.after(nc.vector.tensor_tensor(stat[:, 6, :], stat[:, 0, :], stat[:, 5, :], ALU.mult))
            for r in range(2):
                for t in range(LB):
                    last = nc.vector.tensor_scalar(diag[:, r, t, :], ident[:], stat[:, 5 + r, t:t + 1], None, ALU.mult)
            last.then_inc(diag_ready, 1)
            lo_part(FIRST0 + 1)
            dve.wait_ge(spread, 1)

            def lo_x(m):
                dve.wait_ge(x1m_hi_ready, m + 1)
                nc.vector.tensor_tensor(x1m_lo[:, m, :], x1m[:, m % 2, :], x1m_hi[:, m, :].bitcast(F32), ALU.subtract)\
                  .then_inc(x1m_lo_ready, 1)

            for m in range(KT + 2):
                if m < KT:
                    if m >= 2:
                        dve.wait_ge(x1m_ready, m - 1)
                    nc.vector.scalar_tensor_tensor(a[:, m % 2, :], x1T[:, m, :], fold[:, GP, m:m + 1], ps[:, 6, :],
                                                   ALU.mult, ALU.mult).then_inc(a_ready, 1)
                if m >= 2:
                    lo_x(m - 2)

            def alpha_part(m):
                ln.after(nc.vector.scalar_tensor_tensor(x1T[:, m, :], x1T[:, m, :], fold[:, AG, m:m + 1], ps[:, 6, :],
                                                        ALU.mult, ALU.mult))
                dve.wait_ge(u2_ready, m + 1)
                nc.vector.tensor_tensor(x1T[:, m, :], x1T[:, m, :], u[:, m % 2, :], ALU.subtract)\
                  .then_inc(alpha_ready if m < KT - 1 else down_kept, 1)

            def chunk(c, j, slots):
                own.at(2 * c)
                dve.wait_ge(slot_done, slots)
                g = ps[:, 2 * (j % 2), :]
                up = ps[:, 2 * (j % 2) + 1, :]

                def col(v):
                    return vecs[:, c + v:c + v + 1] if isinstance(c, int) else vecs[:, bass.ds(c + v, 1)]

                if not isinstance(c, int) or c:
                    dve.wait_ge(silu_ready, c)
                own.after(nc.vector.tensor_scalar(conv[:], g, col(V_FW + FC), col(V_FB), ALU.mult, ALU.add))
                own.after(nc.vector.scalar_tensor_tensor(conv[:, 1:LAT], g[:, 0:LAT - 1], col(V_FW), conv[:, 1:LAT],
                                                         ALU.mult, ALU.add))
                nc.vector.scalar_tensor_tensor(conv[:, 0:LAT - 1], g[:, 1:LAT], col(V_FW + 2 * FC), conv[:, 0:LAT - 1],
                                               ALU.mult, ALU.add).then_inc(conv_ready, 1)
                dve.wait_ge(silu_ready, c + 1)
                if not isinstance(c, int) or c:
                    dve.wait_ge(h_lo_ready, c)
                nc.vector.tensor_tensor(h[:], act_out[:], up, ALU.mult).then_inc(h_ready, 1)
                dve.wait_ge(h_hi_ready, c + 1)
                nc.vector.tensor_tensor(h_lo[:, j, :], h[:], h_hi[:, j, :].bitcast(F32), ALU.subtract)\
                  .then_inc(h_lo_ready, 1)

            def add_down(n, q, group, it=0):
                for e in range(4):
                    m = 4 * q + e
                    if e < 3:
                        dve.wait_ge(down_done, group * (KT - 4) + 3 * q + e + 1)
                    else:
                        dve.wait_ge(slot_done, it * BODY + n + 1)
                    nc.vector.scalar_tensor_tensor(x1T[:, m, :], ps[:, 4 + e, :], modR[:, 3 * KT + m:3 * KT + m + 1],
                                                   x1T[:, m, :], ALU.mult, ALU.add).then_inc(down_kept, 1)

            for k, (kind, j, half) in enumerate(FIRST):
                if k:
                    lo_part(FIRST0 + k + 1)
                for m in (2 * k, 2 * k + 1):
                    alpha_part(m)
                if half == 1:
                    chunk(j, j, FIRST0 + k + 1)
            dve.wait_ge(down_kept, 1)
            with dve.Fori(0, GROUPS - 1) as i:
                for k, (kind, j, half) in enumerate(TURN):
                    if k == 6:
                        chunk(G * i + G, 0, i * BODY + TURN0 + 6)
                    lo_part(TURN0 + k + 1, i, BODY)
                    if kind == "down":
                        add_down(TURN0 + k, j, i, i)
                    elif half == 1 and j > 0:
                        chunk(G * i + G + j, j, i * BODY + TURN0 + k + 1)

            def see_turned(q):
                for t in range(LB):
                    dve.wait_ge(turned_kept, LB * q + t + 1)
                    last = nc.vector.bn_stats(stats[:, t, q, :], xnat[:, t, q * 512:(q + 1) * 512])
                last.then_inc(turned_seen, 1)

            for k in range(4):
                if k < 3:
                    lo_part(LAST0 + k + 1)
                add_down(LAST0 + k, k, GROUPS - 1)
                if k >= 2:
                    see_turned(k - 2)
            see_turned(2)
            see_turned(3)
            dve.wait_ge(turned_seen, 4)
            for t in range(LB):
                last = nc.vector.bn_aggr(mv[:, t, :], stats[:, t, :, :].rearrange("p a b -> p (a b)"))
            last.then_inc(gvar_ready, 1)
            dve.wait_ge(groot_ready, 1)
            ln.after(nc.vector.reciprocal(ginv[:, 0, :], ginv[:, 0, :]))
            nc.vector.scalar_tensor_tensor(ginv[:, 1, :], mv[:, :, 0], -1.0, ginv[:, 0, :], ALU.mult, ALU.mult)\
              .then_inc(gfold_ready, 1)
            dve.wait_ge(vec_in, 32)
            for t in range(LB):
                for c in range(2):
                    dve.wait_ge(normed, 2 * t + c + 1)
                    cols = slice(c * D // 2, (c + 1) * D // 2)
                    nc.vector.tensor_tensor(xnat[:, t, cols], xnat[:, t, cols], gain[:, cols], ALU.mult).then_inc(gained, 1)
                dve.wait_ge(gained, 2 * t + 2)
                nc.vector.tensor_tensor(xnat[:, t, D // 2:D], xnat[:, t, D // 2:D], shift[:, D // 2:D], ALU.add)\
                  .then_inc(out_b_ready, 1)

        @block.tensor
        def _(pe):
            passes = [(w_hi, y_hi, x1m_hi, h_hi), (w_hi, y_lo, x1m_lo, h_lo), (w_lo, y_hi, x1m_hi, h_hi)]

            def out_slot(m, it=0):
                pe.wait_ge(xs_in[m % 2], it * 48 + 16 * (m // 2 + 1))
                if not isinstance(it, int) or m >= 2:
                    pe.wait_ge(x1_ready, 6 * it + m - 1)
                for t in range(LB):
                    mm = nc.tensor.transpose(ps[:, 2 + m % 2, t * P:(t + 1) * P], xs[:, m % 2, t, :], ident[:])
                mm.then_inc(x_turned, 1)
                pe.wait_ge(lo_ready, 6 * it + m + 1)
                for k in range(KT):
                    if m == 0:
                        pe.wait_ge(y_lo_ready, k + 1)
                    for p, (w, y, _, _) in enumerate(passes):
                        mm = nc.tensor.matmul(ps[:, m % 2, :], w[:, m % 2, k * P:(k + 1) * P], y[:, k, :],
                                              start=(k == 0 and p == 0), stop=(k == KT - 1 and p == 2))
                mm.then_inc(slot_done, 1)

            def first_pair():
                both = 10
                order = [(k, half) for k in range(both) for half in range(2)]
                order += [(k, half) for half in range(2) for k in range(both, KT)]
                for k, half in order:
                    if half == 0:
                        pe.wait_ge(x1m_lo_ready, k + 1)
                    if k == 0:
                        pe.wait_ge(lo_ready, FIRST0 + half + 1)
                    for p, (w, _, x, _) in enumerate(passes):
                        mm = nc.tensor.matmul(ps[:, half, :], w[:, (FIRST0 + half) % 2, k * P:(k + 1) * P], x[:, k, :],
                                              start=(k == 0 and p == 0), stop=(k == KT - 1 and p == 2))
                    if k == KT - 1:
                        mm.then_inc(slot_done, 1)

            def up_slot(n, j, half, c, it=0):
                if half == 0 and (not isinstance(c, int) or c >= 2):
                    pe.wait_ge(h_ready, c - 1)
                pe.wait_ge(lo_ready, it * BODY + n + 1)
                for k in range(KT):
                    for p, (w, _, x, _) in enumerate(passes):
                        mm = nc.tensor.matmul(ps[:, 2 * (j % 2) + half, :], w[:, n % 2, k * P:(k + 1) * P], x[:, k, :],
                                              start=(k == 0 and p == 0), stop=(k == KT - 1 and p == 2))
                mm.then_inc(slot_done, 1)

            def down_slot(n, q, group, it=0):
                last_first = isinstance(group, int) and q == 0
                if not last_first:
                    pe.wait_ge(h_lo_ready, G * group + G)
                pe.wait_ge(lo_ready, it * BODY + n + 1)
                order = [(e, k) for e in range(4) for k in range(G)]
                if last_first:
                    order.sort(key=lambda ek: ek[1])
                for e, k in order:
                    m = 4 * q + e
                    if last_first and e == 0:
                        pe.wait_ge(h_lo_ready, G * group + k + 1)
                    if k == 0 and q:
                        pe.wait_ge(down_kept, 1 + group * KT + m - 3)
                    elif k == 0 and e == 0:
                        pe.wait_ge(down_kept, 1 + group * KT)
                    for p, (w, _, _, hh) in enumerate(passes):
                        mm = nc.tensor.matmul(ps[:, 4 + e, :], w[:, n % 2, k * 512 + e * P:k * 512 + (e + 1) * P],
                                              hh[:, k, :], start=(k == 0 and p == 0), stop=(k == G - 1 and p == 2))
                    if k == G - 1:
                        mm.then_inc(down_done if e < 3 else slot_done, 1)

            out_slot(0)
            pe.wait_ge(ada_in, 16)
            for c in range(2 * KT):
                mm = nc.tensor.matmul(ps[:, 7, c:c + 1], ada[:, c // 8, c % 8 * P:(c % 8 + 1) * P], ones[:, 0:1],
                                      start=True, stop=True)
            mm.then_inc(ada_summed, 1)
            out_slot(1)
            pe.wait_ge(ln_own, 5)
            nc.tensor.matmul(ps[:, 4, :], ones[:], x1T[:, 0, :], start=True, stop=True).then_inc(pivot_done, 1)
            for m in range(2, E0):
                out_slot(m)
            with pe.Fori(0, 2) as i:
                for k in range(6):
                    out_slot(E0 + k, i)
            pe.wait_ge(total_ready, KT)
            pe.wait_ge(sq_added, KT)
            for r, src in enumerate((total, sqtot)):
                for t in range(LB):
                    mm = nc.tensor.matmul(ps[:, 5, r * LB + t:r * LB + t + 1], src[:, t * P:(t + 1) * P], ones[:, 0:1],
                                          start=True, stop=True)
            mm.then_inc(sums_done, 1)
            pe.wait_ge(diag_ready, 1)
            for r in range(2):
                mm = nc.tensor.matmul(ps[:, 6 + r, :], ones[:], diag[:, r, :, :].rearrange("p a b -> p (a b)"), start=True, stop=True)
            mm.then_inc(spread, 1)
            first_pair()
            for k, (kind, j, half) in enumerate(FIRST[2:]):
                up_slot(FIRST0 + 2 + k, j, half, j)
            pe.wait_ge(down_kept, 1)
            with pe.Fori(0, GROUPS - 1) as i:
                for k, (kind, j, half) in enumerate(TURN):
                    if kind == "up":
                        up_slot(TURN0 + k, j, half, G * i + G + j, i)
                    else:
                        down_slot(TURN0 + k, j, i, i)

            def turn(q):
                pe.wait_ge(down_kept, 1 + GROUPS * KT - KT + 4 * q + 4)
                for t in range(LB):
                    if q:
                        pe.wait_ge(turned_kept, LB * (q - 1) + t + 1)
                    for e in range(4):
                        mm = nc.tensor.transpose(ps[:, t, e * P:(e + 1) * P], x1T[:, 4 * q + e, t * P:(t + 1) * P], ident[:])
                    mm.then_inc(turned, 1)

            for k in range(4):
                down_slot(LAST0 + k, k, GROUPS - 1)
                if k:
                    turn(k - 1)
            turn(3)


IN_NAMES = ["x", "c", "ctx", "c_ctx", "w_ada", "b_ada", "w_in", "g_q", "w_uq", "g_kv", "w_ukv", "ml_conv_w",
            "ml_conv_b", "w_mq", "w_mk", "b_gate", "g_hn", "w_out", "ln1_g", "ln1_b", "w_up", "ffn_conv_w",
            "ffn_conv_b", "w_down", "ln2_g", "ln2_b"]


def trunk_layer(nc, io, last_stage="g"):
    with ExitStack() as stack:
        def at(name, shape, dtype, kb):
            return nc.alloc_sbuf_tensor_at(name, shape, dtype, offset=SB0 + int(kb * KB))

        ps = stack.enter_context(nc.psum_tensor("ps", [P, 8, 512], F32))
        psum = {"all": ps}
        sb = {
            "ident": at("ident", [P, P], F32, 0),
            "ones": at("ones", [P, P], F32, 0.5),
            "vecs": at("vecs", [P, V_ALL], F32, 1),
            "cT": at("cT", [P, 2 * KT], F32, 3),
            "modT": at("modT", [P, 2 * KT, 2], F32, 3.25),
            "modR": at("modR", [P, 4 * KT], F32, 3.5),
            "eps": at("eps", [P, 1], F32, 3.75),
            "zq": at("zq", [P, QK, LAT], F32, 5),
            "zkv": at("zkv", [P, KVK, TOK], F32, 13),
            "krg": at("krg", [P, TOK], F32, 19),
            "hT_hi": at("hT_hi", [P, KT, TOK], F32R, 22),
            "hT_lo": at("hT_lo", [P, KT, TOK], F32R, 70),
            "yT": at("yT", [P, KT, LAT], F32, 22),
            "x1T": at("x1T", [P, KT, LAT], F32, 22),
            "x1m_hi": at("x1m_hi", [P, KT, LAT], F32R, 54),
            "x1m_lo": at("x1m_lo", [P, KT, LAT], F32R, 86),
        }
        sb["rows"] = GateRows(nc)
        sb["first_c"] = FirstLoadsC(nc, stack)
        sb["first_d"] = FirstLoadsD(nc, stack)
        sb["first_e"] = FirstLoadsE(nc, stack)
        sb["ada_in"] = [stack.enter_context(nc.semaphore(f"ada_w_in{s}")) for s in range(4)]
        sb["ada_sent"] = stack.enter_context(nc.semaphore("ada_sent"))
        sb["v_sent"] = [stack.enter_context(nc.semaphore(f"v_sent{s}")) for s in range(4)]
        scratch = {
            "u": nc.dram_tensor("scratch_u", [UK, P, TOK], F32).ap(),
            "v": nc.dram_tensor("scratch_v", [TB, P, ML_INNER], F32).ap(),
            "o": nc.dram_tensor("scratch_o", [UK, P, LAT], F32).ap(),
            "ada": nc.dram_tensor("scratch_ada", [8, P, 1024], F32).ap(),
        }
        stages = [enter, attention, matrix_memory, finish]
        sems = [StageSems(nc) for _ in stages]
        for n, (name, stage) in enumerate(zip("bcdg", stages)):
            sems[n].last = sems[n - 1] if n else None
            stage(nc, io | {"scratch": scratch}, sb, sems[n], psum)
            if n:
                sems[n - 1].close()
            if name == last_stage:
                break
        sems[n].close()


def kernel(**inputs):
    import concourse.bacc as bacc
    from concourse.bass_utils import run_bass_kernel_spmd

    nc = bacc.Bacc("TRN2", target_bir_lowering=False, num_devices=1)
    consts, ident = host_constants()
    arrays, io = {}, {}
    for name, a in [(n, inputs[n]) for n in IN_NAMES] + [("consts", consts), ("ident", ident)]:
        a = np.ascontiguousarray(a)
        arrays[f"in_{name}"] = a
        io[name] = nc.dram_tensor(f"in_{name}", a.shape, F32, kind="ExternalInput").ap()
    io["out"] = nc.dram_tensor("out", [1, LAT, D], F32, kind="ExternalOutput").ap()
    trunk_layer(nc, io)
    r = run_bass_kernel_spmd(nc, [arrays], core_ids=[0])
    return r.results[0]["out"]
```
